# Optimizing a Trainium2 kernel written in Bass

```python
import math
import jax, jax.numpy as jnp
from jax import lax
import numpy as np

D_MODEL = 1024
BATCH = 1
SEQ = 256
DEPTH = 1

D_MIX = D_MODEL
HGRN_WIDTH = (3 * D_MIX) // 4
HGRN_DK = 128
HGRN_HEADS = HGRN_WIDTH // HGRN_DK
HGRN_DV = HGRN_WIDTH // HGRN_HEADS
HGRN_CHUNK = 64
ATTN_WIDTH = D_MIX - HGRN_WIDTH
ATTN_HEAD_DIM = 64
ATTN_HEADS = ATTN_WIDTH // ATTN_HEAD_DIM
ROT_DIM = ATTN_HEAD_DIM // 4
ROPE_THETA = 500000.0
MOBA_BLOCK = 256
MOBA_TOPK = 3
Q_BLOCK = 128
N_EXPERTS = 32
TOP_K = 4
D_FF = D_MODEL
SWIGLU_ALPHA = 1.702
SWIGLU_LIMIT = 7.0
MOE_BLOCK = 256
N_MOD = 6
RMS_EPS = 1e-6
D_PROJ = 4 * HGRN_WIDTH + 3 * ATTN_WIDTH

kernel_name = "hymba_hgrn2_moba_moe_block"

def rms_norm(x, g, eps=RMS_EPS):
    xf = x.astype(jnp.float32)
    y = xf * lax.rsqrt(jnp.mean(xf * xf, axis=-1, keepdims=True) + eps)
    return (y * g.astype(jnp.float32)).astype(x.dtype)

def split_heads(t, n_heads):
    B, S, W = t.shape
    return t.reshape(B, S, n_heads, W // n_heads).transpose(0, 2, 1, 3)

def merge_heads(t):
    B, H, S, d = t.shape
    return t.transpose(0, 2, 1, 3).reshape(B, S, H * d)

def partial_rotary(t, cos, sin):
    half = ROT_DIM // 2
    t1 = t[..., :half].astype(jnp.float32)
    t2 = t[..., half:ROT_DIM].astype(jnp.float32)
    rot = jnp.concatenate([t1 * cos - t2 * sin, t2 * cos + t1 * sin], axis=-1).astype(t.dtype)
    return jnp.concatenate([rot, t[..., ROT_DIM:]], axis=-1)

def hgrn2_recurrence(q, k, v, log_f):
    B, H, S, dk = q.shape
    dv = v.shape[-1]
    n_chunks = S // HGRN_CHUNK

    def chunked(t):
        return jnp.moveaxis(t.reshape(B, H, n_chunks, HGRN_CHUNK, t.shape[-1]), 2, 0)

    qc, kc, vc = chunked(q), chunked(k), chunked(v)
    bc = jnp.cumsum(chunked(log_f), axis=3)
    causal = jnp.tril(jnp.ones((HGRN_CHUNK, HGRN_CHUNK), dtype=bool))[:, :, None]

    def step(state, inp):
        q_c, k_c, v_c, b_c = inp
        b_last = b_c[:, :, -1:, :]
        o_inter = jnp.einsum('bhtk,bhkv->bhtv', q_c * jnp.exp(b_c), state)
        diff = b_c[:, :, :, None, :] - b_c[:, :, None, :, :]
        decay = jnp.exp(jnp.where(causal, diff, -jnp.inf))
        scores = jnp.einsum('bhtk,bhtsk,bhsk->bhts', q_c, decay, k_c)
        o_intra = jnp.einsum('bhts,bhsv->bhtv', scores, v_c)
        new_state = (jnp.exp(b_last[:, :, 0, :])[..., None] * state
                     + jnp.einsum('bhsk,bhsv->bhkv', k_c * jnp.exp(b_last - b_c), v_c))
        return new_state, o_inter + o_intra

    state0 = jnp.zeros((B, H, dk, dv), jnp.float32)
    _, o = lax.scan(step, state0, (qc, kc, vc, bc))
    return jnp.moveaxis(o, 0, 2).reshape(B, H, S, dv)

def moba_attention(q, k, v):
    B, H, S, hd = q.shape
    n_blocks = -(-S // MOBA_BLOCK)
    pad = n_blocks * MOBA_BLOCK - S
    kb = jnp.pad(k, ((0, 0), (0, 0), (0, pad), (0, 0))).reshape(B, H, n_blocks, MOBA_BLOCK, hd)
    vb = jnp.pad(v, ((0, 0), (0, 0), (0, pad), (0, 0))).reshape(B, H, n_blocks, MOBA_BLOCK, hd)
    k_mean = jnp.mean(kb.astype(jnp.float32), axis=3)
    topk = min(MOBA_TOPK, n_blocks)
    n_q = S // Q_BLOCK
    q_blocks = jnp.moveaxis(q.reshape(B, H, n_q, Q_BLOCK, hd), 2, 0)
    b_idx = jnp.arange(B)[:, None, None, None]
    h_idx = jnp.arange(H)[None, :, None, None]
    scale = hd ** -0.5

    def one_block(args):
        qb, n = args
        q_pos = n * Q_BLOCK + jnp.arange(Q_BLOCK)
        own = (n * Q_BLOCK) // MOBA_BLOCK
        gate = jnp.einsum('bhqd,bhnd->bhqn', qb.astype(jnp.float32), k_mean)
        gate = jnp.where(jnp.arange(n_blocks) < own, gate, -jnp.inf)
        _, sel = lax.top_k(gate, topk)
        valid = jnp.arange(topk) < own
        k_sel = kb[b_idx, h_idx, sel]
        v_sel = vb[b_idx, h_idx, sel]
        s_sel = jnp.einsum('bhqd,bhqnkd->bhqnk', qb, k_sel).astype(jnp.float32) * scale
        s_sel = jnp.where(valid[:, None], s_sel, -jnp.inf).reshape(B, H, Q_BLOCK, topk * MOBA_BLOCK)
        k_own = lax.dynamic_index_in_dim(kb, own, axis=2, keepdims=False)
        v_own = lax.dynamic_index_in_dim(vb, own, axis=2, keepdims=False)
        k_pos = own * MOBA_BLOCK + jnp.arange(MOBA_BLOCK)
        s_own = jnp.einsum('bhqd,bhkd->bhqk', qb, k_own).astype(jnp.float32) * scale
        s_own = jnp.where(k_pos[None, :] <= q_pos[:, None], s_own, -jnp.inf)
        p = jax.nn.softmax(jnp.concatenate([s_sel, s_own], axis=-1), axis=-1).astype(q.dtype)
        p_sel = p[..., :topk * MOBA_BLOCK].reshape(B, H, Q_BLOCK, topk, MOBA_BLOCK)
        p_own = p[..., topk * MOBA_BLOCK:]
        return (jnp.einsum('bhqnk,bhqnkd->bhqd', p_sel, v_sel)
                + jnp.einsum('bhqk,bhkd->bhqd', p_own, v_own))

    out = lax.map(one_block, (q_blocks, jnp.arange(n_q)))
    return jnp.moveaxis(out, 0, 2).reshape(B, H, S, hd)

def moe_ffn(h, w_router, b_router, w_gate_up, b_gate_up, w_down, b_down):
    T, D = h.shape
    n_assign = T * TOP_K
    logits = (h @ w_router + b_router).astype(jnp.float32)
    top_val, top_idx = lax.top_k(logits, TOP_K)
    gates = jax.nn.softmax(top_val, axis=-1).astype(h.dtype)
    flat_e = top_idx.reshape(-1)
    flat_tok = jnp.arange(n_assign, dtype=jnp.int32) // TOP_K
    order = jnp.argsort(flat_e)
    sorted_e = flat_e[order]
    sorted_tok = flat_tok[order]
    sorted_gate = gates.reshape(-1)[order]
    counts = jax.ops.segment_sum(jnp.ones_like(flat_e), flat_e, num_segments=N_EXPERTS)
    group_start = jnp.cumsum(counts) - counts
    padded = (counts + MOE_BLOCK - 1) // MOE_BLOCK * MOE_BLOCK
    pad_end = jnp.cumsum(padded)
    pad_start = pad_end - padded
    dest = pad_start[sorted_e] + jnp.arange(n_assign, dtype=jnp.int32) - group_start[sorted_e]
    n_blk = -(-n_assign // MOE_BLOCK) + N_EXPERTS
    tok_buf = jnp.full((n_blk * MOE_BLOCK,), T, jnp.int32).at[dest].set(sorted_tok)
    gate_buf = jnp.zeros((n_blk * MOE_BLOCK,), h.dtype).at[dest].set(sorted_gate)
    blk_expert = jnp.minimum(
        jnp.searchsorted(pad_end, jnp.arange(n_blk, dtype=jnp.int32) * MOE_BLOCK, side='right'),
        N_EXPERTS - 1)
    h_pad = jnp.concatenate([h, jnp.zeros((1, D), h.dtype)], axis=0)

    def expert_block(args):
        toks, g, e = args
        xb = h_pad[toks]
        gu = xb @ w_gate_up[e] + b_gate_up[e]
        gate = jnp.minimum(gu[:, :D_FF], SWIGLU_LIMIT)
        up = jnp.clip(gu[:, D_FF:], -SWIGLU_LIMIT, SWIGLU_LIMIT)
        act = (up + 1.0) * gate * jax.nn.sigmoid(SWIGLU_ALPHA * gate)
        return (act @ w_down[e] + b_down[e]) * g[:, None]

    y = lax.map(expert_block, (tok_buf.reshape(n_blk, MOE_BLOCK),
                               gate_buf.reshape(n_blk, MOE_BLOCK), blk_expert))
    return jax.ops.segment_sum(y.reshape(-1, D), tok_buf, num_segments=T + 1)[:T]

def setup_inputs(seed: int = 0) -> dict:
    key = jax.random.key(seed)
    ks = jax.random.split(key, 20)
    f32 = jnp.float32
    nrm = lambda k, shape, s: jax.random.normal(k, shape, f32) * s
    x = jax.random.normal(ks[0], (BATCH, SEQ, D_MODEL), f32)
    c = jax.random.normal(ks[1], (BATCH, D_MODEL), f32)
    offset = jax.random.randint(ks[2], (BATCH, 1), 0, 4096, dtype=jnp.int32)
    positions = offset + jnp.arange(SEQ, dtype=jnp.int32)[None, :]
    return {
        "x": x,
        "c": c,
        "positions": positions,
        "w_ada": nrm(ks[3], (DEPTH, D_MODEL, N_MOD * D_MODEL), 0.5 * D_MODEL ** -0.5),
        "b_ada": nrm(ks[4], (DEPTH, N_MOD * D_MODEL), 0.02),
        "norm1_g": 1.0 + nrm(ks[5], (DEPTH, D_MODEL), 0.02),
        "w_in": nrm(ks[6], (DEPTH, D_MODEL, D_PROJ), D_MODEL ** -0.5),
        "hgrn_lb_logits": nrm(ks[7], (DEPTH + 1, HGRN_WIDTH), 0.5),
        "hgrn_norm_g": 1.0 + nrm(ks[8], (DEPTH, HGRN_DV), 0.02),
        "attn_norm_g": 1.0 + nrm(ks[9], (DEPTH, ATTN_HEAD_DIM), 0.02),
        "w_out": nrm(ks[10], (DEPTH, D_MIX, D_MODEL), D_MIX ** -0.5),
        "norm2_g": 1.0 + nrm(ks[11], (DEPTH, D_MODEL), 0.02),
        "w_router": nrm(ks[12], (DEPTH, D_MODEL, N_EXPERTS), D_MODEL ** -0.5),
        "b_router": nrm(ks[13], (DEPTH, N_EXPERTS), 0.01),
        "w_gate_up": nrm(ks[14], (DEPTH, N_EXPERTS, D_MODEL, 2 * D_FF), D_MODEL ** -0.5),
        "b_gate_up": nrm(ks[15], (DEPTH, N_EXPERTS, 2 * D_FF), 0.02),
        "w_down": nrm(ks[16], (DEPTH, N_EXPERTS, D_FF, D_MODEL), D_FF ** -0.5),
        "b_down": nrm(ks[17], (DEPTH, N_EXPERTS, D_MODEL), 0.02),
        "final_norm_g": 1.0 + nrm(ks[18], (D_MODEL,), 0.02),
    }

def reference(x, c, positions, w_ada, b_ada, norm1_g, w_in, hgrn_lb_logits, hgrn_norm_g,
              attn_norm_g, w_out, norm2_g, w_router, b_router, w_gate_up, b_gate_up,
              w_down, b_down, final_norm_g):
    B, S, D = x.shape
    inv_freq = jnp.exp(-math.log(ROPE_THETA) * jnp.arange(0, ROT_DIM, 2, dtype=jnp.float32) / ROT_DIM)
    ang = positions.astype(jnp.float32)[:, None, :, None] * inv_freq
    cos, sin = jnp.cos(ang), jnp.sin(ang)
    lower_bounds = jnp.cumsum(jax.nn.softmax(hgrn_lb_logits.astype(jnp.float32), axis=0), axis=0)
    splits = [HGRN_WIDTH, 2 * HGRN_WIDTH, 3 * HGRN_WIDTH, 4 * HGRN_WIDTH,
              4 * HGRN_WIDTH + ATTN_WIDTH, 4 * HGRN_WIDTH + 2 * ATTN_WIDTH]
    for l in range(DEPTH):
        mod = jax.nn.silu(c) @ w_ada[l] + b_ada[l]
        shift1, scale1, gate1, shift2, scale2, gate2 = jnp.split(mod[:, None, :], N_MOD, axis=-1)

        h = rms_norm(x, norm1_g[l]) * (1.0 + scale1) + shift1
        proj = h @ w_in[l]
        hq, hf, hi, hg, aq, ak, av = jnp.split(proj, splits, axis=-1)

        lb = lower_bounds[l]
        f = lb + (1.0 - lb) * jax.nn.sigmoid(hf.astype(jnp.float32))
        q_h = split_heads(jax.nn.silu(hq.astype(jnp.float32)) * HGRN_DK ** -0.5, HGRN_HEADS)
        k_h = split_heads(1.0 - f, HGRN_HEADS)
        v_h = split_heads(hi.astype(jnp.float32), HGRN_HEADS)
        o_h = hgrn2_recurrence(q_h, k_h, v_h, split_heads(jnp.log(f), HGRN_HEADS)).astype(x.dtype)
        o_h = rms_norm(o_h, hgrn_norm_g[l]) * jax.nn.silu(split_heads(hg, HGRN_HEADS))

        q_a = partial_rotary(split_heads(aq, ATTN_HEADS), cos, sin)
        k_a = partial_rotary(split_heads(ak, ATTN_HEADS), cos, sin)
        v_a = split_heads(av, ATTN_HEADS)
        o_a = rms_norm(moba_attention(q_a, k_a, v_a), attn_norm_g[l])

        mix = jnp.concatenate([merge_heads(o_h), merge_heads(o_a)], axis=-1) @ w_out[l]
        x = x + gate1 * mix

        h2 = rms_norm(x, norm2_g[l]) * (1.0 + scale2) + shift2
        y = moe_ffn(h2.reshape(B * S, D), w_router[l], b_router[l], w_gate_up[l],
                    b_gate_up[l], w_down[l], b_down[l]).reshape(B, S, D)
        x = x + gate2 * y
    return rms_norm(x, final_norm_g)


_drawn_inputs = setup_inputs


def setup_inputs(seed=0):
    import zlib

    import numpy as np

    out = dict(_drawn_inputs(seed))
    spreads = {}
    factors = {'norm1_g': 5.565,
     'hgrn_lb_logits': 3.691,
     'hgrn_norm_g': 7.068,
     'attn_norm_g': 40.224,
     'norm2_g': 16.255,
     'b_router': 29.782,
     'b_gate_up': 30.618,
     'b_down': 64.0,
     'final_norm_g': 8.311}
    for name, (base, spread) in spreads.items():
        noise = np.random.default_rng([zlib.crc32(name.encode()), seed]).standard_normal(out[name].shape)
        drawn = base * np.exp(spread * noise) if base else spread * noise
        out[name] = __import__('jax').numpy.asarray(drawn.astype(out[name].dtype))
    for name, factor in factors.items():
        out[name] = (out[name] * factor).astype(out[name].dtype)
    return out
```

```python
import math
from contextlib import ExitStack

import numpy as np
import concourse.bass as bass
from concourse import mybir

F32 = mybir.dt.float32
F32R = mybir.dt.float32r
I32 = mybir.dt.int32
U32 = mybir.dt.uint32
U8 = mybir.dt.uint8
ALU = mybir.AluOpType
ACT = mybir.ActivationFunctionType
AX = mybir.AxisListType

P = 128
D = 1024
T = 256
TT = T // P
KC = D // P
HEADS = 6
HW_ = HEADS * P
AH = 4
HD = 64
AW = AH * HD
ROT = HD // 4
HALF = ROT // 2
THETA = 500000.0
NE = 32
TOPK = 4
FF = D
CAP = 64
PASSES = T // CAP
EPS = 1e-6
ALPHA = 1.702
LIMIT = 7.0

U = 2048
SLOTS = 12
PRE = 4
GU_UNITS = 4
NU = 12
SPLIT = 10
HB = 3
LB = 2
WIN_UNITS = 15
CG = 256
NEG = -1e30


def stream_plan():
    plan = [("ada1", k) for k in range(KC)]
    for j in range(WIN_UNITS):
        plan += [("win", j), ("ada2", j)]
    plan.append(("ada2", WIN_UNITS))
    plan += [("wout", j) for j in range(D // CG)]
    return plan


def decoder_block(nc, x, c, positions, w_ada, b_ada, norm1_g, w_in, lb_logits, hgrn_g, attn_g,
                  w_out, norm2_g, w_router, b_router, w_gate_up, b_gate_up, w_down, b_down,
                  final_g, out, debug=False):
    plan = stream_plan()
    place = {key: n for n, key in enumerate(plan)}

    win_col = [HW_ + CG * j for j in range(3)] + [CG * j for j in range(3)] \
        + [4 * HW_, 4 * HW_ + AW, 4 * HW_ + 2 * AW] \
        + [2 * HW_ + CG * j for j in range(3)] + [3 * HW_ + CG * j for j in range(3)]

    with ExitStack() as ctx:
        def sb(name, shape, dt=F32):
            return ctx.enter_context(nc.sbuf_tensor(name, shape, dt))

        def sem(name):
            return ctx.enter_context(nc.semaphore(name))

        ps = ctx.enter_context(nc.psum_tensor("ps", [P, 8 * 512], F32))

        def bank(b, n=1):
            return ps[:, b * 512:(b + n) * 512]

        ring = sb("ring", [P, SLOTS * U])
        whi = sb("whi", [P, HB, U], F32R)
        wlo = sb("wlo", [P, LB, U], F32R)
        xg = sb("xg", [P, KC, 2, CAP], F32R)
        at = sb("at", [P, 4, 2, CAP], F32R)
        xs = sb("xs", [P, TT, D])
        hb = sb("hb", [P, TT, D])
        ht = sb("ht", [P, KC, T])
        mod = sb("mod", [P, 4, D])
        yacc = sb("yacc", [P, TT, D])

        def slot(s):
            return ring[:, s * U:(s + 1) * U]

        arena_at = [PRE * U]

        def arena(n):
            a = arena_at[0]
            arena_at[0] += n
            assert arena_at[0] <= SLOTS * U
            return ring[:, a:a + n]

        fg = arena(HEADS * T).rearrange("p (h t) -> p h t", h=HEADS)
        qd = arena(HEADS * T).rearrange("p (h t) -> p h t", h=HEADS)
        kd = arena(HEADS * T).rearrange("p (h t) -> p h t", h=HEADS)
        tot = arena(HEADS * T)
        sct = arena(HEADS * T)
        cross = arena(HEADS * P)
        aqk = arena(TT * 2 * AW)
        av = arena(TT * AW).rearrange("p (t n) -> p t n", t=TT)
        qkt = arena(4 * T).rearrange("p (c t) -> p c t", c=4)
        pb = arena(12 * P).rearrange("p (b s) -> p b s", b=12)
        pt = arena(12 * P).rearrange("p (b s) -> p b s", b=12)
        hgate = arena(TT * HW_).rearrange("p (t n) -> p t n", t=TT)
        masks = arena(8 * P // 4).bitcast(U8).rearrange("p (l t) -> p l t", l=8)
        cmask = arena(P)
        hgrow = arena(P)
        agrow = arena(HD)
        lbt = arena(HEADS * 2)
        omlb = arena(HEADS)
        assert arena_at[0] <= SLOTS * U

        tmp = sb("tmp", [P, 512])
        tmp2 = sb("tmp2", [P, 512])
        guT = sb("guT", [P, 8, CAP])
        sgz = sb("sgz", [P, 4, 2, CAP])
        pe_ = sb("pe_", [P, TT, CAP])
        gts = sb("gts", [P, T])
        bgu = sb("bgu", [P, NE, 16])
        posx = sb("posx", [P, TT, PASSES * NE + 1])
        gate = sb("gate", [P, TT, NE])
        msk = sb("msk", [P, TT, NE])
        wr = sb("wr", [P, KC, NE])
        br = sb("br", [P, NE])
        ident = sb("ident", [P, P])
        twin = sb("twin", [P, CAP])
        ones = sb("ones", [P, P])
        tri = sb("tri", [P, P])
        iota_s = sb("iota_s", [P, TT, CAP])
        iota_e = sb("iota_e", [P, NE])
        small = sb("small", [P, 160])
        ismall = sb("ismall", [P, 8], U32)
        count_i = sb("count_i", [P, 1], I32)
        sg = sgz[:, :, 0, :]
        pg = tmp[:, 0:TT * 2 * CAP].rearrange("p (t a s) -> p t a s", t=TT, a=2)
        crow = small[:, 0:8]
        csil = small[:, 8:16]
        ssq = small[:, 16:18]
        rstd = small[:, 18:20]
        post = small[:, 20:22]
        sums = small[:, 24:36]
        rs2 = small[:, 36:48]
        amax = small[:, 48:56]
        asum = small[:, 56:64]
        v8 = small[:, 64:72]
        e4 = small[:, 72:76]
        idf = small[:, 76:84]
        esum = small[:, 84:85]
        cnt = small[:, 86:90]
        invf = small[:, 92:100]
        csn = small[:, 100:148]
        posi = sb("posi", [P, TT], I32)
        gateT = tmp2[0:NE, 0:T]
        a1 = yacc[:, 0, :]
        b1 = yacc[:, 1, :]
        vh = yacc[:, :, :].rearrange("p t d -> p (t d)")[:, 0:TT * HW_].rearrange("p (t n) -> p t n", t=TT)
        crep = ht[:, :, 0:P]
        g1row = hb[:, 0, :]
        gu_a = mod[:, 0, :]
        gu_b = mod[:, 1, :]
        outs = mod[:, 2, :]
        gate2 = mod[:, 3, :]
        gfin = hb[:, 1, :]

        ld = {n: sem("ld_" + n) for n in
              "x c pos g1 ada1_bias ada2_bias lb bgu hg ag wr br g2 bdown gfin".split()}
        raw = [sem(f"raw{s}") for s in range(SLOTS)]
        sig = {n: sem("s_" + n) for n in
               """ident consts masks_iota csil crep lbT lb_read lb_done bguT bgu_read ssq rsq rstd
               h1 h1T h1T_act h1T_dve sin_arg sins rot aT aT_copied sc_even sc sc_read sc_ready expd pT pT_copied
               o_att o_att_read aatt_ms aatt_sq cross cross_copied oh oh_sq oh_ms oh_rs oh_read hg_read hg_cat
               oT oT_act oT_dve ada2 mod_copied acc0 x1 ssq2 rms2 rs2 h2 h2T h2T_act h2T_dve logits v8 e4
               routed cum gT gT_copied yinit yinit_copied npass out_rms out_ssq out_rs fin stored ofin""".split()}
        win_sig = sem("win_sig")
        act_evac = sem("act_evac")
        ada_pe = sem("ada_pe")
        win_pe = sem("win_pe")
        wout_pe = sem("wout_pe")
        ada_dve = sem("ada_dve")
        lev_done = [sem(f"lev_done{g}") for g in range(2)]
        q_upd = [sem(f"q_upd{g}") for g in range(2)]
        k_upd = [sem(f"k_upd{g}") for g in range(2)]
        tot_upd = sem("tot_upd")
        hq_ready = sem("hq_ready")
        hk_ready = sem("hk_ready")
        sct_done = sem("sct_done")
        dve_c = sem("dve_c")
        act_c = sem("act_c")
        pool_c = sem("pool_c")
        hi_rdy = sem("hi_rdy")
        lo_rdy = sem("lo_rdy")
        used = sem("used")
        m = {n: sem("m_" + n) for n in
             """xg_hi xg ga p pg gt gt_cp gua_cp gub_cp ta tb bias_a bias_b g_a g_b sig_a sig_b
             a_a a_b ah_a al_a cb0 cb1 y0 y1 out_cp u_a u_b t""".split()}

        def buffer_user(u, n):
            return u - n + 1 + NU if u >= n else max(v for v in range(SPLIT) if v % n == u) + 1

        block = ctx.enter_context(nc.Block())

        raw_base = [0] * SLOTS
        for n in range(len(plan)):
            raw_base[n % PRE] += 16

        def landed(eng, key):
            n = place[key]
            eng.wait_ge(raw[n % PRE], 16 * (n // PRE + 1))

        def used_by(eng, key):
            kind, j = key
            s = {"ada1": ada_pe, "win": win_pe, "wout": wout_pe, "ada2": ada_dve}[kind]
            eng.wait_ge(s, j + 1)

        ada_v = w_ada.rearrange("l (p k) n -> l p k n", k=KC)
        win_v = w_in.rearrange("l (k p) n -> l p k n", p=P)
        wout_v = w_out.rearrange("l (k p) n -> l p k n", p=P)
        x_v = x.rearrange("b (t p) d -> (b p) t d", p=P)
        out_v = out.rearrange("b (t p) d -> (b p) t d", p=P)

        def unit_src(kind, j):
            if kind == "ada1":
                return ada_v[0, :, j, 0:U]
            if kind == "ada2":
                return ada_v[0, :, j % KC, U * (1 + j // KC):U * (2 + j // KC)]
            if kind == "win":
                return win_v[0, :, :, win_col[j]:win_col[j] + CG]
            return wout_v[0, :, :, CG * j:CG * (j + 1)]

        def model_chunk(k):
            return slice(k // 2 * 2 * P + k % 2, (k // 2 + 1) * 2 * P, 2)

        def expert_load(sp, e, u):
            dst = slot(u)
            if u < 2 * GU_UNITS:
                half, k2 = u // GU_UNITS, u % GU_UNITS
                src = w_gate_up[0, e, k2 * 2 * P:(k2 + 1) * 2 * P, :]
                src = src.rearrange("(p k) (g n) -> p (k g) n", p=P, g=2)[:, :, half * 512:(half + 1) * 512]
                sp.dma_start(dst.rearrange("p (k n) -> p k n", k=4), src).then_inc(raw[u], 16)
            else:
                k2 = u - 2 * GU_UNITS
                src = w_down[0, e, k2 * 2 * P:(k2 + 1) * 2 * P, :].rearrange("(k p) n -> p k n", p=P)
                sp.dma_start(dst.rearrange("p (k n) -> p k n", k=2), src).then_inc(raw[u], 16)

        @block.sync
        def _(sp):
            for n, (kind, j) in enumerate(plan):
                if n >= PRE:
                    used_by(sp, plan[n - PRE])
                src = unit_src(kind, j)
                dst = slot(n % PRE)
                if kind in ("win", "wout"):
                    dst = dst.rearrange("p (k n) -> p k n", k=KC)
                sp.dma_start(dst, src).then_inc(raw[n % PRE], 16)
            if debug:
                sp.wait_ge(sig["x1"], D // CG)
                sp.wait_ge(ld["wr"], 16)
                sp.wait_ge(ld["br"], 16)
                sp.dma_start(out_v, xs[:, :, :]).then_inc(sig["stored"], 16)
                sp.wait_ge(sig["stored"], 16)
                return
            sp.wait_ge(sig["hg_cat"], TT)
            for u in range(PRE, NU):
                expert_load(sp, 0, u)
            sp.wait_ge(wout_pe, D // CG)
            for u in range(PRE):
                expert_load(sp, 0, u)
            sp.wait_ge(sig["npass"], 1)
            turns = sp.value_load(count_i[0:1, 0:1], min_val=NE, max_val=NE * PASSES)
            with sp.Fori(1, turns) as i:
                e = sp.snap(i & (NE - 1))
                done = sp.snap(i >> (NE.bit_length() - 1))
                for u in range(NU):
                    if u < SPLIT:
                        sp.wait_ge(lo_rdy, done * (NE * SPLIT) + e * SPLIT + (u + 1))
                    else:
                        sp.wait_ge(used, done * (NE * NU) + e * NU + (u + 1))
                    expert_load(sp, e, u)
            sp.wait_ge(sig["fin"], 1)
            sp.dma_start(out_v, xs[:, :, :]).then_inc(sig["stored"], 16)
            sp.wait_ge(sig["stored"], 16)

        def block_decay(n, g=None):
            if n == 1:
                v = fg if g is None else fg[:, 3 * g:3 * g + 3, :]
                return v.rearrange("p h (b r) -> p (h b) r", r=2)
            off = 0
            k = 2
            while k < n:
                off += HEADS * T // k
                k *= 2
            w = HEADS * T // n
            v = tot[:, off:off + w]
            if g is not None:
                v = v[:, g * w // 2:(g + 1) * w // 2]
            return v.rearrange("p (b r) -> p b r", r=2)

        @block.gpsimd
        def _(pool):
            own = [0]

            def link(ins):
                own[0] += 1
                ins.then_inc(pool_c, 1)
                pool.wait_ge(pool_c, own[0])

            link(pool.memset(ident[:, :], 0.0))
            pool.affine_select(out=ident[:, :], in_=ident[:, :], compare_op=ALU.not_equal, fill=1.0,
                               base=0, pattern=[[-1, P]], channel_multiplier=1).then_inc(sig["ident"], 1)
            link(pool.memset(twin[:, :], 0.0))
            for off in (0, CAP):
                link(pool.affine_select(out=twin[:, :], in_=twin[:, :], compare_op=ALU.not_equal, fill=1.0,
                                        base=-off, pattern=[[-1, CAP]], channel_multiplier=1))
            pool.memset(ones[:, :], 1.0).then_inc(sig["consts"], 1)
            pool.iota(tmp[:, 0:P].bitcast(I32), pattern=[[0, P]], base=0, channel_multiplier=1)
            pool.iota(tmp[:, P:2 * P].bitcast(I32), pattern=[[1, P]], base=0,
                      channel_multiplier=0).then_inc(sig["masks_iota"], 1)
            link(pool.memset(tri[:, :], 1.0))
            pool.affine_select(out=tri[:, :], in_=tri[:, :], compare_op=ALU.is_ge, fill=0.0,
                               base=0, pattern=[[1, P]], channel_multiplier=-1)
            link(pool.memset(cmask, 0.0))
            pool.affine_select(out=cmask, in_=cmask, compare_op=ALU.is_ge, fill=NEG,
                               base=0, pattern=[[-1, P]], channel_multiplier=1)
            for j in range(HALF):
                v = float(np.exp(np.float32(-math.log(THETA)) * np.float32(2 * j) / np.float32(ROT)))
                pool.memset(invf[:, j:j + 1], v)
            pool.iota(iota_s[:, :, :], pattern=[[0, TT], [1, CAP]], base=0, channel_multiplier=0,
                      allow_small_or_imprecise_dtypes=True)
            pool.iota(iota_e[:, :], pattern=[[1, NE]], base=0, channel_multiplier=0,
                      allow_small_or_imprecise_dtypes=True)
            pool.memset(gts[:, :], 0.0).then_inc(m["gt_cp"], 1)
            pool.memset(sgz[:, :, :, :], 0.0)
            pool.memset(posx[:, :, :], -1.0)
            pool.memset(sct, 0.0).then_inc(sig["consts"], 1)

            for lv in range(1, 8):
                n = 1 << (lv - 1)
                for g in range(2):
                    if lv == 1:
                        pool.wait_ge(hk_ready, 3)
                    else:
                        pool.wait_ge(tot_upd, lv - 1)
                    pool.wait_ge(lev_done[g], lv + 1)
                    kv = kd[:, 3 * g:3 * g + 3, :].rearrange("p h (b r n) -> p (h b) r n", r=2, n=n)[:, :, 0, :]
                    right = block_decay(n, g)[:, :, 1]
                    nb = 3 * T // (2 * n)
                    pool.tensor_tensor(kv, kv, right.unsqueeze(2).to_broadcast([P, nb, n]),
                                       ALU.mult).then_inc(k_upd[g], 1)
            if debug:
                return
            pool.wait_ge(sig["npass"], 1)

            turns = pool.value_load(count_i[0:1, 0:1], min_val=NE, max_val=NE * PASSES)
            with pool.Fori(0, turns) as i:
                e = pool.snap(i & (NE - 1))
                pool.wait_ge(m["p"], i + 1)
                pool.wait_ge(m["gt_cp"], i + 1)
                pool.tensor_tensor(pg[:, :, :, :], pe_[:, :, :].unsqueeze(2).to_broadcast([P, TT, 2, CAP]),
                                   gate[:, :, bass.ds(e, 1)].unsqueeze(3).to_broadcast([P, TT, 2, CAP]),
                                   ALU.mult).then_inc(m["pg"], 1)

        @block.scalar
        def _(act):
            own = [0]

            def link(ins):
                own[0] += 1
                ins.then_inc(act_c, 1)
                act.wait_ge(act_c, own[0])

            A = nc.scalar.activation
            act.dma_start(small[:, 0:8], c.rearrange("b (p k) -> (b p) k", p=P)).then_inc(ld["c"], 16)
            act.dma_start(xs[:, :, :], x_v).then_inc(ld["x"], 16)
            act.dma_start(yacc[0:1, :, :].rearrange("p t d -> p (t d)"), b_ada[0:1, 0:U]).then_inc(ld["ada1_bias"], 16)
            act.dma_start(hb[:, 0, :], norm1_g.to_broadcast([P, D])).then_inc(ld["g1"], 16)
            act.dma_start(tmp2[0:12, 0:P], lb_logits.rearrange("l (h p) -> (l h) p", p=P)).then_inc(ld["lb"], 16)
            act.dma_start(posi[:, :], positions.rearrange("b (t p) -> p (b t)", p=P),
                          allow_slow_non_contiguous=True).then_inc(ld["pos"], 16)
            act.dma_start(guT[:, :, :].rearrange("p c s -> p (c s)").rearrange("p (a f) -> p a f", a=4),
                          b_gate_up.rearrange("l e (c f) -> (l e c) f", f=P)
                          .rearrange("(a r) f -> r a f", r=P)).then_inc(ld["bgu"], 16)
            act.dma_start(hgrow, hgrn_g.to_broadcast([P, P])).then_inc(ld["hg"], 16)
            act.dma_start(agrow, attn_g.to_broadcast([P, HD])).then_inc(ld["ag"], 16)
            act.dma_start(br[:, :], b_router.to_broadcast([P, NE])).then_inc(ld["br"], 16)
            act.dma_start(wr[:, :, :], w_router[0].rearrange("(k p) e -> p k e", p=P)).then_inc(ld["wr"], 16)
            act.wait_ge(sig["acc0"], 1)
            act.dma_start(mod[0:1, :, :].rearrange("p a d -> p (a d)"), b_ada[0:1, U:3 * U]).then_inc(ld["ada2_bias"], 16)

            act.wait_ge(ld["c"], 16)
            A(csil, crow, ACT.Sigmoid).then_inc(sig["csil"], 1)
            act.wait_ge(ld["x"], 16)
            for t in range(TT):
                A(slot(PRE + t)[:, 0:D], xs[:, t, :], ACT.Square, accum_out=ssq[:, t:t + 1]).then_inc(sig["ssq"], 1)
            act.wait_ge(sig["lbT"], 2)
            A(lbt, lbt, ACT.Exp).then_inc(sig["lb_done"], 1)
            act.wait_ge(sig["sin_arg"], 1)
            link(A(csn[:, 32:48], csn[:, 16:32], ACT.Sin, scale=0.5))
            A(csn[:, 16:32], csn[:, 16:32], ACT.Sin).then_inc(sig["sins"], 1)
            act.wait_ge(sig["rsq"], 1)
            A(rstd, rstd, ACT.Sqrt).then_inc(sig["rstd"], 1)

            def half_copy(name):
                act.wait_ge(sig[name], 1)
                nc.scalar.copy(ht[:, 0:KC // 2, :].rearrange("p k t -> p (k t)"), bank(4, 2)).then_inc(sig[name + "_act"], 1)

            half_copy("h1T")

            def group(j):
                b = 6 + j % 2
                act.wait_ge(win_pe, j + 1)
                wide = bank(b).rearrange("p (t n) -> p t n", t=TT)
                if j < 3:
                    A(fg[:, 2 * j:2 * j + 2, :].rearrange("p h t -> p (h t)"), bank(b), ACT.Sigmoid).then_inc(win_sig, 1)
                elif j < 6:
                    A(qd[:, 2 * (j - 3):2 * (j - 3) + 2, :].rearrange("p h t -> p (h t)"), bank(b),
                      ACT.Sigmoid).then_inc(win_sig, 1)
                elif j < 8:
                    nc.scalar.copy(aqk.rearrange("p (t n) -> p t n", t=TT)[:, :, (j - 6) * AW:(j - 5) * AW],
                                   wide).then_inc(act_evac, 1)
                elif j == 8:
                    nc.scalar.copy(av, wide).then_inc(act_evac, 1)
                elif j < 12:
                    nc.scalar.copy(vh[:, :, (j - 9) * CG:(j - 8) * CG], wide).then_inc(act_evac, 1)
                else:
                    A(hgate[:, :, (j - 12) * CG:(j - 11) * CG], wide, ACT.Sigmoid).then_inc(win_sig, 1)

            for j in range(WIN_UNITS):
                if j == 9:
                    act.wait_ge(sig["aT"], 1)
                    nc.scalar.copy(qkt.rearrange("p c t -> p (c t)"), bank(3, 2)).then_inc(sig["aT_copied"], 1)
                if j == 11:
                    act.wait_ge(sig["sc_ready"], 1)
                    A(pb.rearrange("p b s -> p (b s)"), pb.rearrange("p b s -> p (b s)"), ACT.Exp).then_inc(sig["expd"], 1)
                if j == 12:
                    act.wait_ge(sig["pT"], 1)
                    nc.scalar.copy(pt.rearrange("p b s -> p (b s)"), bank(3, 3)).then_inc(sig["pT_copied"], 1)
                if j == 14:
                    act.wait_ge(sig["aatt_ms"], 1)
                    A(asum, asum, ACT.Sqrt).then_inc(sig["aatt_sq"], 1)
                group(j)
            act.wait_ge(sig["cross"], 1)
            nc.scalar.copy(cross, ps[:, 0:HEADS * P]).then_inc(sig["cross_copied"], 1)
            act.wait_ge(sig["oh"], 1)
            A(fg.rearrange("p h t -> p (h t)"), bank(3, 3), ACT.Square).then_inc(sig["oh_sq"], 1)
            act.wait_ge(sig["oh_ms"], 1)
            A(rs2, rs2, ACT.Sqrt).then_inc(sig["oh_rs"], 1)
            for j in range(8):
                act.wait_ge(sig["ada2"], j + 1)
                nc.scalar.copy(mod[:, j // 2, (j % 2) * 512:(j % 2 + 1) * 512], bank(6 + j % 2)).then_inc(sig["mod_copied"], 1)
            half_copy("oT")
            if debug:
                return
            act.wait_ge(sig["hg_cat"], TT)
            act.dma_start(yacc[:, 0, :], norm2_g.to_broadcast([P, D])).then_inc(ld["g2"], 16)
            act.wait_ge(sig["x1"], D // CG)
            act.dma_start(mod[0:NE, 0, :], b_down[0]).then_inc(ld["bdown"], 16)
            for t in range(TT):
                A(hb[:, t, :], xs[:, t, :], ACT.Square, accum_out=ssq[:, t:t + 1]).then_inc(sig["ssq2"], 1)
            act.wait_ge(sig["rms2"], 1)
            A(rstd, rstd, ACT.Sqrt).then_inc(sig["rs2"], 1)
            half_copy("h2T")
            for t in range(TT):
                act.wait_ge(sig["v8"], t + 1)
                A(e4, e4, ACT.Exp).then_inc(sig["e4"], 1)
            act.wait_ge(sig["gT"], 1)
            nc.scalar.copy(gateT, ps[0:NE, 512 * 2:512 * 2 + T]).then_inc(sig["gT_copied"], 1)

            act.wait_ge(m["ga"], 1)
            nc.scalar.copy(xg[:, :, 0, :], bank(5).rearrange("p (k s) -> p k s", k=KC)).then_inc(m["xg_hi"], 1)
            act.wait_ge(sig["yinit_copied"], 1)
            turns = act.value_load(count_i[0:1, 0:1], min_val=NE, max_val=NE * PASSES)
            with act.Fori(0, turns) as i:
                def hi(u):
                    act.wait_ge(raw[u], i * 16 + (raw_base[u] + 16))
                    act.wait_ge(used, i * NU + buffer_user(u, HB))
                    nc.scalar.copy(whi[:, u % HB, :], slot(u)).then_inc(hi_rdy, 1)

                def silu_part(s):
                    act.wait_ge(m["g_" + s], i + 1)
                    A(sg, guT[:, 0:4, :], ACT.Sigmoid, scale=ALPHA).then_inc(m["sig_" + s], 1)

                hi(0)
                hi(1)
                hi(2)
                act.wait_ge(used, i * NU + NU)
                nc.scalar.copy(outs, bank(6, 2)).then_inc(m["out_cp"], 1)
                for u in range(3, 7):
                    hi(u)
                act.wait_ge(used, i * NU + (NU + GU_UNITS))
                nc.scalar.copy(gu_a, bank(0, 2)).then_inc(m["gua_cp"], 1)
                hi(7)
                hi(8)
                silu_part("a")
                act.wait_ge(m["a_a"], i + 1)
                nc.scalar.copy(at[:, :, 0, :], sg).then_inc(m["ah_a"], 1)
                hi(9)
                act.wait_ge(used, i * NU + (NU + 2 * GU_UNITS))
                nc.scalar.copy(gu_b, bank(2, 2)).then_inc(m["gub_cp"], 1)
                act.wait_ge(m["ga"], i + 2)
                nc.scalar.copy(xg[:, :, 0, :], bank(5).rearrange("p (k s) -> p k s", k=KC)).then_inc(m["xg_hi"], 1)
                silu_part("b")
                act.wait_ge(m["gt"], i + 1)
                nc.scalar.copy(gts[:, :], ps[:, 4 * 512:4 * 512 + T]).then_inc(m["gt_cp"], 1)
            act.wait_ge(used, turns * NU + NU)
            nc.scalar.copy(outs, bank(6, 2)).then_inc(m["out_cp"], 1)
            act.dma_start(gfin, final_g.rearrange("(a d) -> a d", a=1).to_broadcast([P, D])).then_inc(ld["gfin"], 16)
            for t in range(TT):
                act.wait_ge(sig["ofin"], t + 1)
                A(ht[:, 4 * t:4 * t + 4, :].rearrange("p k t -> p (k t)"), xs[:, t, :], ACT.Square, accum_out=ssq[:, t:t + 1]).then_inc(sig["out_ssq"], 1)
            act.wait_ge(sig["out_rms"], 1)
            A(rstd, rstd, ACT.Sqrt).then_inc(sig["out_rs"], 1)

        @block.tensor
        def _(pe):
            mm = nc.tensor.matmul

            def turn_all(src, name, ready):
                for t in range(TT):
                    pe.wait_ge(ready, t + 1)
                    for k in range(KC):
                        last = nc.tensor.transpose(ps[:, 2048 + k * T + t * P:2048 + k * T + (t + 1) * P],
                                                   src[:, t, k * P:(k + 1) * P], ident[:, :])
                last.then_inc(sig[name], 1)

            pe.wait_ge(sig["ident"], 1)
            pe.wait_ge(ld["lb"], 16)
            nc.tensor.transpose(ps[:, 2048:2048 + 12], tmp2[0:12, 0:P], ident[0:12, 0:12]).then_inc(sig["lbT"], 1)
            pe.wait_ge(ld["bgu"], 16)
            bsrc = guT[:, :, :].rearrange("p c s -> p (c s)")
            for a in range(4):
                last = nc.tensor.transpose(ps[:, 2560 + a * P:2560 + (a + 1) * P], bsrc[:, a * P:(a + 1) * P], ident[:, :])
            last.then_inc(sig["bguT"], 1)
            pe.wait_ge(sig["consts"], 2)
            pe.wait_ge(ld["ada1_bias"], 16)
            for b in range(4):
                mm(bank(b), ones[0:1, :], yacc[0:1, :, :].rearrange("p t d -> p (t d)")[:, b * 512:(b + 1) * 512],
                   start=True, stop=False)
            pe.wait_ge(sig["crep"], 1)
            for k in range(KC):
                landed(pe, ("ada1", k))
                w = slot(place[("ada1", k)] % PRE)
                for b in range(4):
                    last = mm(bank(b), crep[:, k, :], w[:, b * 512:(b + 1) * 512], start=False, stop=(k == KC - 1))
                last.then_inc(ada_pe, 1)

            pe.wait_ge(sig["lb_read"], 1)
            pe.wait_ge(sig["bgu_read"], 1)
            turn_all(hb, "h1T", sig["h1"])
            pe.wait_ge(sig["h1T_act"], 1)
            pe.wait_ge(sig["h1T_dve"], 1)

            def level(lv):
                b0 = 3 * (lv % 2)
                if lv > 1:
                    pe.wait_ge(sct_done, lv - 1)
                for g in range(2):
                    if lv == 0:
                        pe.wait_ge(hq_ready, 3)
                        pe.wait_ge(hk_ready, 3)
                    else:
                        pe.wait_ge(q_upd[g], lv)
                        if lv > 1:
                            pe.wait_ge(k_upd[g], lv - 1)
                    for h in range(3 * g, 3 * g + 3):
                        for t in range(TT):
                            j = h * TT + t
                            last = mm(ps[:, b0 * 512 + j * P:b0 * 512 + (j + 1) * P], kd[:, h, t * P:(t + 1) * P],
                                      qd[:, h, t * P:(t + 1) * P], start=True, stop=True)
                    last.then_inc(lev_done[g], 1)

            def attention_turn():
                pe.wait_ge(sct_done, 2)
                pe.wait_ge(sig["rot"], 1)
                for ch in range(4):
                    for t in range(TT):
                        last = nc.tensor.transpose(ps[:, 3 * 512 + ch * T + t * P:3 * 512 + ch * T + (t + 1) * P],
                                                   aqk[:, t * 2 * AW + ch * P:t * 2 * AW + (ch + 1) * P], ident[:, :])
                last.then_inc(sig["aT"], 1)

            def attention_scores():
                pe.wait_ge(sct_done, 3)
                pe.wait_ge(sig["aT_copied"], 1)
                for n, h in enumerate((0, 2, 1, 3)):
                    if n == 2:
                        pe.wait_ge(sig["sc_even"], 1)
                    r = slice(HD * (h % 2), HD * (h % 2) + HD)
                    q, k = qkt[r, h // 2, :], qkt[r, 2 + h // 2, :]
                    mm(ps[:, h * P:(h + 1) * P], q[:, 0:P], k[:, 0:P], start=True, stop=True)
                    last = mm(ps[:, (4 + 2 * h) * P:(6 + 2 * h) * P], q[:, P:T], k, start=True, stop=True)
                    if n == 1:
                        last.then_inc(sig["sc_even"], 1)
                last.then_inc(sig["sc"], 1)

            def attention_pt():
                pe.wait_ge(sct_done, 6)
                pe.wait_ge(sig["expd"], 1)
                for j in range(12):
                    last = nc.tensor.transpose(ps[:, 3 * 512 + j * P:3 * 512 + (j + 1) * P], pb[:, j, :], ident[:, :])
                last.then_inc(sig["pT"], 1)

            def attention_out():
                pe.wait_ge(sig["pT_copied"], 1)
                for h in range(AH):
                    o = ps[:, 3 * 512 + h * HD:3 * 512 + (h + 1) * HD]
                    mm(o, pt[:, h, :], av[:, 0, h * HD:(h + 1) * HD], start=True, stop=True)
                    o = ps[:, 3 * 512 + AW + h * HD:3 * 512 + AW + (h + 1) * HD]
                    for s in range(TT):
                        last = mm(o, pt[:, 4 + 2 * h + s, :], av[:, s, h * HD:(h + 1) * HD],
                                  start=(s == 0), stop=(s == 1))
                last.then_inc(sig["o_att"], 1)

            for j in range(WIN_UNITS):
                b = 6 + j % 2
                if j >= 2:
                    r = j - 2
                    s, v = (win_sig, r + 1) if r < 3 else (hq_ready, r - 2) if r < 6 else \
                        (act_evac, r - 5) if r < 12 else (sig["hg_read"], r - 11)
                    pe.wait_ge(s, v)
                landed(pe, ("win", j))
                w = slot(place[("win", j)] % PRE).rearrange("p (k n) -> p k n", k=KC)
                for i2 in range(2):
                    o = ps[:, b * 512 + i2 * T:b * 512 + (i2 + 1) * T]
                    for k in range(KC):
                        if j < 6:
                            last = mm(o, w[:, k, i2 * P:(i2 + 1) * P], ht[:, k, :], start=(k == 0), stop=(k == KC - 1))
                        else:
                            last = mm(o, ht[:, k, i2 * P:(i2 + 1) * P], w[:, k, :], start=(k == 0), stop=(k == KC - 1))
                last.then_inc(win_pe, 1)
                if j == 7:
                    level(0)
                if j == 8:
                    level(1)
                    level(2)
                    attention_turn()
                if j == 9:
                    attention_scores()
                    level(3)
                if j == 10:
                    pe.wait_ge(sig["sc_read"], 1)
                    level(4)
                if j == 11:
                    level(5)
                    attention_pt()
                if j == 12:
                    attention_out()
                    level(6)
                if j == 13:
                    pe.wait_ge(sig["o_att_read"], 1)
                    level(7)
            pe.wait_ge(sct_done, 7)
            for g in range(2):
                pe.wait_ge(q_upd[g], 8)
                pe.wait_ge(k_upd[g], 7)
            for h in range(HEADS):
                last = mm(ps[:, h * P:(h + 1) * P], kd[:, h, 0:P], qd[:, h, P:T], start=True, stop=True)
            last.then_inc(sig["cross"], 1)
            pe.wait_ge(sct_done, 8)
            pe.wait_ge(act_evac, 6)
            pe.wait_ge(sig["cross_copied"], 1)
            sc4 = sct.rearrange("p (h t n) -> p h t n", h=HEADS, t=TT)
            for h in range(HEADS):
                for t in range(TT):
                    o = ps[:, 3 * 512 + (2 * h + t) * P:3 * 512 + (2 * h + t + 1) * P]
                    last = mm(o, sc4[:, h, t, :], vh[:, t, h * P:(h + 1) * P], start=True, stop=(t == 0))
                    if t == 1:
                        last = mm(o, cross[:, h * P:(h + 1) * P], vh[:, 0, h * P:(h + 1) * P], start=False, stop=True)
            last.then_inc(sig["oh"], 1)
            for j in range(8):
                b = 6 + j % 2
                if j < 2:
                    pe.wait_ge(sig["hg_read"], 3)
                else:
                    pe.wait_ge(sig["mod_copied"], j - 1)
                pe.wait_ge(ada_dve, KC * (1 + j // 4))
                mm(bank(b), ones[:, :], mod[:, j // 2, (j % 2) * 512:(j % 2 + 1) * 512],
                   start=True, stop=True).then_inc(sig["ada2"], 1)
            pe.wait_ge(sig["mod_copied"], 8)
            turn_all(hb, "oT", sig["hg_cat"])
            pe.wait_ge(sig["oT_act"], 1)
            pe.wait_ge(sig["oT_dve"], 1)
            for j in range(D // CG):
                landed(pe, ("wout", j))
                w = slot(place[("wout", j)] % PRE).rearrange("p (k n) -> p k n", k=KC)
                for t in range(TT):
                    for k in range(KC):
                        last = mm(ps[:, j * 512 + t * CG:j * 512 + (t + 1) * CG], ht[:, k, t * P:(t + 1) * P],
                                  w[:, k, :], start=(k == 0), stop=(k == KC - 1))
                last.then_inc(wout_pe, 1)
            if debug:
                return
            turn_all(hb, "h2T", sig["h2"])
            pe.wait_ge(sig["h2T_act"], 1)
            pe.wait_ge(sig["h2T_dve"], 1)
            pe.wait_ge(ld["wr"], 16)
            for t in range(TT):
                for k in range(KC):
                    last = mm(ps[:, t * NE:(t + 1) * NE], ht[:, k, t * P:(t + 1) * P], wr[:, k, :],
                              start=(k == 0), stop=(k == KC - 1))
            last.then_inc(sig["logits"], 1)
            pe.wait_ge(sig["routed"], 1)
            mm(ps[:, 512:512 + NE], tri[:, :], msk[:, 0, :], start=True, stop=True)
            mm(ps[:, 512 + NE:512 + 2 * NE], tri[:, :], msk[:, 1, :], start=True, stop=False)
            mm(ps[:, 512 + NE:512 + 2 * NE], ones[:, :], msk[:, 0, :], start=False, stop=True)
            mm(ps[:, 512 + 2 * NE:512 + 3 * NE], ones[:, :], msk[:, 0, :], start=True, stop=False)
            mm(ps[:, 512 + 2 * NE:512 + 3 * NE], ones[:, :], msk[:, 1, :], start=False, stop=True).then_inc(sig["cum"], 1)
            for t in range(TT):
                last = nc.tensor.transpose(ps[0:NE, 1024 + t * P:1024 + (t + 1) * P], gate[:, t, :], ident[:, :])
            last.then_inc(sig["gT"], 1)
            pe.wait_ge(sig["gT_copied"], 1)
            pe.wait_ge(ld["bdown"], 16)
            for t in range(TT):
                for n in range(2):
                    last = mm(bank((3, 4, 6, 7)[2 * t + n]), gateT[:, t * P:(t + 1) * P],
                              mod[0:NE, 0, n * 512:(n + 1) * 512], start=True, stop=True)
            last.then_inc(sig["yinit"], 1)

            def gather():
                for k in range(KC):
                    for t in range(TT):
                        last = mm(ps[:, 5 * 512 + k * CAP:5 * 512 + (k + 1) * CAP], hb[:, t, model_chunk(k)],
                                  pe_[:, t, :], start=(t == 0), stop=(t == TT - 1))
                last.then_inc(m["ga"], 1)

            def turn_gates():
                for t in range(TT):
                    last = nc.tensor.transpose(ps[:, 4 * 512 + t * P:4 * 512 + (t + 1) * P],
                                               pg[:, t, :, :].rearrange("p a s -> p (a s)"), ident[:, :])
                last.then_inc(m["gt"], 1)

            def combine():
                for t in (1, 0):
                    for n in range(2):
                        last = mm(bank((0, 6)[t] + n), gts[:, t * P:(t + 1) * P], outs[:, n * 512:(n + 1) * 512],
                                  start=True, stop=True)
                    last.then_inc(m["cb%d" % t], 1)

            def turn_gu(src, name):
                for ch in range(8):
                    last = mm(ps[:, 4 * 512 + ch * CAP:4 * 512 + (ch + 1) * CAP], src[:, ch * P:(ch + 1) * P],
                              twin[:, :], start=True, stop=True)
                last.then_inc(m[name], 1)

            pe.wait_ge(m["p"], 1)
            gather()
            pe.wait_ge(sig["yinit_copied"], 1)
            pe.wait_ge(sig["npass"], 1)
            turns = pe.value_load(count_i[0:1, 0:1], min_val=NE, max_val=NE * PASSES)
            with pe.Fori(0, turns) as i:
                def unit(u, b0, lhs, first):
                    k0 = 2 * (u % GU_UNITS)
                    for part, w in ((0, whi[:, u % HB, :]), (1, wlo[:, u % LB, :])):
                        pe.wait_ge((hi_rdy, lo_rdy)[part], i * SPLIT + (u + 1 + part * SPLIT))
                        for k in range(2):
                            for n in range(2):
                                last = mm(bank(b0 + n), lhs[:, k0 + k, :, :].rearrange("p a s -> p (a s)"),
                                          w[:, (2 * k + n) * 512:(2 * k + n + 1) * 512],
                                          start=(first and part == 0 and k == 0),
                                          stop=(u % GU_UNITS == GU_UNITS - 1 and part == 1 and k == 1))
                    last.then_inc(used, 1)

                def unit_f32(u):
                    pe.wait_ge(raw[u], i * 16 + (raw_base[u] + 16))
                    for k in range(2):
                        for n in range(2):
                            last = mm(bank(6 + n), sgz[:, 2 * (u - SPLIT) + k, :, :].rearrange("p a s -> p (a s)"),
                                      slot(u)[:, (2 * k + n) * 512:(2 * k + n + 1) * 512],
                                      start=False, stop=(u == NU - 1 and k == 1))
                    last.then_inc(used, 1)

                pe.wait_ge(m["xg"], i + 1)
                pe.wait_ge(m["y0"], i + 1)
                for u in range(4):
                    unit(u, 0, xg, u == 0)
                unit(4, 2, xg, True)
                unit(5, 2, xg, False)
                pe.wait_ge(m["gua_cp"], i + 1)
                pe.wait_ge(m["gt_cp"], i + 1)
                turn_gu(gu_a, "ta")
                unit(6, 2, xg, False)
                unit(7, 2, xg, False)
                pe.wait_ge(m["p"], i + 2)
                gather()
                pe.wait_ge(m["out_cp"], i + 1)
                combine()
                pe.wait_ge(m["bias_a"], i + 1)
                pe.wait_ge(m["gub_cp"], i + 1)
                turn_gu(gu_b, "tb")
                pe.wait_ge(m["al_a"], i + 1)
                pe.wait_ge(m["y1"], i + 1)
                unit(8, 6, at, True)
                unit(9, 6, at, False)
                pe.wait_ge(m["bias_b"], i + 1)
                pe.wait_ge(m["pg"], i + 1)
                turn_gates()
                pe.wait_ge(m["a_b"], i + 1)
                unit_f32(10)
                unit_f32(11)
            pe.wait_ge(m["gt_cp"], turns + 1)
            pe.wait_ge(m["y0"], turns + 1)
            pe.wait_ge(m["out_cp"], turns + 1)
            combine()

        @block.vector
        def _(dve):
            own = [0]
            V = nc.vector

            def link(ins):
                own[0] += 1
                ins.then_inc(dve_c, 1)
                dve.wait_ge(dve_c, own[0])

            def mean_to_rsqrt(dst, src, n, done, sqrt_sem):
                V.tensor_scalar(dst, src, 1.0 / n, EPS, ALU.mult, ALU.add).then_inc(sig[done], 1)
                dve.wait_ge(sig[sqrt_sem], 1)
                link(V.reciprocal(dst, dst))

            V.memset(sums[:, 0:1], 0.0).then_inc(used, NU)
            V.memset(sums[:, 1:2], 0.0).then_inc(lo_rdy, SPLIT)
            V.memset(sums[:, 2:3], 0.0).then_inc(m["y0"], 1)
            V.memset(mod[:, :, :], 0.0).then_inc(sig["acc0"], 1)
            dve.wait_ge(sig["csil"], 1)
            link(V.tensor_tensor(csil, csil, crow, ALU.mult))
            V.tensor_copy(crep, csil.unsqueeze(2).to_broadcast([P, KC, P])).then_inc(sig["crep"], 1)
            dve.wait_ge(sig["lbT"], 1)
            V.tensor_copy(lbt, ps[:, 2048:2048 + 12]).then_inc(sig["lb_read"], 1)
            dve.wait_ge(sig["lb_read"], 1)
            link(V.tensor_tensor(omlb, lbt[:, 0:6], lbt[:, 6:12], ALU.max))
            V.tensor_tensor(lbt.rearrange("p (l h) -> p l h", l=2), lbt.rearrange("p (l h) -> p l h", l=2),
                            omlb.unsqueeze(1).to_broadcast([P, 2, HEADS]), ALU.subtract).then_inc(sig["lbT"], 1)
            dve.wait_ge(sig["masks_iota"], 1)
            it = tmp[:, 0:2 * P].bitcast(I32)
            link(V.tensor_tensor(tmp[:, 2 * P:3 * P].bitcast(I32), it[:, 0:P], it[:, P:2 * P], ALU.bitwise_xor))
            link(V.tensor_copy(tmp2[:, 3 * P:4 * P], tmp[:, 2 * P:3 * P].bitcast(I32)))
            link(V.tensor_copy(tmp2[:, 2 * P:3 * P], it[:, 0:P]))
            link(V.tensor_copy(tmp[:, 3 * P:4 * P], it[:, P:2 * P]))
            link(V.tensor_tensor(tmp[:, 0:P], tmp[:, 3 * P:4 * P], tmp2[:, 2 * P:3 * P], ALU.is_ge))
            link(V.scalar_tensor_tensor(out=tmp[:, P:2 * P], in0=tmp2[:, 3 * P:4 * P], scalar=1.0,
                                        in1=tmp[:, 0:P], op0=ALU.add, op1=ALU.mult))
            for lv in range(8):
                lo = 0 if lv == 0 else 1 << (lv - 1)
                up = 1 if lv == 0 else 1 << lv
                link(V.tensor_scalar(tmp[:, 0:P], tmp[:, P:2 * P], float(up) + 0.5, None, ALU.is_lt))
                link(V.scalar_tensor_tensor(out=masks[:, lv, :], in0=tmp[:, P:2 * P], scalar=float(lo) + 0.5,
                                            in1=tmp[:, 0:P], op0=ALU.is_gt, op1=ALU.mult))
            dve.wait_ge(sig["lb_done"], 1)
            link(V.tensor_tensor(omlb, lbt[:, 0:6], lbt[:, 6:12], ALU.add))
            link(V.reciprocal(omlb, omlb))
            link(V.tensor_tensor(lbt[:, 0:6], lbt[:, 0:6], omlb, ALU.mult))
            V.tensor_scalar(omlb, lbt[:, 0:6], -1.0, 1.0, ALU.mult, ALU.add)
            dve.wait_ge(sig["bguT"], 1)
            V.tensor_copy(bgu[:, :, :].rearrange("p e c -> p (e c)"), bank(5)).then_inc(sig["bgu_read"], 1)
            dve.wait_ge(ld["pos"], 16)
            dve.wait_ge(sig["consts"], 2)
            link(V.tensor_copy(post, posi[:, :]))
            ang = csn[:, 16:32].rearrange("p (t j) -> p t j", t=TT)
            turn = csn[:, 0:16].rearrange("p (t j) -> p t j", t=TT)
            link(V.tensor_tensor(ang, post.unsqueeze(2).to_broadcast([P, TT, HALF]),
                                 invf.unsqueeze(1).to_broadcast([P, TT, HALF]), ALU.mult))
            magic = 12582912.0
            link(V.tensor_scalar(turn, ang, 1.0 / (2 * math.pi), magic, ALU.mult, ALU.add))
            link(V.tensor_scalar(turn, turn, -magic, None, ALU.add))
            c1 = 6.28125
            c2 = float(np.float32(np.floor((2 * math.pi - c1) * 2 ** 19) / 2 ** 19))
            c3 = 2 * math.pi - c1 - c2
            for cc in (c1, c2, c3):
                link(V.scalar_tensor_tensor(out=csn[:, 16:32], in0=csn[:, 0:16], scalar=-cc, in1=csn[:, 16:32],
                                            op0=ALU.mult, op1=ALU.add))
            V.tensor_scalar(ang, ang, 3.1415925, -3.1415925, ALU.min, ALU.max).then_inc(sig["sin_arg"], 1)
            dve.wait_ge(sig["ssq"], TT)
            mean_to_rsqrt(rstd, ssq, D, "rsq", "rstd")
            dve.wait_ge(sig["sins"], 1)
            link(V.tensor_tensor(csn[:, 0:16], csn[:, 32:48], csn[:, 32:48], ALU.mult))
            link(V.tensor_scalar(csn[:, 0:16], csn[:, 0:16], -2.0, 1.0, ALU.mult, ALU.add))
            dve.wait_ge(ada_pe, KC)
            dve.wait_ge(ld["g1"], 16)
            for n in range(2):
                link(V.scalar_tensor_tensor(out=a1[:, n * 512:(n + 1) * 512], in0=bank(2 + n), scalar=1.0,
                                            in1=g1row[:, n * 512:(n + 1) * 512], op0=ALU.add, op1=ALU.mult))
            link(V.tensor_copy(b1, bank(0, 2)))
            for t in range(TT):
                link(V.scalar_tensor_tensor(out=hb[:, t, :], in0=xs[:, t, :], scalar=rstd[:, t:t + 1], in1=a1,
                                            op0=ALU.mult, op1=ALU.mult))
                V.tensor_tensor(hb[:, t, :], hb[:, t, :], b1, ALU.add).then_inc(sig["h1"], 1)

            def half_copy(name):
                dve.wait_ge(sig[name], 1)
                V.tensor_copy(ht[:, KC // 2:KC, :].rearrange("p k t -> p (k t)"), bank(6, 2)).then_inc(sig[name + "_dve"], 1)

            half_copy("h1T")
            dve.wait_ge(ld["ada2_bias"], 16)

            def accumulate(j):
                landed(dve, ("ada2", j))
                a = mod[:, 2 * (j // KC):2 * (j // KC) + 2, :].rearrange("p a d -> p (a d)")
                V.scalar_tensor_tensor(out=a, in0=slot(place[("ada2", j)] % PRE), scalar=csil[:, j % KC:j % KC + 1],
                                       in1=a, op0=ALU.mult, op1=ALU.add).then_inc(ada_dve, 1)
                dve.wait_ge(ada_dve, j + 1)

            def group(j):
                b = 6 + j % 2
                if j < 3:
                    dve.wait_ge(win_sig, j + 1)
                    for h in (2 * j, 2 * j + 1):
                        link(V.tensor_scalar(fg[:, h, :], fg[:, h, :], omlb[:, h:h + 1], lbt[:, h:h + 1],
                                             ALU.mult, ALU.add))
                    V.tensor_scalar(kd[:, 2 * j:2 * j + 2, :], fg[:, 2 * j:2 * j + 2, :], -1.0, 1.0,
                                    ALU.mult, ALU.add).then_inc(hk_ready, 1)
                elif j < 6:
                    dve.wait_ge(win_sig, j + 1)
                    q = qd[:, 2 * (j - 3):2 * (j - 3) + 2, :].rearrange("p h t -> p (h t)")
                    V.scalar_tensor_tensor(out=q, in0=bank(b), scalar=float(P) ** -0.5, in1=q,
                                           op0=ALU.mult, op1=ALU.mult).then_inc(hq_ready, 1)
                elif j >= 12:
                    dve.wait_ge(win_sig, j - 12 + 7)
                    g = hgate[:, :, (j - 12) * CG:(j - 11) * CG]
                    V.tensor_tensor(g, g, bank(b).rearrange("p (t n) -> p t n", t=TT), ALU.mult).then_inc(sig["hg_read"], 1)
                    dve.wait_ge(sig["hg_read"], j - 11)
                    gg = g.rearrange("p t (h n) -> p t h n", h=2)
                    for t in range(TT):
                        link(V.tensor_tensor(gg[:, t], gg[:, t], hgrow.unsqueeze(1).to_broadcast([P, 2, P]), ALU.mult))

            def update(lv):
                if lv == 1:
                    for g in range(2):
                        dve.wait_ge(lev_done[g], 1)
                        V.tensor_tensor(qd[:, 3 * g:3 * g + 3, :], qd[:, 3 * g:3 * g + 3, :], fg[:, 3 * g:3 * g + 3, :],
                                        ALU.mult).then_inc(q_upd[g], 1)
                    return
                n = 1 << (lv - 2)
                d = block_decay(n)
                if n > 1:
                    dve.wait_ge(tot_upd, lv - 2)
                if lv < 8:
                    V.tensor_tensor(block_decay(2 * n).rearrange("p b r -> p (b r)"), d[:, :, 0], d[:, :, 1],
                                    ALU.mult).then_inc(tot_upd, 1)
                for g in range(2):
                    dve.wait_ge(lev_done[g], lv)
                    dve.wait_ge(q_upd[g], lv - 1)
                    qv = qd[:, 3 * g:3 * g + 3, :].rearrange("p h (b r n) -> p (h b) r n", r=2, n=n)[:, :, 1, :]
                    left = block_decay(n, g)[:, :, 0]
                    V.tensor_tensor(qv, qv, left.unsqueeze(2).to_broadcast([P, 3 * T // (2 * n), n]),
                                    ALU.mult).then_inc(q_upd[g], 1)

            def merge(lv):
                b0 = 3 * (lv % 2)
                for g in range(2):
                    dve.wait_ge(lev_done[g], lv + 1)
                if lv:
                    dve.wait_ge(sct_done, lv)
                V.copy_predicated(sct.rearrange("p (j n) -> p j n", n=P),
                                  masks[:, lv, :].unsqueeze(1).to_broadcast([P, 12, P]),
                                  bank(b0, 3).rearrange("p (j n) -> p j n", n=P)).then_inc(sct_done, 1)

            def rotate():
                dve.wait_ge(act_evac, 2)
                q8 = aqk.rearrange("p (t h d) -> p t h d", t=TT, h=2 * AH)
                t1, t2 = q8[:, :, :, 0:HALF], q8[:, :, :, HALF:ROT]
                cos = csn[:, 0:16].rearrange("p (t j) -> p t j", t=TT).unsqueeze(2).to_broadcast([P, TT, 2 * AH, HALF])
                sin = csn[:, 16:32].rearrange("p (t j) -> p t j", t=TT).unsqueeze(2).to_broadcast([P, TT, 2 * AH, HALF])
                b = [tmp[:, n * P:(n + 1) * P].rearrange("p (t h j) -> p t h j", t=TT, h=2 * AH) for n in range(4)]
                V.tensor_tensor(b[0], t1, cos, ALU.mult)
                V.tensor_tensor(b[1], t2, sin, ALU.mult)
                V.tensor_tensor(b[2], t2, cos, ALU.mult)
                link(V.tensor_tensor(b[3], t1, sin, ALU.mult))
                V.tensor_tensor(t1, b[0], b[1], ALU.subtract)
                V.tensor_tensor(t2, b[2], b[3], ALU.add).then_inc(sig["rot"], 1)

            def softmax_in():
                dve.wait_ge(sig["sc"], 1)
                sc = bank(0, 3).rearrange("p (b s) -> p b s", b=12)
                scale = float(HD) ** -0.5
                cm = cmask.unsqueeze(1).to_broadcast([P, AH, P])
                V.scalar_tensor_tensor(out=pb[:, 0:4, :], in0=sc[:, 0:4, :], scalar=scale, in1=cm, op0=ALU.mult, op1=ALU.add)
                V.scalar_tensor_tensor(out=pb[:, 5:12:2, :], in0=sc[:, 5:12:2, :], scalar=scale, in1=cm,
                                       op0=ALU.mult, op1=ALU.add)
                V.tensor_scalar(pb[:, 4:12:2, :], sc[:, 4:12:2, :], scale, None, ALU.mult).then_inc(sig["sc_read"], 1)
                dve.wait_ge(sig["sc_read"], 1)
                late = pb[:, 4:12, :].rearrange("p (h s) n -> p h (s n)", h=AH)
                link(V.tensor_reduce(amax[:, 0:4], pb[:, 0:4, :], AX.X, ALU.max))
                link(V.tensor_reduce(amax[:, 4:8], late, AX.X, ALU.max))
                link(V.tensor_tensor(pb[:, 0:4, :], pb[:, 0:4, :], amax[:, 0:4].unsqueeze(2).to_broadcast([P, AH, P]),
                                     ALU.subtract))
                V.tensor_tensor(late, late, amax[:, 4:8].unsqueeze(2).to_broadcast([P, AH, T]),
                                ALU.subtract).then_inc(sig["sc_ready"], 1)

            def softmax_sum():
                dve.wait_ge(sig["expd"], 1)
                late = pb[:, 4:12, :].rearrange("p (h s) n -> p h (s n)", h=AH)
                V.tensor_reduce(asum[:, 0:4], pb[:, 0:4, :], AX.X, ALU.add)
                link(V.tensor_reduce(asum[:, 4:8], late, AX.X, ALU.add))
                link(V.reciprocal(amax, asum))

            oa = pb.rearrange("p b s -> p (b s)")[:, 0:512].rearrange("p (j d) -> p j d", d=HD)
            ob = pb.rearrange("p b s -> p (b s)")[:, 512:1024].rearrange("p (j d) -> p j d", d=HD)

            def attention_norm():
                dve.wait_ge(sig["o_att"], 1)
                V.tensor_tensor(oa, bank(3).rearrange("p (j d) -> p j d", d=HD),
                                amax.unsqueeze(2).to_broadcast([P, 8, HD]), ALU.mult).then_inc(sig["o_att_read"], 1)
                dve.wait_ge(sig["o_att_read"], 1)
                link(V.tensor_tensor(ob, oa, oa, ALU.mult))
                link(V.tensor_reduce(asum, ob, AX.X, ALU.add))
                V.tensor_scalar(asum, asum, 1.0 / HD, EPS, ALU.mult, ALU.add).then_inc(sig["aatt_ms"], 1)

            def attention_cat():
                dve.wait_ge(sig["aatt_sq"], 1)
                link(V.reciprocal(asum, asum))
                link(V.tensor_tensor(oa, oa, asum.unsqueeze(2).to_broadcast([P, 8, HD]), ALU.mult))
                for t in range(TT):
                    V.tensor_tensor(hb[:, t, HW_:D].rearrange("p (h d) -> p h d", h=AH), oa[:, 4 * t:4 * t + 4, :],
                                    agrow.unsqueeze(1).to_broadcast([P, AH, HD]), ALU.mult)

            dve.wait_ge(ld["hg"], 16)
            dve.wait_ge(ld["ag"], 16)
            for j in range(WIN_UNITS):
                accumulate(j)
                group(j)
                if j == 7:
                    rotate()
                    update(1)
                    merge(0)
                if j == 8:
                    update(2)
                    merge(1)
                    update(3)
                    merge(2)
                if j == 9:
                    softmax_in()
                    update(4)
                    merge(3)
                if j == 10:
                    update(5)
                    merge(4)
                if j == 11:
                    update(6)
                    merge(5)
                    softmax_sum()
                if j == 12:
                    attention_norm()
                    update(7)
                    merge(6)
                if j == 13:
                    update(8)
                    merge(7)
            attention_cat()
            accumulate(WIN_UNITS)
            dve.wait_ge(sig["oh_sq"], 1)
            link(V.tensor_reduce(rs2, fg.rearrange("p h (t n) -> p (h t) n", t=TT), AX.X, ALU.add))
            V.tensor_scalar(rs2, rs2, 1.0 / P, EPS, ALU.mult, ALU.add).then_inc(sig["oh_ms"], 1)
            dve.wait_ge(sig["oh_rs"], 1)
            link(V.reciprocal(rs2, rs2))
            tt3 = tot.rearrange("p (j n) -> p j n", n=P)
            link(V.tensor_tensor(tt3, bank(3, 3).rearrange("p (j n) -> p j n", n=P),
                                 rs2.unsqueeze(2).to_broadcast([P, 12, P]), ALU.mult))
            tt4 = tot.rearrange("p (h t n) -> p h t n", h=HEADS, t=TT)
            for t in range(TT):
                V.tensor_tensor(hb[:, t, 0:HW_].rearrange("p (h n) -> p h n", h=HEADS), tt4[:, :, t, :],
                                hgate[:, t, :].rearrange("p (h n) -> p h n", h=HEADS), ALU.mult).then_inc(sig["hg_cat"], 1)
            half_copy("oT")
            dve.wait_ge(sig["mod_copied"], 8)
            if not debug:
                dve.wait_ge(ld["g2"], 16)
                link(V.scalar_tensor_tensor(out=mod[:, 2, :], in0=mod[:, 2, :], scalar=1.0, in1=yacc[:, 0, :],
                                            op0=ALU.add, op1=ALU.mult))
            for j in range(D // CG):
                dve.wait_ge(wout_pe, j + 1)
                mv = tmp[:, :].rearrange("p (t n) -> p t n", t=TT)
                link(V.tensor_tensor(mv, bank(j).rearrange("p (t n) -> p t n", t=TT),
                                     mod[:, 0, j * CG:(j + 1) * CG].unsqueeze(1).to_broadcast([P, TT, CG]), ALU.mult))
                xv = xs[:, :, j * CG:(j + 1) * CG]
                V.tensor_tensor(xv, xv, mv, ALU.add).then_inc(sig["x1"], 1)
                dve.wait_ge(sig["x1"], j + 1)
            if debug:
                return
            dve.wait_ge(sig["ssq2"], TT)
            mean_to_rsqrt(rstd, ssq, D, "rms2", "rs2")
            for t in range(TT):
                link(V.scalar_tensor_tensor(out=hb[:, t, :], in0=xs[:, t, :], scalar=rstd[:, t:t + 1], in1=mod[:, 2, :],
                                            op0=ALU.mult, op1=ALU.mult))
                V.tensor_tensor(hb[:, t, :], hb[:, t, :], mod[:, 1, :], ALU.add).then_inc(sig["h2"], 1)
            half_copy("h2T")
            dve.wait_ge(sig["logits"], 1)
            dve.wait_ge(ld["br"], 16)
            lg = tmp[:, 0:TT * NE].rearrange("p (t e) -> p t e", t=TT)
            link(V.tensor_tensor(lg, ps[:, 0:TT * NE].rearrange("p (t e) -> p t e", t=TT),
                                 br[:, :].unsqueeze(1).to_broadcast([P, TT, NE]), ALU.add))
            eq = tmp[:, 128:128 + NE]
            for t in range(TT):
                link(V.max(v8, lg[:, t, :]))
                link(V.max_index(ismall[:, :], v8, lg[:, t, :]))
                link(V.tensor_copy(idf, ismall[:, :]))
                V.tensor_scalar(e4, v8[:, 0:TOPK], v8[:, 0:1], None, ALU.subtract).then_inc(sig["v8"], 1)
                dve.wait_ge(sig["e4"], t + 1)
                link(V.tensor_reduce(esum, e4, AX.X, ALU.add))
                link(V.reciprocal(esum, esum))
                link(V.tensor_scalar(e4, e4, esum, None, ALU.mult))
                link(V.tensor_scalar(msk[:, t, :], iota_e[:, :], idf[:, 0:1], None, ALU.is_equal))
                link(V.tensor_scalar(gate[:, t, :], iota_e[:, :], idf[:, 0:1], e4[:, 0:1], ALU.is_equal, ALU.mult))
                for k in range(1, TOPK):
                    link(V.tensor_scalar(eq, iota_e[:, :], idf[:, k:k + 1], None, ALU.is_equal))
                    link(V.tensor_tensor(msk[:, t, :], msk[:, t, :], eq, ALU.add))
                    link(V.scalar_tensor_tensor(out=gate[:, t, :], in0=eq, scalar=e4[:, k:k + 1], in1=gate[:, t, :],
                                                op0=ALU.mult, op1=ALU.add))
            V.tensor_copy(cnt[:, 0:1], e4[:, 0:1]).then_inc(sig["routed"], 1)
            dve.wait_ge(sig["cum"], 1)
            cum = ps[:, 512:512 + 2 * NE].rearrange("p (t e) -> p t e", t=TT)
            pos = tmp[:, 192:192 + TT * NE].rearrange("p (t e) -> p t e", t=TT)
            link(V.tensor_tensor(pos, cum, msk[:, :, :], ALU.mult))
            link(V.tensor_reduce(cnt[:, 0:1], ps[:, 512 + 2 * NE:512 + 3 * NE], AX.X, ALU.max))
            for p_ in range(PASSES):
                last = V.tensor_scalar(posx[:, :, p_ * NE:(p_ + 1) * NE], pos, -1.0 - CAP * p_, None, ALU.add)
            link(last)
            link(V.tensor_scalar(cnt[:, 1:2], cnt[:, 0:1], CAP + 0.5, float(NE), ALU.is_gt, ALU.mult))
            link(V.tensor_scalar(cnt[:, 2:3], cnt[:, 0:1], 2 * CAP + 0.5, float(NE), ALU.is_gt, ALU.mult))
            link(V.tensor_scalar(cnt[:, 3:4], cnt[:, 0:1], 3 * CAP + 0.5, float(NE), ALU.is_gt, ALU.mult))
            link(V.tensor_reduce(cnt[:, 0:1], cnt[:, 1:4], AX.X, ALU.add))
            V.tensor_scalar(count_i[:, :], cnt[:, 0:1], float(NE), None, ALU.add).then_inc(sig["npass"], 1)
            dve.wait_ge(sig["yinit"], 1)
            V.tensor_copy(yacc[:, 0, :], bank(3, 2))
            V.tensor_copy(yacc[:, 1, :], bank(6, 2)).then_inc(sig["yinit_copied"], 1)

            def one_hot(i):
                col = posx[:, :, i:i + 1] if isinstance(i, int) else posx[:, :, bass.ds(i, 1)]
                V.tensor_tensor(pe_[:, :, :], iota_s[:, :, :], col.to_broadcast([P, TT, CAP]),
                                ALU.is_equal).then_inc(m["p"], 1)

            one_hot(0)
            dve.wait_ge(m["xg_hi"], 1)
            g5 = bank(5).rearrange("p (k s) -> p k s", k=KC)
            V.tensor_tensor(xg[:, :, 1, :], g5, xg[:, :, 0, :].bitcast(F32), ALU.subtract).then_inc(m["xg"], 1)
            dve.wait_ge(sig["npass"], 1)
            turns = dve.value_load(count_i[0:1, 0:1], min_val=NE, max_val=NE * PASSES)
            with dve.Fori(0, turns) as i:
                e = dve.snap(i & (NE - 1))

                def lo(u):
                    dve.wait_ge(hi_rdy, i * SPLIT + (u + 1))
                    dve.wait_ge(used, i * NU + buffer_user(u, LB))
                    V.tensor_tensor(wlo[:, u % LB, :], slot(u), whi[:, u % HB, :].bitcast(F32),
                                    ALU.subtract).then_inc(lo_rdy, 1)

                def half_in(s, h):
                    dve.wait_ge(m["t" + s], i + 1)
                    bias = bgu[:, bass.ds(e, 1), :].rearrange("p a (g c) -> p (a g) c", g=2)[:, :, 4 * h:4 * h + 4]
                    V.tensor_tensor(guT[:, :, :].rearrange("p (g c) s -> p g c s", g=2),
                                    bank(4).rearrange("p (g c s) -> p g c s", g=2, c=4),
                                    bias.unsqueeze(3).to_broadcast([P, 2, 4, CAP]), ALU.add).then_inc(m["bias_" + s], 1)
                    dve.wait_ge(m["bias_" + s], i + 1)
                    V.tensor_scalar(guT[:, 0:4, :], guT[:, 0:4, :], LIMIT, None, ALU.min).then_inc(m["g_" + s], 1)
                    V.tensor_scalar(guT[:, 4:8, :], guT[:, 4:8, :], LIMIT, -LIMIT, ALU.min, ALU.max).then_inc(m["u_" + s], 1)

                def half_act(s, h):
                    dve.wait_ge(m["u_" + s], i + 1)
                    V.scalar_tensor_tensor(out=guT[:, 4:8, :], in0=guT[:, 4:8, :], scalar=1.0, in1=guT[:, 0:4, :],
                                           op0=ALU.add, op1=ALU.mult).then_inc(m["t"], 1)
                    dve.wait_ge(m["t"], i * 2 + (h + 1))
                    dve.wait_ge(m["sig_" + s], i + 1)
                    V.tensor_tensor(sg, sg, guT[:, 4:8, :], ALU.mult).then_inc(m["a_" + s], 1)

                for u in range(2):
                    lo(u)
                dve.wait_ge(m["pg"], i + 1)
                one_hot(dve.snap(i + 1))
                for u in range(2, 8):
                    lo(u)
                half_in("a", 0)
                half_act("a", 0)
                lo(8)
                dve.wait_ge(m["ah_a"], i + 1)
                V.tensor_tensor(at[:, :, 1, :], sg, at[:, :, 0, :].bitcast(F32),
                                ALU.subtract).then_inc(m["al_a"], 1)
                lo(9)
                dve.wait_ge(m["cb1"], i + 1)
                V.tensor_tensor(yacc[:, 1, :], yacc[:, 1, :], bank(6, 2), ALU.add).then_inc(m["y1"], 1)
                dve.wait_ge(m["xg_hi"], i + 2)
                V.tensor_tensor(xg[:, :, 1, :], g5, xg[:, :, 0, :].bitcast(F32), ALU.subtract).then_inc(m["xg"], 1)
                half_in("b", 1)
                half_act("b", 1)
                dve.wait_ge(m["cb0"], i + 1)
                V.tensor_tensor(yacc[:, 0, :], yacc[:, 0, :], bank(0, 2), ALU.add).then_inc(m["y0"], 1)
            for t in range(TT):
                dve.wait_ge(m["cb%d" % t], turns + 1)
                link(V.tensor_tensor(yacc[:, t, :], yacc[:, t, :], bank((0, 6)[t], 2), ALU.add))
                link(V.tensor_tensor(yacc[:, t, :], yacc[:, t, :], gate2, ALU.mult))
                V.tensor_tensor(xs[:, t, :], xs[:, t, :], yacc[:, t, :], ALU.add).then_inc(sig["ofin"], 1)
            dve.wait_ge(sig["out_ssq"], TT)
            mean_to_rsqrt(rstd, ssq, D, "out_rms", "out_rs")
            dve.wait_ge(ld["gfin"], 16)
            for t in range(TT):
                last = V.scalar_tensor_tensor(out=xs[:, t, :], in0=xs[:, t, :], scalar=rstd[:, t:t + 1], in1=gfin,
                                              op0=ALU.mult, op1=ALU.mult)
            last.then_inc(sig["fin"], 1)


_INS = ["x", "c", "positions", "w_ada", "b_ada", "norm1_g", "w_in", "hgrn_lb_logits", "hgrn_norm_g", "attn_norm_g",
        "w_out", "norm2_g", "w_router", "b_router", "w_gate_up", "b_gate_up", "w_down", "b_down", "final_norm_g"]
DEBUG = False


def kernel(**inputs):
    import concourse.bacc as _bacc
    from concourse.bass_utils import run_bass_kernel_spmd as _run

    nc = _bacc.Bacc("TRN2", target_bir_lowering=False, num_devices=1)
    arrays, args = {}, []
    for name in _INS:
        a = np.ascontiguousarray(inputs[name])
        arrays[f"in_{name}_dram"] = a
        args.append(nc.dram_tensor(f"in_{name}_dram", a.shape, mybir.dt.from_np(a.dtype), kind="ExternalInput").ap())
    args.append(nc.dram_tensor("out_dram", (1, T, D), F32, kind="ExternalOutput").ap())
    decoder_block(nc, *args, debug=DEBUG)
    r = _run(nc, [arrays], core_ids=[0])
    return r.results[0]["out_dram"]
```

```python
import math
from contextlib import ExitStack

import numpy as np
import concourse.bass as bass
from concourse import mybir

F32 = mybir.dt.float32
F32R = mybir.dt.float32r
I32 = mybir.dt.int32
U32 = mybir.dt.uint32
U8 = mybir.dt.uint8
ALU = mybir.AluOpType
ACT = mybir.ActivationFunctionType
AX = mybir.AxisListType

P = 128
D = 1024
T = 256
TT = T // P
KC = D // P
HEADS = 6
HW_ = HEADS * P
AH = 4
HD = 64
AW = AH * HD
ROT = HD // 4
HALF = ROT // 2
THETA = 500000.0
NE = 32
TOPK = 4
FF = D
CAP = 64
PASSES = T // CAP
EPS = 1e-6
ALPHA = 1.702
LIMIT = 7.0

U = 2048
SLOTS = 12
PRE = 4
GU_UNITS = 4
NU = 12
F32_UNIT = 10
SPLIT = [u for u in range(NU) if u != F32_UNIT]
BUFS = 3
BUF = {u: u % BUFS for u in SPLIT}
SG = {"a": slice(0, 4), "b": slice(2, 4)}
AT = {"a": slice(0, 4), "b": slice(4, 6)}
WIN_UNITS = 15
CG = 256
NEG = -1e30


def stream_plan():
    plan = [("ada1", k) for k in range(KC)]
    for j in range(WIN_UNITS):
        plan += [("win", j), ("ada2", j)]
    plan.append(("ada2", WIN_UNITS))
    plan += [("wout", j) for j in range(D // CG)]
    return plan


def decoder_block(nc, x, c, positions, w_ada, b_ada, norm1_g, w_in, lb_logits, hgrn_g, attn_g,
                  w_out, norm2_g, w_router, b_router, w_gate_up, b_gate_up, w_down, b_down,
                  final_g, out, debug=False):
    plan = stream_plan()
    place = {key: n for n, key in enumerate(plan)}

    win_col = [HW_ + CG * j for j in range(3)] + [CG * j for j in range(3)] \
        + [4 * HW_, 4 * HW_ + AW, 4 * HW_ + 2 * AW] \
        + [2 * HW_ + CG * j for j in range(3)] + [3 * HW_ + CG * j for j in range(3)]

    with ExitStack() as ctx:
        def sb(name, shape, dt=F32):
            return ctx.enter_context(nc.sbuf_tensor(name, shape, dt))

        def sem(name):
            return ctx.enter_context(nc.semaphore(name))

        ps = ctx.enter_context(nc.psum_tensor("ps", [P, 8 * 512], F32))

        def bank(b, n=1):
            return ps[:, b * 512:(b + n) * 512]

        ring = sb("ring", [P, SLOTS * U])
        whi = sb("whi", [P, BUFS, U], F32R)
        with nc.sbuf_tensor("ht", [P, KC, T], F32) as ht:
            pass
        wlo = sb("wlo", [P, BUFS, U], F32R)
        xg = sb("xg", [P, KC, 2, CAP], F32R)
        at = sb("at", [P, 6, 2, CAP], F32R)
        xs = sb("xs", [P, TT, D])
        hb = sb("hb", [P, TT, D])
        mod = sb("mod", [P, 4, D])
        yacc = sb("yacc", [P, TT, D])

        def slot(s):
            return ring[:, s * U:(s + 1) * U]

        arena_at = [PRE * U]

        def arena(n):
            a = arena_at[0]
            arena_at[0] += n
            assert arena_at[0] <= SLOTS * U
            return ring[:, a:a + n]

        fg = arena(HEADS * T).rearrange("p (h t) -> p h t", h=HEADS)
        qd = arena(HEADS * T).rearrange("p (h t) -> p h t", h=HEADS)
        kd = arena(HEADS * T).rearrange("p (h t) -> p h t", h=HEADS)
        tot = arena(HEADS * T)
        sct = arena(HEADS * T)
        cross = arena(HEADS * P)
        aqk = arena(TT * 2 * AW)
        av = arena(TT * AW).rearrange("p (t n) -> p t n", t=TT)
        qkt = arena(4 * T).rearrange("p (c t) -> p c t", c=4)
        pb = arena(12 * P).rearrange("p (b s) -> p b s", b=12)
        pt = arena(12 * P).rearrange("p (b s) -> p b s", b=12)
        hgate = arena(TT * HW_).rearrange("p (t n) -> p t n", t=TT)
        masks = arena(8 * P // 4).bitcast(U8).rearrange("p (l t) -> p l t", l=8)
        cmask = arena(P)
        bsrc = pt.rearrange("p b s -> p (b s)")[:, 0:4 * P]
        hgrow = arena(P)
        agrow = arena(HD)
        lbt = arena(HEADS * 2)
        omlb = arena(HEADS)
        assert arena_at[0] <= SLOTS * U

        tmp = sb("tmp", [P, 512])
        tmp2 = sb("tmp2", [P, 512])
        guT = sb("guT", [P, 8, CAP])
        sgz = sb("sgz", [P, 4, 2, CAP])
        pe_ = sb("pe_", [P, TT, CAP])
        gts = sb("gts", [P, T])
        bgu = sb("bgu", [P, NE, 16])
        posx = sb("posx", [P, TT, PASSES * NE + 1])
        gate = sb("gate", [P, TT, NE])
        msk = sb("msk", [P, TT, NE])
        br = sb("br", [P, NE])
        ident = sb("ident", [P, P])
        twin = sb("twin", [P, CAP])
        ones = sb("ones", [P, P])
        tri = sb("tri", [P, P])
        iota_s = sb("iota_s", [P, TT, CAP])
        iota_e = sb("iota_e", [P, NE])
        small = sb("small", [P, 160])
        ismall = sb("ismall", [P, 16], U32)
        count_i = sb("count_i", [P, 1], I32)
        sg = sgz[:, :, 0, :]
        wr = guT[:, 0:KC * NE // CAP, :].rearrange("p c s -> p (c s)").rearrange("p (k e) -> p k e", k=KC)
        pg = tmp[:, 0:TT * 2 * CAP].rearrange("p (t a s) -> p t a s", t=TT, a=2)
        crow = small[:, 0:8]
        csil = small[:, 8:16]
        ssq = small[:, 16:18]
        rstd = small[:, 18:20]
        post = small[:, 20:22]
        sums = small[:, 24:36]
        rs2 = small[:, 36:48]
        amax = small[:, 48:56]
        asum = small[:, 56:64]
        v8 = small[:, 64:80].rearrange("p (t k) -> p t k", t=TT)
        e4 = small[:, 40:48].rearrange("p (t k) -> p t k", t=TT)
        idf = small[:, 24:40].rearrange("p (t k) -> p t k", t=TT)
        esum = small[:, 84:86]
        cnt = small[:, 86:90]
        invf = small[:, 92:100]
        csn = small[:, 100:148]
        posi = sb("posi", [P, TT], I32)
        gate_pad = tmp[:, 0:TT * P].rearrange("p (t n) -> p t n", t=TT)
        a1 = yacc[:, 0, :]
        b1 = yacc[:, 1, :]
        vh = yacc[:, :, :].rearrange("p t d -> p (t d)")[:, 0:TT * HW_].rearrange("p (t n) -> p t n", t=TT)
        crep = ht[:, :, 0:P]
        g1row = hb[:, 0, :]
        gu_a = mod[:, 0, :]
        gu_b = mod[:, 1, :]
        outs = mod[:, 2, :]
        gate2 = mod[:, 3, :]
        gfin = hb[:, 1, :]

        ld = {n: sem("ld_" + n) for n in
              "x c pos g1 ada1_bias ada2_bias lb bgu hg ag wr br g2 bdown gfin".split()}
        raw = [sem(f"raw{s}") for s in range(SLOTS)]
        sig = {n: sem("s_" + n) for n in
               """ident consts masks_iota csil crep lbT lb_read lb_done bguT bgu_read ssq rsq rstd
               h1 h1T h1T_act h1T_dve sin_arg sins rot aT aT_copied sc_even sc sc_read sc_ready expd pT pT_copied
               o_att o_att_read aatt_ms aatt_sq cross cross_copied oh oh_sq oh_ms oh_rs oh_read hg_read hg_cat
               oT oT_act oT_dve ada2 mod_copied g2_read acc0 x1 ssq2 rms2 rs2 h2 h2T h2T_act h2T_dve logits v8 e4 gates
               routed cum bd y_zero npass out_rms out_ssq out_rs fin stored ofin""".split()}
        win_sig = sem("win_sig")
        act_evac = sem("act_evac")
        ada_pe = sem("ada_pe")
        win_pe = sem("win_pe")
        wout_pe = sem("wout_pe")
        ada_dve = sem("ada_dve")
        lev_done = [sem(f"lev_done{g}") for g in range(2)]
        q_upd = [sem(f"q_upd{g}") for g in range(2)]
        k_upd = [sem(f"k_upd{g}") for g in range(2)]
        tot_upd = sem("tot_upd")
        hq_ready = sem("hq_ready")
        hk_ready = sem("hk_ready")
        sct_done = sem("sct_done")
        dve_c = sem("dve_c")
        act_c = sem("act_c")
        pool_c = sem("pool_c")
        hi_rdy = sem("hi_rdy")
        lo_rdy = sem("lo_rdy")
        used = sem("used")
        m = {n: sem("m_" + n) for n in
             """xg_hi xg ga p pg gt gt_cp gua_cp gub_cp ta tb bias_a bias_b g_a g_b sig_a sig_b
             a_a a_b ah_a ah_b al_a al_b cb0 cb1 y0 y1 out_cp u_a u_b t""".split()}

        def buffer_user(u):
            before = [v for v in SPLIT if v < u and BUF[v] == BUF[u]]
            return before[-1] + 1 + NU if before else max(v for v in SPLIT if BUF[v] == BUF[u]) + 1

        block = ctx.enter_context(nc.Block())

        raw_base = [0] * SLOTS
        for n in range(len(plan)):
            raw_base[n % PRE] += 16

        def landed(eng, key):
            n = place[key]
            eng.wait_ge(raw[n % PRE], 16 * (n // PRE + 1))

        def used_by(eng, key):
            kind, j = key
            s = {"ada1": ada_pe, "win": win_pe, "wout": wout_pe, "ada2": ada_dve}[kind]
            eng.wait_ge(s, j + 1)

        ada_v = w_ada.rearrange("l (p k) n -> l p k n", k=KC)
        win_v = w_in.rearrange("l (k p) n -> l p k n", p=P)
        wout_v = w_out.rearrange("l (k p) n -> l p k n", p=P)
        x_v = x.rearrange("b (t p) d -> (b p) t d", p=P)
        out_v = out.rearrange("b (t p) d -> (b p) t d", p=P)

        def unit_src(kind, j):
            if kind == "ada1":
                return ada_v[0, :, j, 0:U]
            if kind == "ada2":
                return ada_v[0, :, j % KC, U * (1 + j // KC):U * (2 + j // KC)]
            if kind == "win":
                return win_v[0, :, :, win_col[j]:win_col[j] + CG]
            return wout_v[0, :, :, CG * j:CG * (j + 1)]

        def model_chunk(k):
            return slice(k // 2 * 2 * P + k % 2, (k // 2 + 1) * 2 * P, 2)

        def expert_load(sp, e, u):
            dst = slot(u)
            if u < 2 * GU_UNITS:
                half, k2 = u // GU_UNITS, u % GU_UNITS
                src = w_gate_up[0, e, k2 * 2 * P:(k2 + 1) * 2 * P, :]
                src = src.rearrange("(p k) (g n) -> p (k g) n", p=P, g=2)[:, :, half * 512:(half + 1) * 512]
                sp.dma_start(dst.rearrange("p (k n) -> p k n", k=4), src).then_inc(raw[u], 16)
            else:
                k2 = u - 2 * GU_UNITS
                src = w_down[0, e, k2 * 2 * P:(k2 + 1) * 2 * P, :].rearrange("(k p) n -> p k n", p=P)
                sp.dma_start(dst.rearrange("p (k n) -> p k n", k=2), src).then_inc(raw[u], 16)

        @block.sync
        def _(sp):
            for n, (kind, j) in enumerate(plan):
                if n >= PRE:
                    used_by(sp, plan[n - PRE])
                src = unit_src(kind, j)
                dst = slot(n % PRE)
                if kind in ("win", "wout"):
                    dst = dst.rearrange("p (k n) -> p k n", k=KC)
                sp.dma_start(dst, src).then_inc(raw[n % PRE], 16)
            if debug:
                sp.wait_ge(sig["x1"], D // CG)
                sp.wait_ge(ld["wr"], 16)
                sp.wait_ge(ld["br"], 16)
                sp.dma_start(out_v, xs[:, :, :]).then_inc(sig["stored"], 16)
                sp.wait_ge(sig["stored"], 16)
                return
            sp.wait_ge(sig["hg_cat"], TT)
            for u in range(PRE, NU):
                expert_load(sp, 0, u)
            sp.wait_ge(wout_pe, D // CG)
            for u in range(PRE):
                expert_load(sp, 0, u)
            sp.wait_ge(sig["npass"], 1)
            turns = sp.value_load(count_i[0:1, 0:1], min_val=NE, max_val=NE * PASSES)
            with sp.Fori(1, turns) as i:
                e = sp.snap(i & (NE - 1))
                done = sp.snap(i >> (NE.bit_length() - 1))
                for u in range(NU):
                    if u in SPLIT:
                        sp.wait_ge(lo_rdy, done * (NE * len(SPLIT)) + e * len(SPLIT) + (SPLIT.index(u) + 1))
                    else:
                        sp.wait_ge(used, done * (NE * NU) + e * NU + (u + 1))
                    expert_load(sp, e, u)
            for n, t in enumerate((1, 0)):
                sp.wait_ge(sig["fin"], n + 1)
                sp.dma_start(out_v[:, t, :], xs[:, t, :]).then_inc(sig["stored"], 16)
            sp.wait_ge(sig["stored"], 16 * TT)

        def block_decay(n, g=None):
            if n == 1:
                v = fg if g is None else fg[:, 3 * g:3 * g + 3, :]
                return v.rearrange("p h (b r) -> p (h b) r", r=2)
            off = 0
            k = 2
            while k < n:
                off += HEADS * T // k
                k *= 2
            w = HEADS * T // n
            v = tot[:, off:off + w]
            if g is not None:
                v = v[:, g * w // 2:(g + 1) * w // 2]
            return v.rearrange("p (b r) -> p b r", r=2)

        @block.gpsimd
        def _(pool):
            own = [0]

            def link(ins):
                own[0] += 1
                ins.then_inc(pool_c, 1)
                pool.wait_ge(pool_c, own[0])

            link(pool.memset(ident[:, :], 0.0))
            pool.affine_select(out=ident[:, :], in_=ident[:, :], compare_op=ALU.not_equal, fill=1.0,
                               base=0, pattern=[[-1, P]], channel_multiplier=1).then_inc(sig["ident"], 1)
            link(pool.memset(twin[:, :], 0.0))
            for off in (0, CAP):
                link(pool.affine_select(out=twin[:, :], in_=twin[:, :], compare_op=ALU.not_equal, fill=1.0,
                                        base=-off, pattern=[[-1, CAP]], channel_multiplier=1))
            pool.memset(ones[:, :], 1.0).then_inc(sig["consts"], 1)
            pool.iota(tmp[:, 0:P].bitcast(I32), pattern=[[0, P]], base=0, channel_multiplier=1)
            pool.iota(tmp[:, P:2 * P].bitcast(I32), pattern=[[1, P]], base=0,
                      channel_multiplier=0).then_inc(sig["masks_iota"], 1)
            link(pool.memset(tri[:, :], 1.0))
            pool.affine_select(out=tri[:, :], in_=tri[:, :], compare_op=ALU.is_ge, fill=0.0,
                               base=0, pattern=[[1, P]], channel_multiplier=-1)
            link(pool.memset(cmask, 0.0))
            pool.affine_select(out=cmask, in_=cmask, compare_op=ALU.is_ge, fill=NEG,
                               base=0, pattern=[[-1, P]], channel_multiplier=1)
            for j in range(HALF):
                v = float(np.exp(np.float32(-math.log(THETA)) * np.float32(2 * j) / np.float32(ROT)))
                pool.memset(invf[:, j:j + 1], v)
            pool.iota(iota_s[:, :, :], pattern=[[0, TT], [1, CAP]], base=0, channel_multiplier=0,
                      allow_small_or_imprecise_dtypes=True)
            pool.iota(iota_e[:, :], pattern=[[1, NE]], base=0, channel_multiplier=0,
                      allow_small_or_imprecise_dtypes=True)
            pool.memset(sgz[:, :, :, :], 0.0)
            pool.memset(posx[:, :, :], -1.0)
            pool.memset(sct, 0.0).then_inc(sig["consts"], 1)

            for lv in range(1, 8):
                n = 1 << (lv - 1)
                for g in range(2):
                    if lv == 1:
                        pool.wait_ge(hk_ready, 3)
                    else:
                        pool.wait_ge(tot_upd, lv - 1)
                    pool.wait_ge(lev_done[g], lv + 1)
                    kv = kd[:, 3 * g:3 * g + 3, :].rearrange("p h (b r n) -> p (h b) r n", r=2, n=n)[:, :, 0, :]
                    right = block_decay(n, g)[:, :, 1]
                    nb = 3 * T // (2 * n)
                    pool.tensor_tensor(kv, kv, right.unsqueeze(2).to_broadcast([P, nb, n]),
                                       ALU.mult).then_inc(k_upd[g], 1)
            if debug:
                return
            pool.wait_ge(sig["g2_read"], 1)
            pool.memset(yacc[:, :, :], 0.0).then_inc(sig["y_zero"], 1)
            pool.wait_ge(sig["npass"], 1)

            turns = pool.value_load(count_i[0:1, 0:1], min_val=NE, max_val=NE * PASSES)
            with pool.Fori(0, turns) as i:
                e = pool.snap(i & (NE - 1))
                pool.wait_ge(m["p"], i + 1)
                pool.wait_ge(m["gt_cp"], i + 1)
                pool.tensor_tensor(pg[:, :, :, :], pe_[:, :, :].unsqueeze(2).to_broadcast([P, TT, 2, CAP]),
                                   gate[:, :, bass.ds(e, 1)].unsqueeze(3).to_broadcast([P, TT, 2, CAP]),
                                   ALU.mult).then_inc(m["pg"], 1)

        @block.scalar
        def _(act):
            own = [0]

            def link(ins):
                own[0] += 1
                ins.then_inc(act_c, 1)
                act.wait_ge(act_c, own[0])

            A = nc.scalar.activation
            act.dma_start(small[:, 0:8], c.rearrange("b (p k) -> (b p) k", p=P)).then_inc(ld["c"], 16)
            act.dma_start(xs[:, :, :], x_v).then_inc(ld["x"], 16)
            act.dma_start(yacc[0:1, :, :].rearrange("p t d -> p (t d)"), b_ada[0:1, 0:U]).then_inc(ld["ada1_bias"], 16)
            act.dma_start(hb[:, 0, :], norm1_g.to_broadcast([P, D])).then_inc(ld["g1"], 16)
            act.dma_start(tmp2[0:12, 0:P], lb_logits.rearrange("l (h p) -> (l h) p", p=P)).then_inc(ld["lb"], 16)
            act.dma_start(posi[:, :], positions.rearrange("b (t p) -> p (b t)", p=P),
                          allow_slow_non_contiguous=True).then_inc(ld["pos"], 16)
            act.dma_start(bsrc.rearrange("p (a f) -> p a f", a=4),
                          b_gate_up.rearrange("l e (c f) -> (l e c) f", f=P)
                          .rearrange("(a r) f -> r a f", r=P)).then_inc(ld["bgu"], 16)
            act.dma_start(hgrow, hgrn_g.to_broadcast([P, P])).then_inc(ld["hg"], 16)
            act.dma_start(agrow, attn_g.to_broadcast([P, HD])).then_inc(ld["ag"], 16)
            act.dma_start(br[:, :], b_router.to_broadcast([P, NE])).then_inc(ld["br"], 16)
            act.dma_start(wr[:, :, :], w_router[0].rearrange("(k p) e -> p k e", p=P)).then_inc(ld["wr"], 16)
            act.wait_ge(sig["acc0"], 1)
            act.dma_start(mod[0:1, :, :].rearrange("p a d -> p (a d)"), b_ada[0:1, U:3 * U]).then_inc(ld["ada2_bias"], 16)

            act.wait_ge(ld["c"], 16)
            A(csil, crow, ACT.Sigmoid).then_inc(sig["csil"], 1)
            act.wait_ge(ld["x"], 16)
            for t in range(TT):
                A(slot(PRE + t)[:, 0:D], xs[:, t, :], ACT.Square, accum_out=ssq[:, t:t + 1]).then_inc(sig["ssq"], 1)
            act.wait_ge(sig["lbT"], 2)
            A(lbt, lbt, ACT.Exp).then_inc(sig["lb_done"], 1)
            act.wait_ge(sig["sin_arg"], 1)
            link(A(csn[:, 32:48], csn[:, 16:32], ACT.Sin, scale=0.5))
            A(csn[:, 16:32], csn[:, 16:32], ACT.Sin).then_inc(sig["sins"], 1)
            act.wait_ge(sig["rsq"], 1)
            A(rstd, rstd, ACT.Sqrt).then_inc(sig["rstd"], 1)

            def half_copy(name):
                act.wait_ge(sig[name], 1)
                nc.scalar.copy(ht[:, 0:KC // 2, :].rearrange("p k t -> p (k t)"), bank(4, 2)).then_inc(sig[name + "_act"], 1)

            half_copy("h1T")

            def group(j):
                b = 6 + j % 2
                act.wait_ge(win_pe, j + 1)
                wide = bank(b).rearrange("p (t n) -> p t n", t=TT)
                if j < 3:
                    A(fg[:, 2 * j:2 * j + 2, :].rearrange("p h t -> p (h t)"), bank(b), ACT.Sigmoid).then_inc(win_sig, 1)
                elif j < 6:
                    A(qd[:, 2 * (j - 3):2 * (j - 3) + 2, :].rearrange("p h t -> p (h t)"), bank(b),
                      ACT.Sigmoid).then_inc(win_sig, 1)
                elif j < 8:
                    nc.scalar.copy(aqk.rearrange("p (t n) -> p t n", t=TT)[:, :, (j - 6) * AW:(j - 5) * AW],
                                   wide).then_inc(act_evac, 1)
                elif j == 8:
                    nc.scalar.copy(av, wide).then_inc(act_evac, 1)
                elif j < 12:
                    nc.scalar.copy(vh[:, :, (j - 9) * CG:(j - 8) * CG], wide).then_inc(act_evac, 1)
                else:
                    A(hgate[:, :, (j - 12) * CG:(j - 11) * CG], wide, ACT.Sigmoid).then_inc(win_sig, 1)

            for j in range(WIN_UNITS):
                if j == 9:
                    act.wait_ge(sig["aT"], 1)
                    nc.scalar.copy(qkt.rearrange("p c t -> p (c t)"), bank(3, 2)).then_inc(sig["aT_copied"], 1)
                if j == 11:
                    act.wait_ge(sig["sc_ready"], 1)
                    A(pb.rearrange("p b s -> p (b s)"), pb.rearrange("p b s -> p (b s)"), ACT.Exp).then_inc(sig["expd"], 1)
                if j == 12:
                    act.wait_ge(sig["pT"], 1)
                    nc.scalar.copy(pt.rearrange("p b s -> p (b s)"), bank(3, 3)).then_inc(sig["pT_copied"], 1)
                if j == 14:
                    act.wait_ge(sig["aatt_ms"], 1)
                    A(asum, asum, ACT.Sqrt).then_inc(sig["aatt_sq"], 1)
                group(j)
            act.wait_ge(sig["cross"], 1)
            nc.scalar.copy(cross, ps[:, 0:HEADS * P]).then_inc(sig["cross_copied"], 1)
            act.wait_ge(sig["oh"], 1)
            A(fg.rearrange("p h t -> p (h t)"), bank(3, 3), ACT.Square).then_inc(sig["oh_sq"], 1)
            act.wait_ge(sig["oh_ms"], 1)
            A(rs2, rs2, ACT.Sqrt).then_inc(sig["oh_rs"], 1)
            for j in range(8):
                act.wait_ge(sig["ada2"], j + 1)
                nc.scalar.copy(mod[:, j // 2, (j % 2) * 512:(j % 2 + 1) * 512], bank(6 + j % 2)).then_inc(sig["mod_copied"], 1)
            half_copy("oT")
            if debug:
                return
            act.wait_ge(sig["hg_cat"], TT)
            act.dma_start(yacc[:, 0, :], norm2_g.to_broadcast([P, D])).then_inc(ld["g2"], 16)
            act.wait_ge(sig["x1"], D // CG)
            act.dma_start(mod[0:NE, 0, :], b_down[0]).then_inc(ld["bdown"], 16)
            for t in range(TT):
                A(hb[:, t, :], xs[:, t, :], ACT.Square, accum_out=ssq[:, t:t + 1]).then_inc(sig["ssq2"], 1)
            act.wait_ge(sig["rms2"], 1)
            A(rstd, rstd, ACT.Sqrt).then_inc(sig["rs2"], 1)
            half_copy("h2T")
            act.wait_ge(sig["v8"], 1)
            A(e4, e4, ACT.Exp).then_inc(sig["e4"], 1)

            act.wait_ge(m["ga"], 1)
            nc.scalar.copy(xg[:, :, 0, :], bank(5).rearrange("p (k s) -> p k s", k=KC)).then_inc(m["xg_hi"], 1)
            act.wait_ge(sig["bd"], 1)
            turns = act.value_load(count_i[0:1, 0:1], min_val=NE, max_val=NE * PASSES)
            def hi(i, u):
                act.wait_ge(raw[u], i * 16 + (raw_base[u] + 16))
                act.wait_ge(used, i * NU + buffer_user(u))
                nc.scalar.copy(whi[:, BUF[u], :], slot(u)).then_inc(hi_rdy, 1)

            def silu_part(i, s):
                act.wait_ge(m["g_" + s], i + 1)
                A(sg, guT[:, 0:4, :], ACT.Sigmoid, scale=ALPHA).then_inc(m["sig_" + s], 1)

            def act_hi(i, s):
                act.wait_ge(m["a_" + s], i + 1)
                nc.scalar.copy(at[:, AT[s], 0, :], sg[:, SG[s], :]).then_inc(m["ah_" + s], 1)

            def first_part(i):
                hi(i, 0)
                act.wait_ge(m["gt"], i + 1)
                nc.scalar.copy(gts[:, :], ps[:, 4 * 512:4 * 512 + T]).then_inc(m["gt_cp"], 1)
                hi(i, 1)
                act.wait_ge(used, i * NU + NU)
                nc.scalar.copy(outs, bank(6, 2)).then_inc(m["out_cp"], 1)
                for u in range(2, 6):
                    hi(i, u)
                act.wait_ge(used, i * NU + (NU + GU_UNITS))
                nc.scalar.copy(gu_a, bank(0, 2)).then_inc(m["gua_cp"], 1)
                for u in range(6, 9):
                    hi(i, u)

            def second_part(i):
                silu_part(i, "a")
                act_hi(i, "a")
                hi(i, 9)
                act.wait_ge(used, i * NU + (NU + 2 * GU_UNITS))
                nc.scalar.copy(gu_b, bank(2, 2)).then_inc(m["gub_cp"], 1)
                act.wait_ge(m["ga"], i + 2)
                nc.scalar.copy(xg[:, :, 0, :], bank(5).rearrange("p (k s) -> p k s", k=KC)).then_inc(m["xg_hi"], 1)
                hi(i, 11)
                silu_part(i, "b")
                act_hi(i, "b")

            first_part(0)
            with act.Fori(0, act.snap(turns - 1)) as i:
                second_part(i)
                first_part(act.snap(i + 1))
            second_part(act.snap(turns - 1))
            act.wait_ge(m["gt"], turns + 1)
            nc.scalar.copy(gts[:, :], ps[:, 4 * 512:4 * 512 + T]).then_inc(m["gt_cp"], 1)
            act.wait_ge(used, turns * NU + NU)
            nc.scalar.copy(outs, bank(6, 2)).then_inc(m["out_cp"], 1)
            act.dma_start(gfin, final_g.rearrange("(a d) -> a d", a=1).to_broadcast([P, D])).then_inc(ld["gfin"], 16)
            for n, t in enumerate((1, 0)):
                act.wait_ge(sig["ofin"], n + 1)
                A(hb[:, 0, :], xs[:, t, :], ACT.Square,
                  accum_out=ssq[:, t:t + 1]).then_inc(sig["out_ssq"], 1)
                act.wait_ge(sig["out_rms"], n + 1)
                A(rstd[:, t:t + 1], rstd[:, t:t + 1], ACT.Sqrt).then_inc(sig["out_rs"], 1)

        @block.tensor
        def _(pe):
            mm = nc.tensor.matmul

            def turn_all(src, name, ready):
                for t in range(TT):
                    pe.wait_ge(ready, t + 1)
                    for k in range(KC):
                        last = nc.tensor.transpose(ps[:, 2048 + k * T + t * P:2048 + k * T + (t + 1) * P],
                                                   src[:, t, k * P:(k + 1) * P], ident[:, :])
                last.then_inc(sig[name], 1)

            pe.wait_ge(sig["ident"], 1)
            pe.wait_ge(ld["lb"], 16)
            nc.tensor.transpose(ps[:, 2048:2048 + 12], tmp2[0:12, 0:P], ident[0:12, 0:12]).then_inc(sig["lbT"], 1)
            pe.wait_ge(ld["bgu"], 16)
            for a in range(4):
                last = nc.tensor.transpose(ps[:, 2560 + a * P:2560 + (a + 1) * P], bsrc[:, a * P:(a + 1) * P], ident[:, :])
            last.then_inc(sig["bguT"], 1)
            pe.wait_ge(sig["consts"], 2)
            pe.wait_ge(ld["ada1_bias"], 16)
            for b in range(4):
                mm(bank(b), ones[0:1, :], yacc[0:1, :, :].rearrange("p t d -> p (t d)")[:, b * 512:(b + 1) * 512],
                   start=True, stop=False)
            pe.wait_ge(sig["crep"], 1)
            for k in range(KC):
                landed(pe, ("ada1", k))
                w = slot(place[("ada1", k)] % PRE)
                for b in range(4):
                    last = mm(bank(b), crep[:, k, :], w[:, b * 512:(b + 1) * 512], start=False, stop=(k == KC - 1))
                last.then_inc(ada_pe, 1)

            pe.wait_ge(sig["lb_read"], 1)
            pe.wait_ge(sig["bgu_read"], 1)
            turn_all(hb, "h1T", sig["h1"])
            pe.wait_ge(sig["h1T_act"], 1)
            pe.wait_ge(sig["h1T_dve"], 1)

            def level(lv):
                b0 = 3 * (lv % 2)
                if lv > 1:
                    pe.wait_ge(sct_done, lv - 1)
                for g in range(2):
                    if lv == 0:
                        pe.wait_ge(hq_ready, 3)
                        pe.wait_ge(hk_ready, 3)
                    else:
                        pe.wait_ge(q_upd[g], lv)
                        if lv > 1:
                            pe.wait_ge(k_upd[g], lv - 1)
                    for h in range(3 * g, 3 * g + 3):
                        for t in range(TT):
                            j = h * TT + t
                            last = mm(ps[:, b0 * 512 + j * P:b0 * 512 + (j + 1) * P], kd[:, h, t * P:(t + 1) * P],
                                      qd[:, h, t * P:(t + 1) * P], start=True, stop=True)
                    last.then_inc(lev_done[g], 1)

            def attention_turn():
                pe.wait_ge(sct_done, 2)
                pe.wait_ge(sig["rot"], 1)
                for ch in range(4):
                    for t in range(TT):
                        last = nc.tensor.transpose(ps[:, 3 * 512 + ch * T + t * P:3 * 512 + ch * T + (t + 1) * P],
                                                   aqk[:, t * 2 * AW + ch * P:t * 2 * AW + (ch + 1) * P], ident[:, :])
                last.then_inc(sig["aT"], 1)

            def attention_scores():
                pe.wait_ge(sct_done, 3)
                pe.wait_ge(sig["aT_copied"], 1)
                for n, h in enumerate((0, 2, 1, 3)):
                    if n == 2:
                        pe.wait_ge(sig["sc_even"], 1)
                    r = slice(HD * (h % 2), HD * (h % 2) + HD)
                    q, k = qkt[r, h // 2, :], qkt[r, 2 + h // 2, :]
                    mm(ps[:, h * P:(h + 1) * P], q[:, 0:P], k[:, 0:P], start=True, stop=True)
                    last = mm(ps[:, (4 + 2 * h) * P:(6 + 2 * h) * P], q[:, P:T], k, start=True, stop=True)
                    if n == 1:
                        last.then_inc(sig["sc_even"], 1)
                last.then_inc(sig["sc"], 1)

            def attention_pt():
                pe.wait_ge(sct_done, 6)
                pe.wait_ge(sig["expd"], 1)
                for j in range(12):
                    last = nc.tensor.transpose(ps[:, 3 * 512 + j * P:3 * 512 + (j + 1) * P], pb[:, j, :], ident[:, :])
                last.then_inc(sig["pT"], 1)

            def attention_out():
                pe.wait_ge(sig["pT_copied"], 1)
                for h in range(AH):
                    o = ps[:, 3 * 512 + h * HD:3 * 512 + (h + 1) * HD]
                    mm(o, pt[:, h, :], av[:, 0, h * HD:(h + 1) * HD], start=True, stop=True)
                    o = ps[:, 3 * 512 + AW + h * HD:3 * 512 + AW + (h + 1) * HD]
                    for s in range(TT):
                        last = mm(o, pt[:, 4 + 2 * h + s, :], av[:, s, h * HD:(h + 1) * HD],
                                  start=(s == 0), stop=(s == 1))
                last.then_inc(sig["o_att"], 1)

            for j in range(WIN_UNITS):
                b = 6 + j % 2
                if j >= 2:
                    r = j - 2
                    s, v = (win_sig, r + 1) if r < 3 else (hq_ready, r - 2) if r < 6 else \
                        (act_evac, r - 5) if r < 12 else (sig["hg_read"], r - 11)
                    pe.wait_ge(s, v)
                landed(pe, ("win", j))
                w = slot(place[("win", j)] % PRE).rearrange("p (k n) -> p k n", k=KC)
                for i2 in range(2):
                    o = ps[:, b * 512 + i2 * T:b * 512 + (i2 + 1) * T]
                    for k in range(KC):
                        if j < 6:
                            last = mm(o, w[:, k, i2 * P:(i2 + 1) * P], ht[:, k, :], start=(k == 0), stop=(k == KC - 1))
                        else:
                            last = mm(o, ht[:, k, i2 * P:(i2 + 1) * P], w[:, k, :], start=(k == 0), stop=(k == KC - 1))
                last.then_inc(win_pe, 1)
                if j == 7:
                    level(0)
                if j == 8:
                    level(1)
                    level(2)
                    attention_turn()
                if j == 9:
                    attention_scores()
                    level(3)
                if j == 10:
                    pe.wait_ge(sig["sc_read"], 1)
                    level(4)
                if j == 11:
                    level(5)
                    attention_pt()
                if j == 12:
                    attention_out()
                    level(6)
                if j == 13:
                    pe.wait_ge(sig["o_att_read"], 1)
                    level(7)
            pe.wait_ge(sct_done, 7)
            for g in range(2):
                pe.wait_ge(q_upd[g], 8)
                pe.wait_ge(k_upd[g], 7)
            for h in range(HEADS):
                last = mm(ps[:, h * P:(h + 1) * P], kd[:, h, 0:P], qd[:, h, P:T], start=True, stop=True)
            last.then_inc(sig["cross"], 1)
            pe.wait_ge(sct_done, 8)
            pe.wait_ge(act_evac, 6)
            pe.wait_ge(sig["cross_copied"], 1)
            sc4 = sct.rearrange("p (h t n) -> p h t n", h=HEADS, t=TT)
            for h in range(HEADS):
                for t in range(TT):
                    o = ps[:, 3 * 512 + (2 * h + t) * P:3 * 512 + (2 * h + t + 1) * P]
                    last = mm(o, sc4[:, h, t, :], vh[:, t, h * P:(h + 1) * P], start=True, stop=(t == 0))
                    if t == 1:
                        last = mm(o, cross[:, h * P:(h + 1) * P], vh[:, 0, h * P:(h + 1) * P], start=False, stop=True)
            last.then_inc(sig["oh"], 1)
            for j in range(8):
                b = 6 + j % 2
                if j < 2:
                    pe.wait_ge(sig["hg_read"], 3)
                else:
                    pe.wait_ge(sig["mod_copied"], j - 1)
                pe.wait_ge(ada_dve, KC * (1 + j // 4))
                mm(bank(b), ones[:, :], mod[:, j // 2, (j % 2) * 512:(j % 2 + 1) * 512],
                   start=True, stop=True).then_inc(sig["ada2"], 1)
            pe.wait_ge(sig["mod_copied"], 8)
            turn_all(hb, "oT", sig["hg_cat"])
            pe.wait_ge(sig["oT_act"], 1)
            pe.wait_ge(sig["oT_dve"], 1)
            for j in range(D // CG):
                landed(pe, ("wout", j))
                w = slot(place[("wout", j)] % PRE).rearrange("p (k n) -> p k n", k=KC)
                for t in range(TT):
                    for k in range(KC):
                        last = mm(ps[:, j * 512 + t * CG:j * 512 + (t + 1) * CG], ht[:, k, t * P:(t + 1) * P],
                                  w[:, k, :], start=(k == 0), stop=(k == KC - 1))
                last.then_inc(wout_pe, 1)
            if debug:
                return
            turn_all(hb, "h2T", sig["h2"])
            pe.wait_ge(sig["h2T_act"], 1)
            pe.wait_ge(sig["h2T_dve"], 1)
            pe.wait_ge(ld["wr"], 16)
            for t in range(TT):
                for k in range(KC):
                    last = mm(ps[:, t * NE:(t + 1) * NE], ht[:, k, t * P:(t + 1) * P], wr[:, k, :],
                              start=(k == 0), stop=(k == KC - 1))
            last.then_inc(sig["logits"], 1)
            pe.wait_ge(sig["routed"], 1)
            mm(ps[:, 512:512 + NE], tri[:, :], msk[:, 0, :], start=True, stop=True)
            mm(ps[:, 512 + NE:512 + 2 * NE], tri[:, :], msk[:, 1, :], start=True, stop=False)
            mm(ps[:, 512 + NE:512 + 2 * NE], ones[:, :], msk[:, 0, :], start=False, stop=True)
            mm(ps[:, 512 + 2 * NE:512 + 3 * NE], ones[:, :], msk[:, 0, :], start=True, stop=False)
            mm(ps[:, 512 + 2 * NE:512 + 3 * NE], ones[:, :], msk[:, 1, :], start=False, stop=True).then_inc(sig["cum"], 1)
            pe.wait_ge(sig["gates"], 1)
            for t in range(TT):
                last = nc.tensor.transpose(ps[:, 4 * 512 + t * P:4 * 512 + (t + 1) * P], gate_pad[:, t, :], ident[:, :])
            last.then_inc(m["gt"], 1)
            pe.wait_ge(ld["bdown"], 16)
            for n in range(2):
                last = mm(bank(6 + n), ident[0:NE, :], mod[0:NE, 0, n * 512:(n + 1) * 512], start=True, stop=True)
            last.then_inc(sig["bd"], 1)

            def gather():
                for k in range(KC):
                    for t in range(TT):
                        last = mm(ps[:, 5 * 512 + k * CAP:5 * 512 + (k + 1) * CAP], hb[:, t, model_chunk(k)],
                                  pe_[:, t, :], start=(t == 0), stop=(t == TT - 1))
                last.then_inc(m["ga"], 1)

            def turn_gates():
                for t in range(TT):
                    last = nc.tensor.transpose(ps[:, 4 * 512 + t * P:4 * 512 + (t + 1) * P],
                                               pg[:, t, :, :].rearrange("p a s -> p (a s)"), ident[:, :])
                last.then_inc(m["gt"], 1)

            def combine(t):
                for n in range(2):
                    last = mm(bank((2, 6)[t] + n), gts[:, t * P:(t + 1) * P], outs[:, n * 512:(n + 1) * 512],
                              start=True, stop=True)
                last.then_inc(m["cb%d" % t], 1)

            def turn_gu(src, name):
                for ch in range(8):
                    last = mm(ps[:, 4 * 512 + ch * CAP:4 * 512 + (ch + 1) * CAP], src[:, ch * P:(ch + 1) * P],
                              twin[:, :], start=True, stop=True)
                last.then_inc(m[name], 1)

            pe.wait_ge(m["p"], 1)
            gather()
            pe.wait_ge(sig["npass"], 1)
            turns = pe.value_load(count_i[0:1, 0:1], min_val=NE, max_val=NE * PASSES)
            with pe.Fori(0, turns) as i:
                def unit(u, b0, lhs, first, k0):
                    for part, w in ((0, whi[:, BUF[u], :]), (1, wlo[:, BUF[u], :])):
                        pe.wait_ge((hi_rdy, lo_rdy)[part], i * len(SPLIT) + (SPLIT.index(u) + 1 + part * len(SPLIT)))
                        for k in range(2):
                            for n in range(2):
                                last = mm(bank(b0 + n), lhs[:, k0 + k, :, :].rearrange("p a s -> p (a s)"),
                                          w[:, (2 * k + n) * 512:(2 * k + n + 1) * 512],
                                          start=(first and part == 0 and k == 0),
                                          stop=(u % GU_UNITS == GU_UNITS - 1 and part == 1 and k == 1))
                    last.then_inc(used, 1)

                def unit_f32(u):
                    pe.wait_ge(raw[u], i * 16 + (raw_base[u] + 16))
                    for k in range(2):
                        for n in range(2):
                            last = mm(bank(6 + n), sgz[:, k, :, :].rearrange("p a s -> p (a s)"),
                                      slot(u)[:, (2 * k + n) * 512:(2 * k + n + 1) * 512],
                                      start=False, stop=False)
                    last.then_inc(used, 1)

                pe.wait_ge(m["xg"], i + 1)
                unit(0, 0, xg, True, 0)
                pe.wait_ge(m["out_cp"], i + 1)
                pe.wait_ge(m["gt_cp"], i + 1)
                combine(1)
                unit(1, 0, xg, False, 2)
                combine(0)
                unit(2, 0, xg, False, 4)
                unit(3, 0, xg, False, 6)
                pe.wait_ge(m["y0"], i + 1)
                unit(4, 2, xg, True, 0)
                unit(5, 2, xg, False, 2)
                pe.wait_ge(m["gua_cp"], i + 1)
                turn_gu(gu_a, "ta")
                unit(6, 2, xg, False, 4)
                pe.wait_ge(m["p"], i + 2)
                gather()
                unit(7, 2, xg, False, 6)
                pe.wait_ge(m["al_a"], i + 1)
                pe.wait_ge(m["y1"], i + 1)
                unit(8, 6, at, True, 0)
                pe.wait_ge(m["bias_a"], i + 1)
                pe.wait_ge(m["gub_cp"], i + 1)
                turn_gu(gu_b, "tb")
                unit(9, 6, at, False, 2)
                pe.wait_ge(m["bias_b"], i + 1)
                pe.wait_ge(m["pg"], i + 1)
                turn_gates()
                pe.wait_ge(m["a_b"], i + 1)
                unit_f32(F32_UNIT)
                pe.wait_ge(m["al_b"], i + 1)
                unit(11, 6, at, False, 4)
            pe.wait_ge(m["out_cp"], turns + 1)
            pe.wait_ge(m["gt_cp"], turns + 1)
            for t in (1, 0):
                combine(t)

        @block.vector
        def _(dve):
            own = [0]
            V = nc.vector

            def link(ins):
                own[0] += 1
                ins.then_inc(dve_c, 1)
                dve.wait_ge(dve_c, own[0])

            def mean_to_rsqrt(dst, src, n, done, sqrt_sem):
                V.tensor_scalar(dst, src, 1.0 / n, EPS, ALU.mult, ALU.add).then_inc(sig[done], 1)
                dve.wait_ge(sig[sqrt_sem], 1)
                link(V.reciprocal(dst, dst))

            V.memset(sums[:, 0:1], 0.0).then_inc(used, NU)
            V.memset(sums[:, 1:2], 0.0).then_inc(lo_rdy, len(SPLIT))
            V.memset(mod[:, :, :], 0.0).then_inc(sig["acc0"], 1)
            dve.wait_ge(sig["csil"], 1)
            link(V.tensor_tensor(csil, csil, crow, ALU.mult))
            V.tensor_copy(crep, csil.unsqueeze(2).to_broadcast([P, KC, P])).then_inc(sig["crep"], 1)
            dve.wait_ge(sig["lbT"], 1)
            V.tensor_copy(lbt, ps[:, 2048:2048 + 12]).then_inc(sig["lb_read"], 1)
            dve.wait_ge(sig["lb_read"], 1)
            link(V.tensor_tensor(omlb, lbt[:, 0:6], lbt[:, 6:12], ALU.max))
            V.tensor_tensor(lbt.rearrange("p (l h) -> p l h", l=2), lbt.rearrange("p (l h) -> p l h", l=2),
                            omlb.unsqueeze(1).to_broadcast([P, 2, HEADS]), ALU.subtract).then_inc(sig["lbT"], 1)
            dve.wait_ge(sig["masks_iota"], 1)
            it = tmp[:, 0:2 * P].bitcast(I32)
            link(V.tensor_tensor(tmp[:, 2 * P:3 * P].bitcast(I32), it[:, 0:P], it[:, P:2 * P], ALU.bitwise_xor))
            link(V.tensor_copy(tmp2[:, 3 * P:4 * P], tmp[:, 2 * P:3 * P].bitcast(I32)))
            link(V.tensor_copy(tmp2[:, 2 * P:3 * P], it[:, 0:P]))
            link(V.tensor_copy(tmp[:, 3 * P:4 * P], it[:, P:2 * P]))
            link(V.tensor_tensor(tmp[:, 0:P], tmp[:, 3 * P:4 * P], tmp2[:, 2 * P:3 * P], ALU.is_ge))
            link(V.scalar_tensor_tensor(out=tmp[:, P:2 * P], in0=tmp2[:, 3 * P:4 * P], scalar=1.0,
                                        in1=tmp[:, 0:P], op0=ALU.add, op1=ALU.mult))
            for lv in range(8):
                lo = 0 if lv == 0 else 1 << (lv - 1)
                up = 1 if lv == 0 else 1 << lv
                link(V.tensor_scalar(tmp[:, 0:P], tmp[:, P:2 * P], float(up) + 0.5, None, ALU.is_lt))
                link(V.scalar_tensor_tensor(out=masks[:, lv, :], in0=tmp[:, P:2 * P], scalar=float(lo) + 0.5,
                                            in1=tmp[:, 0:P], op0=ALU.is_gt, op1=ALU.mult))
            dve.wait_ge(sig["lb_done"], 1)
            link(V.tensor_tensor(omlb, lbt[:, 0:6], lbt[:, 6:12], ALU.add))
            link(V.reciprocal(omlb, omlb))
            link(V.tensor_tensor(lbt[:, 0:6], lbt[:, 0:6], omlb, ALU.mult))
            V.tensor_scalar(omlb, lbt[:, 0:6], -1.0, 1.0, ALU.mult, ALU.add)
            dve.wait_ge(sig["bguT"], 1)
            V.tensor_copy(bgu[:, :, :].rearrange("p e c -> p (e c)"), bank(5)).then_inc(sig["bgu_read"], 1)
            dve.wait_ge(ld["pos"], 16)
            dve.wait_ge(sig["consts"], 2)
            link(V.tensor_copy(post, posi[:, :]))
            ang = csn[:, 16:32].rearrange("p (t j) -> p t j", t=TT)
            turn = csn[:, 0:16].rearrange("p (t j) -> p t j", t=TT)
            link(V.tensor_tensor(ang, post.unsqueeze(2).to_broadcast([P, TT, HALF]),
                                 invf.unsqueeze(1).to_broadcast([P, TT, HALF]), ALU.mult))
            magic = 12582912.0
            link(V.tensor_scalar(turn, ang, 1.0 / (2 * math.pi), magic, ALU.mult, ALU.add))
            link(V.tensor_scalar(turn, turn, -magic, None, ALU.add))
            c1 = 6.28125
            c2 = float(np.float32(np.floor((2 * math.pi - c1) * 2 ** 19) / 2 ** 19))
            c3 = 2 * math.pi - c1 - c2
            for cc in (c1, c2, c3):
                link(V.scalar_tensor_tensor(out=csn[:, 16:32], in0=csn[:, 0:16], scalar=-cc, in1=csn[:, 16:32],
                                            op0=ALU.mult, op1=ALU.add))
            V.tensor_scalar(ang, ang, 3.1415925, -3.1415925, ALU.min, ALU.max).then_inc(sig["sin_arg"], 1)
            dve.wait_ge(sig["ssq"], TT)
            mean_to_rsqrt(rstd, ssq, D, "rsq", "rstd")
            dve.wait_ge(sig["sins"], 1)
            link(V.tensor_tensor(csn[:, 0:16], csn[:, 32:48], csn[:, 32:48], ALU.mult))
            link(V.tensor_scalar(csn[:, 0:16], csn[:, 0:16], -2.0, 1.0, ALU.mult, ALU.add))
            dve.wait_ge(ada_pe, KC)
            dve.wait_ge(ld["g1"], 16)
            for n in range(2):
                link(V.scalar_tensor_tensor(out=a1[:, n * 512:(n + 1) * 512], in0=bank(2 + n), scalar=1.0,
                                            in1=g1row[:, n * 512:(n + 1) * 512], op0=ALU.add, op1=ALU.mult))
            link(V.tensor_copy(b1, bank(0, 2)))
            for t in range(TT):
                link(V.scalar_tensor_tensor(out=hb[:, t, :], in0=xs[:, t, :], scalar=rstd[:, t:t + 1], in1=a1,
                                            op0=ALU.mult, op1=ALU.mult))
                V.tensor_tensor(hb[:, t, :], hb[:, t, :], b1, ALU.add).then_inc(sig["h1"], 1)

            def half_copy(name):
                dve.wait_ge(sig[name], 1)
                V.tensor_copy(ht[:, KC // 2:KC, :].rearrange("p k t -> p (k t)"), bank(6, 2)).then_inc(sig[name + "_dve"], 1)

            half_copy("h1T")
            dve.wait_ge(ld["ada2_bias"], 16)

            def accumulate(j):
                landed(dve, ("ada2", j))
                a = mod[:, 2 * (j // KC):2 * (j // KC) + 2, :].rearrange("p a d -> p (a d)")
                V.scalar_tensor_tensor(out=a, in0=slot(place[("ada2", j)] % PRE), scalar=csil[:, j % KC:j % KC + 1],
                                       in1=a, op0=ALU.mult, op1=ALU.add).then_inc(ada_dve, 1)
                dve.wait_ge(ada_dve, j + 1)

            def group(j):
                b = 6 + j % 2
                if j < 3:
                    dve.wait_ge(win_sig, j + 1)
                    for h in (2 * j, 2 * j + 1):
                        link(V.tensor_scalar(fg[:, h, :], fg[:, h, :], omlb[:, h:h + 1], lbt[:, h:h + 1],
                                             ALU.mult, ALU.add))
                    V.tensor_scalar(kd[:, 2 * j:2 * j + 2, :], fg[:, 2 * j:2 * j + 2, :], -1.0, 1.0,
                                    ALU.mult, ALU.add).then_inc(hk_ready, 1)
                elif j < 6:
                    dve.wait_ge(win_sig, j + 1)
                    q = qd[:, 2 * (j - 3):2 * (j - 3) + 2, :].rearrange("p h t -> p (h t)")
                    V.scalar_tensor_tensor(out=q, in0=bank(b), scalar=float(P) ** -0.5, in1=q,
                                           op0=ALU.mult, op1=ALU.mult).then_inc(hq_ready, 1)
                elif j >= 12:
                    dve.wait_ge(win_sig, j - 12 + 7)
                    g = hgate[:, :, (j - 12) * CG:(j - 11) * CG]
                    V.tensor_tensor(g, g, bank(b).rearrange("p (t n) -> p t n", t=TT), ALU.mult).then_inc(sig["hg_read"], 1)
                    dve.wait_ge(sig["hg_read"], j - 11)
                    gg = g.rearrange("p t (h n) -> p t h n", h=2)
                    for t in range(TT):
                        link(V.tensor_tensor(gg[:, t], gg[:, t], hgrow.unsqueeze(1).to_broadcast([P, 2, P]), ALU.mult))

            def update(lv):
                if lv == 1:
                    for g in range(2):
                        dve.wait_ge(lev_done[g], 1)
                        V.tensor_tensor(qd[:, 3 * g:3 * g + 3, :], qd[:, 3 * g:3 * g + 3, :], fg[:, 3 * g:3 * g + 3, :],
                                        ALU.mult).then_inc(q_upd[g], 1)
                    return
                n = 1 << (lv - 2)
                d = block_decay(n)
                if n > 1:
                    dve.wait_ge(tot_upd, lv - 2)
                if lv < 8:
                    V.tensor_tensor(block_decay(2 * n).rearrange("p b r -> p (b r)"), d[:, :, 0], d[:, :, 1],
                                    ALU.mult).then_inc(tot_upd, 1)
                for g in range(2):
                    dve.wait_ge(lev_done[g], lv)
                    dve.wait_ge(q_upd[g], lv - 1)
                    qv = qd[:, 3 * g:3 * g + 3, :].rearrange("p h (b r n) -> p (h b) r n", r=2, n=n)[:, :, 1, :]
                    left = block_decay(n, g)[:, :, 0]
                    V.tensor_tensor(qv, qv, left.unsqueeze(2).to_broadcast([P, 3 * T // (2 * n), n]),
                                    ALU.mult).then_inc(q_upd[g], 1)

            def merge(lv):
                b0 = 3 * (lv % 2)
                for g in range(2):
                    dve.wait_ge(lev_done[g], lv + 1)
                if lv:
                    dve.wait_ge(sct_done, lv)
                V.copy_predicated(sct.rearrange("p (j n) -> p j n", n=P),
                                  masks[:, lv, :].unsqueeze(1).to_broadcast([P, 12, P]),
                                  bank(b0, 3).rearrange("p (j n) -> p j n", n=P)).then_inc(sct_done, 1)

            def rotate():
                dve.wait_ge(act_evac, 2)
                q8 = aqk.rearrange("p (t h d) -> p t h d", t=TT, h=2 * AH)
                t1, t2 = q8[:, :, :, 0:HALF], q8[:, :, :, HALF:ROT]
                cos = csn[:, 0:16].rearrange("p (t j) -> p t j", t=TT).unsqueeze(2).to_broadcast([P, TT, 2 * AH, HALF])
                sin = csn[:, 16:32].rearrange("p (t j) -> p t j", t=TT).unsqueeze(2).to_broadcast([P, TT, 2 * AH, HALF])
                b = [tmp[:, n * P:(n + 1) * P].rearrange("p (t h j) -> p t h j", t=TT, h=2 * AH) for n in range(4)]
                V.tensor_tensor(b[0], t1, cos, ALU.mult)
                V.tensor_tensor(b[1], t2, sin, ALU.mult)
                V.tensor_tensor(b[2], t2, cos, ALU.mult)
                link(V.tensor_tensor(b[3], t1, sin, ALU.mult))
                V.tensor_tensor(t1, b[0], b[1], ALU.subtract)
                V.tensor_tensor(t2, b[2], b[3], ALU.add).then_inc(sig["rot"], 1)

            def softmax_in():
                dve.wait_ge(sig["sc"], 1)
                sc = bank(0, 3).rearrange("p (b s) -> p b s", b=12)
                scale = float(HD) ** -0.5
                cm = cmask.unsqueeze(1).to_broadcast([P, AH, P])
                V.scalar_tensor_tensor(out=pb[:, 0:4, :], in0=sc[:, 0:4, :], scalar=scale, in1=cm, op0=ALU.mult, op1=ALU.add)
                V.scalar_tensor_tensor(out=pb[:, 5:12:2, :], in0=sc[:, 5:12:2, :], scalar=scale, in1=cm,
                                       op0=ALU.mult, op1=ALU.add)
                V.tensor_scalar(pb[:, 4:12:2, :], sc[:, 4:12:2, :], scale, None, ALU.mult).then_inc(sig["sc_read"], 1)
                dve.wait_ge(sig["sc_read"], 1)
                late = pb[:, 4:12, :].rearrange("p (h s) n -> p h (s n)", h=AH)
                link(V.tensor_reduce(amax[:, 0:4], pb[:, 0:4, :], AX.X, ALU.max))
                link(V.tensor_reduce(amax[:, 4:8], late, AX.X, ALU.max))
                link(V.tensor_tensor(pb[:, 0:4, :], pb[:, 0:4, :], amax[:, 0:4].unsqueeze(2).to_broadcast([P, AH, P]),
                                     ALU.subtract))
                V.tensor_tensor(late, late, amax[:, 4:8].unsqueeze(2).to_broadcast([P, AH, T]),
                                ALU.subtract).then_inc(sig["sc_ready"], 1)

            def softmax_sum():
                dve.wait_ge(sig["expd"], 1)
                late = pb[:, 4:12, :].rearrange("p (h s) n -> p h (s n)", h=AH)
                V.tensor_reduce(asum[:, 0:4], pb[:, 0:4, :], AX.X, ALU.add)
                link(V.tensor_reduce(asum[:, 4:8], late, AX.X, ALU.add))
                link(V.reciprocal(amax, asum))

            oa = pb.rearrange("p b s -> p (b s)")[:, 0:512].rearrange("p (j d) -> p j d", d=HD)
            ob = pb.rearrange("p b s -> p (b s)")[:, 512:1024].rearrange("p (j d) -> p j d", d=HD)

            def attention_norm():
                dve.wait_ge(sig["o_att"], 1)
                V.tensor_tensor(oa, bank(3).rearrange("p (j d) -> p j d", d=HD),
                                amax.unsqueeze(2).to_broadcast([P, 8, HD]), ALU.mult).then_inc(sig["o_att_read"], 1)
                dve.wait_ge(sig["o_att_read"], 1)
                link(V.tensor_tensor(ob, oa, oa, ALU.mult))
                link(V.tensor_reduce(asum, ob, AX.X, ALU.add))
                V.tensor_scalar(asum, asum, 1.0 / HD, EPS, ALU.mult, ALU.add).then_inc(sig["aatt_ms"], 1)

            def attention_cat():
                dve.wait_ge(sig["aatt_sq"], 1)
                link(V.reciprocal(asum, asum))
                link(V.tensor_tensor(oa, oa, asum.unsqueeze(2).to_broadcast([P, 8, HD]), ALU.mult))
                for t in range(TT):
                    V.tensor_tensor(hb[:, t, HW_:D].rearrange("p (h d) -> p h d", h=AH), oa[:, 4 * t:4 * t + 4, :],
                                    agrow.unsqueeze(1).to_broadcast([P, AH, HD]), ALU.mult)

            dve.wait_ge(ld["hg"], 16)
            dve.wait_ge(ld["ag"], 16)
            for j in range(WIN_UNITS):
                accumulate(j)
                group(j)
                if j == 7:
                    rotate()
                    update(1)
                    merge(0)
                if j == 8:
                    update(2)
                    merge(1)
                    update(3)
                    merge(2)
                if j == 9:
                    softmax_in()
                    update(4)
                    merge(3)
                if j == 10:
                    update(5)
                    merge(4)
                if j == 11:
                    update(6)
                    merge(5)
                    softmax_sum()
                if j == 12:
                    attention_norm()
                    update(7)
                    merge(6)
                if j == 13:
                    update(8)
                    merge(7)
            attention_cat()
            accumulate(WIN_UNITS)
            dve.wait_ge(sig["oh_sq"], 1)
            link(V.tensor_reduce(rs2, fg.rearrange("p h (t n) -> p (h t) n", t=TT), AX.X, ALU.add))
            V.tensor_scalar(rs2, rs2, 1.0 / P, EPS, ALU.mult, ALU.add).then_inc(sig["oh_ms"], 1)
            dve.wait_ge(sig["oh_rs"], 1)
            link(V.reciprocal(rs2, rs2))
            tt3 = tot.rearrange("p (j n) -> p j n", n=P)
            link(V.tensor_tensor(tt3, bank(3, 3).rearrange("p (j n) -> p j n", n=P),
                                 rs2.unsqueeze(2).to_broadcast([P, 12, P]), ALU.mult))
            tt4 = tot.rearrange("p (h t n) -> p h t n", h=HEADS, t=TT)
            for t in range(TT):
                V.tensor_tensor(hb[:, t, 0:HW_].rearrange("p (h n) -> p h n", h=HEADS), tt4[:, :, t, :],
                                hgate[:, t, :].rearrange("p (h n) -> p h n", h=HEADS), ALU.mult).then_inc(sig["hg_cat"], 1)
            half_copy("oT")
            dve.wait_ge(sig["mod_copied"], 8)
            if not debug:
                dve.wait_ge(ld["g2"], 16)
                V.scalar_tensor_tensor(out=mod[:, 2, :], in0=mod[:, 2, :], scalar=1.0, in1=yacc[:, 0, :],
                                       op0=ALU.add, op1=ALU.mult).then_inc(sig["g2_read"], 1)
                dve.wait_ge(sig["g2_read"], 1)
            for j in range(D // CG):
                dve.wait_ge(wout_pe, j + 1)
                mv = tmp[:, :].rearrange("p (t n) -> p t n", t=TT)
                link(V.tensor_tensor(mv, bank(j).rearrange("p (t n) -> p t n", t=TT),
                                     mod[:, 0, j * CG:(j + 1) * CG].unsqueeze(1).to_broadcast([P, TT, CG]), ALU.mult))
                xv = xs[:, :, j * CG:(j + 1) * CG]
                V.tensor_tensor(xv, xv, mv, ALU.add).then_inc(sig["x1"], 1)
                dve.wait_ge(sig["x1"], j + 1)
            if debug:
                return
            dve.wait_ge(sig["ssq2"], TT)
            mean_to_rsqrt(rstd, ssq, D, "rms2", "rs2")
            for t in range(TT):
                link(V.scalar_tensor_tensor(out=hb[:, t, :], in0=xs[:, t, :], scalar=rstd[:, t:t + 1], in1=mod[:, 2, :],
                                            op0=ALU.mult, op1=ALU.mult))
                V.tensor_tensor(hb[:, t, :], hb[:, t, :], mod[:, 1, :], ALU.add).then_inc(sig["h2"], 1)
            half_copy("h2T")
            dve.wait_ge(sig["logits"], 1)
            dve.wait_ge(ld["br"], 16)
            lg = tmp2[:, 0:TT * NE].rearrange("p (t e) -> p t e", t=TT)
            V.memset(gate_pad, 0.0)
            link(V.tensor_tensor(lg, ps[:, 0:TT * NE].rearrange("p (t e) -> p t e", t=TT),
                                 br[:, :].unsqueeze(1).to_broadcast([P, TT, NE]), ALU.add))
            V.max(v8[:, 0, :], lg[:, 0, :])
            link(V.max(v8[:, 1, :], lg[:, 1, :]))
            V.tensor_tensor(e4, v8[:, :, 0:TOPK], v8[:, :, 0:1].to_broadcast([P, TT, TOPK]),
                            ALU.subtract).then_inc(sig["v8"], 1)
            V.max_index(ismall[:, 0:8], v8[:, 0, :], lg[:, 0, :])
            link(V.max_index(ismall[:, 8:16], v8[:, 1, :], lg[:, 1, :]))
            link(V.tensor_copy(idf, ismall[:, :].rearrange("p (t k) -> p t k", t=TT)))
            hot = tmp2[:, 0:TT * TOPK * NE].rearrange("p (t k e) -> p t k e", t=TT, k=TOPK)
            link(V.tensor_tensor(hot, iota_e[:, :].unsqueeze(1).unsqueeze(1).to_broadcast([P, TT, TOPK, NE]),
                                 idf[:, :, 0:TOPK].unsqueeze(3).to_broadcast([P, TT, TOPK, NE]), ALU.is_equal))
            V.tensor_reduce(msk[:, :, :], hot.rearrange("p t k e -> p t e k"), AX.X, ALU.add).then_inc(sig["routed"], 1)
            dve.wait_ge(sig["e4"], 1)
            link(V.tensor_reduce(esum, e4, AX.X, ALU.add))
            link(V.reciprocal(esum, esum))
            link(V.tensor_tensor(e4, e4, esum.unsqueeze(2).to_broadcast([P, TT, TOPK]), ALU.mult))
            link(V.tensor_tensor(hot, hot, e4.unsqueeze(3).to_broadcast([P, TT, TOPK, NE]), ALU.mult))
            link(V.tensor_reduce(gate[:, :, :], hot.rearrange("p t k e -> p t e k"), AX.X, ALU.add))
            V.tensor_copy(gate_pad[:, :, 0:NE], gate[:, :, :]).then_inc(sig["gates"], 1)
            dve.wait_ge(sig["cum"], 1)
            cum = ps[:, 512:512 + 2 * NE].rearrange("p (t e) -> p t e", t=TT)
            pos = tmp2[:, 256:256 + TT * NE].rearrange("p (t e) -> p t e", t=TT)
            link(V.tensor_tensor(pos, cum, msk[:, :, :], ALU.mult))
            V.tensor_reduce(cnt[:, 0:1], ps[:, 512 + 2 * NE:512 + 3 * NE], AX.X, ALU.max)
            for p_ in range(PASSES):
                last = V.tensor_scalar(posx[:, :, p_ * NE:(p_ + 1) * NE], pos, -1.0 - CAP * p_, None, ALU.add)
            link(last)
            for p_ in range(1, PASSES):
                last = V.tensor_scalar(cnt[:, p_:p_ + 1], cnt[:, 0:1], p_ * CAP + 0.5, float(NE), ALU.is_gt, ALU.mult)
            link(last)
            link(V.tensor_reduce(cnt[:, 0:1], cnt[:, 1:PASSES], AX.X, ALU.add))
            V.tensor_scalar(count_i[:, :], cnt[:, 0:1], float(NE), None, ALU.add).then_inc(sig["npass"], 1)
            dve.wait_ge(sig["y_zero"], 1)

            def one_hot(i):
                col = posx[:, :, i:i + 1] if isinstance(i, int) else posx[:, :, bass.ds(i, 1)]
                V.tensor_tensor(pe_[:, :, :], iota_s[:, :, :], col.to_broadcast([P, TT, CAP]),
                                ALU.is_equal).then_inc(m["p"], 1)

            one_hot(0)
            dve.wait_ge(m["xg_hi"], 1)
            g5 = bank(5).rearrange("p (k s) -> p k s", k=KC)
            V.tensor_tensor(xg[:, :, 1, :], g5, xg[:, :, 0, :].bitcast(F32), ALU.subtract).then_inc(m["xg"], 1)
            dve.wait_ge(sig["npass"], 1)
            turns = dve.value_load(count_i[0:1, 0:1], min_val=NE, max_val=NE * PASSES)
            with dve.Fori(0, turns) as i:
                e = dve.snap(i & (NE - 1))

                def lo(u):
                    dve.wait_ge(hi_rdy, i * len(SPLIT) + (SPLIT.index(u) + 1))
                    dve.wait_ge(used, i * NU + buffer_user(u))
                    V.tensor_tensor(wlo[:, BUF[u], :], slot(u), whi[:, BUF[u], :].bitcast(F32),
                                    ALU.subtract).then_inc(lo_rdy, 1)

                def half_in(s, h):
                    dve.wait_ge(m["t" + s], i + 1)
                    bias = bgu[:, bass.ds(e, 1), :].rearrange("p a (g c) -> p (a g) c", g=2)[:, :, 4 * h:4 * h + 4]
                    V.tensor_tensor(guT[:, :, :].rearrange("p (g c) s -> p g c s", g=2),
                                    bank(4).rearrange("p (g c s) -> p g c s", g=2, c=4),
                                    bias.unsqueeze(3).to_broadcast([P, 2, 4, CAP]), ALU.add).then_inc(m["bias_" + s], 1)
                    dve.wait_ge(m["bias_" + s], i + 1)
                    V.tensor_scalar(guT[:, 0:4, :], guT[:, 0:4, :], LIMIT, None, ALU.min).then_inc(m["g_" + s], 1)
                    V.tensor_scalar(guT[:, 4:8, :], guT[:, 4:8, :], LIMIT, -LIMIT, ALU.min, ALU.max).then_inc(m["u_" + s], 1)

                def half_act(s, h):
                    dve.wait_ge(m["u_" + s], i + 1)
                    V.scalar_tensor_tensor(out=guT[:, 4:8, :], in0=guT[:, 4:8, :], scalar=1.0, in1=guT[:, 0:4, :],
                                           op0=ALU.add, op1=ALU.mult).then_inc(m["t"], 1)
                    dve.wait_ge(m["t"], i * 2 + (h + 1))
                    dve.wait_ge(m["sig_" + s], i + 1)
                    V.tensor_tensor(sg, sg, guT[:, 4:8, :], ALU.mult).then_inc(m["a_" + s], 1)

                def half_lo(s):
                    dve.wait_ge(m["ah_" + s], i + 1)
                    V.tensor_tensor(at[:, AT[s], 1, :], sg[:, SG[s], :], at[:, AT[s], 0, :].bitcast(F32),
                                    ALU.subtract).then_inc(m["al_" + s], 1)

                for u in range(3):
                    lo(u)
                dve.wait_ge(m["cb1"], i + 1)
                V.tensor_tensor(yacc[:, 1, :], yacc[:, 1, :], bank(6, 2), ALU.add).then_inc(m["y1"], 1)
                lo(3)
                dve.wait_ge(m["cb0"], i + 1)
                V.tensor_tensor(yacc[:, 0, :], yacc[:, 0, :], bank(2, 2), ALU.add).then_inc(m["y0"], 1)
                lo(4)
                dve.wait_ge(m["pg"], i + 1)
                one_hot(dve.snap(i + 1))
                for u in range(5, 8):
                    lo(u)
                half_in("a", 0)
                half_act("a", 0)
                lo(8)
                half_lo("a")
                lo(9)
                dve.wait_ge(m["xg_hi"], i + 2)
                V.tensor_tensor(xg[:, :, 1, :], g5, xg[:, :, 0, :].bitcast(F32), ALU.subtract).then_inc(m["xg"], 1)
                half_in("b", 1)
                half_act("b", 1)
                half_lo("b")
                lo(11)
            for t in range(TT):
                dve.wait_ge(m["y%d" % t], turns)
                link(V.tensor_tensor(yacc[:, t, :], yacc[:, t, :], gate2, ALU.mult))
                link(V.tensor_tensor(xs[:, t, :], xs[:, t, :], yacc[:, t, :], ALU.add))
            for t in (1, 0):
                dve.wait_ge(m["cb%d" % t], turns + 1)
                link(V.tensor_tensor(yacc[:, t, :], bank((2, 6)[t], 2), gate2, ALU.mult))
                V.tensor_tensor(xs[:, t, :], xs[:, t, :], yacc[:, t, :], ALU.add).then_inc(sig["ofin"], 1)
            dve.wait_ge(ld["gfin"], 16)
            for n, t in enumerate((1, 0)):
                r_ = rstd[:, t:t + 1]
                dve.wait_ge(sig["out_ssq"], n + 1)
                V.tensor_scalar(r_, ssq[:, t:t + 1], 1.0 / D, EPS, ALU.mult, ALU.add).then_inc(sig["out_rms"], 1)
                dve.wait_ge(sig["out_rs"], n + 1)
                link(V.reciprocal(r_, r_))
                V.scalar_tensor_tensor(out=xs[:, t, :], in0=xs[:, t, :], scalar=r_, in1=gfin,
                                       op0=ALU.mult, op1=ALU.mult).then_inc(sig["fin"], 1)


_INS = ["x", "c", "positions", "w_ada", "b_ada", "norm1_g", "w_in", "hgrn_lb_logits", "hgrn_norm_g", "attn_norm_g",
        "w_out", "norm2_g", "w_router", "b_router", "w_gate_up", "b_gate_up", "w_down", "b_down", "final_norm_g"]
DEBUG = False


def kernel(**inputs):
    import concourse.bacc as _bacc
    from concourse.bass_utils import run_bass_kernel_spmd as _run

    nc = _bacc.Bacc("TRN2", target_bir_lowering=False, num_devices=1)
    arrays, args = {}, []
    for name in _INS:
        a = np.ascontiguousarray(inputs[name])
        arrays[f"in_{name}_dram"] = a
        args.append(nc.dram_tensor(f"in_{name}_dram", a.shape, mybir.dt.from_np(a.dtype), kind="ExternalInput").ap())
    args.append(nc.dram_tensor("out_dram", (1, T, D), F32, kind="ExternalOutput").ap())
    decoder_block(nc, *args, debug=DEBUG)
    r = _run(nc, [arrays], core_ids=[0])
    return r.results[0]["out_dram"]
```

```python
import math
from contextlib import ExitStack

import numpy as np
import concourse.bass as bass
from concourse import mybir

F32 = mybir.dt.float32
F32R = mybir.dt.float32r
I32 = mybir.dt.int32
U32 = mybir.dt.uint32
U8 = mybir.dt.uint8
ALU = mybir.AluOpType
ACT = mybir.ActivationFunctionType
AX = mybir.AxisListType


P = 128
D = 1024
T = 256
TT = T // P
KC = D // P
HEADS = 6
HW_ = HEADS * P
AH = 4
HD = 64
AW = AH * HD
ROT = HD // 4
HALF = ROT // 2
THETA = 500000.0
NE = 32
TOPK = 4
FF = D
CAP = 64
PASSES = T // CAP
EPS = 1e-6
ALPHA = 1.702
LIMIT = 7.0

U = 2048
SLOTS = 12
PRE = 4
GU_UNITS = 4
NU = 12
F32_UNIT = 10
SPLIT = [u for u in range(NU) if u != F32_UNIT]
BUFS = 3
BUF = {u: u % BUFS for u in SPLIT}
SG = {"a": slice(0, 4), "b": slice(2, 4)}
AT = {"a": slice(0, 4), "b": slice(4, 6)}
WIN_UNITS = 15
CG = 256
NEG = -1e30
MOD_BANKS = (6, 7, 0, 1, 2)
ROWS = 3 * KC + 2 * HEADS


EARLY = {4: PRE + 1, 5: PRE + 2, 6: PRE + 4, 7: PRE + 5}


def stream_plan():
    plan = [("ada1", k) for k in range(PRE)]
    for j in range(WIN_UNITS):
        plan += [("win", j), ("ada2", j)]
    plan.append(("ada2", WIN_UNITS))
    plan += [("wout", j) for j in range(D // CG)]
    return plan


def decoder_block(nc, x, c, positions, w_ada, b_ada, norm1_g, w_in, lb_logits, hgrn_g, attn_g,
                  w_out, norm2_g, w_router, b_router, w_gate_up, b_gate_up, w_down, b_down,
                  final_g, out):
    plan = stream_plan()
    place = {key: n for n, key in enumerate(plan)}

    win_col = [HW_ + CG * j for j in range(3)] + [CG * j for j in range(3)] \
        + [4 * HW_, 4 * HW_ + AW, 4 * HW_ + 2 * AW] \
        + [2 * HW_ + CG * j for j in range(3)] + [3 * HW_ + CG * j for j in range(3)]

    with ExitStack() as ctx:
        def sb(name, shape, dt=F32):
            return ctx.enter_context(nc.sbuf_tensor(name, shape, dt))

        def sem(name):
            return ctx.enter_context(nc.semaphore(name))

        ps = ctx.enter_context(nc.psum_tensor("ps", [P, 8 * 512], F32))

        def bank(b, n=1):
            return ps[:, b * 512:(b + n) * 512]

        ring = sb("ring", [P, SLOTS * U])
        whi = sb("whi", [P, BUFS, U], F32R)
        with nc.sbuf_tensor("ht", [P, KC, T], F32) as ht:
            pass
        wlo = sb("wlo", [P, BUFS, U], F32R)
        xg = sb("xg", [P, KC, 2, CAP], F32R)
        at = sb("at", [P, 6, 2, CAP], F32R)
        xs = sb("xs", [P, TT, D])
        hb = sb("hb", [P, TT, D])
        mod = sb("mod", [P, 4, D])
        yacc = sb("yacc", [P, TT, D])

        def slot(s):
            return ring[:, s * U:(s + 1) * U]

        arena_at = [PRE * U]

        def arena(n):
            a = arena_at[0]
            arena_at[0] += n
            assert arena_at[0] <= SLOTS * U
            return ring[:, a:a + n]

        fg = arena(HEADS * T).rearrange("p (h t) -> p h t", h=HEADS)
        qd = arena(HEADS * T).rearrange("p (h t) -> p h t", h=HEADS)
        kd = arena(HEADS * T).rearrange("p (h t) -> p h t", h=HEADS)
        tot = arena(HEADS * T)
        sct = arena(HEADS * T)
        cross = arena(HEADS * P)
        aqk = arena(TT * 2 * AW)
        av = arena(TT * AW).rearrange("p (t n) -> p t n", t=TT)
        qkt = arena(4 * T).rearrange("p (c t) -> p c t", c=4)
        pb = arena(12 * P).rearrange("p (b s) -> p b s", b=12)
        pt = arena(12 * P).rearrange("p (b s) -> p b s", b=12)
        hgate = arena(TT * HW_).rearrange("p (t n) -> p t n", t=TT)
        masks = arena(8 * P // 4).bitcast(U8).rearrange("p (l t) -> p l t", l=8)
        cmask = arena(P)
        bsrc = pt.rearrange("p b s -> p (b s)")[:, 0:4 * P]
        hgrow = arena(P)
        agrow = arena(HD)
        cols = arena(3 * KC + 2 * HEADS)
        a1 = arena(KC)
        b1 = arena(KC)
        lbt = cols[:, 3 * KC:]
        omlb = arena(HEADS)
        assert arena_at[0] <= SLOTS * U

        tmp = sb("tmp", [P, 512])
        tmp2 = sb("tmp2", [P, 512])
        guT = sb("guT", [P, 8, CAP])
        sgz = sb("sgz", [P, 4, 2, CAP])
        pe_ = sb("pe_", [P, TT, CAP])
        gts = sb("gts", [P, T])
        bgu = sb("bgu", [P, NE, 16])
        posx = sb("posx", [P, TT, PASSES * NE + 1])
        gate = sb("gate", [P, TT, NE])
        msk = sb("msk", [P, TT, NE])
        br = sb("br", [P, NE])
        ident = sb("ident", [P, P])
        twin = sb("twin", [P, CAP])
        ones = sb("ones", [P, P])
        tri = sb("tri", [P, P])
        iota_s = sb("iota_s", [P, TT, CAP])
        iota_e = sb("iota_e", [P, NE])
        small = sb("small", [P, 160])
        ismall = sb("ismall", [P, 16], U32)
        count_i = sb("count_i", [P, 1], I32)
        sg = sgz[:, :, 0, :]
        wr = guT[:, 0:KC * NE // CAP, :].rearrange("p c s -> p (c s)").rearrange("p (k e) -> p k e", k=KC)
        pg = tmp[:, 0:TT * 2 * CAP].rearrange("p (t a s) -> p t a s", t=TT, a=2)
        crow = small[:, 0:8]
        csil = small[:, 8:16]
        ssq = small[:, 16:18]
        rstd = small[:, 18:20]
        ssq4 = small[:, 92:100].rearrange("p (t j) -> p t j", t=TT)
        post = small[:, 20:22]
        seed = small[:, 24:36]
        rs2 = small[:, 36:48]
        amax = small[:, 48:56]
        asum = small[:, 56:64]
        v8 = small[:, 64:80].rearrange("p (t k) -> p t k", t=TT)
        e4 = small[:, 40:48].rearrange("p (t k) -> p t k", t=TT)
        idf = small[:, 24:40].rearrange("p (t k) -> p t k", t=TT)
        esum = small[:, 84:86]
        cnt = small[:, 86:90]
        invf = small[:, 92:100]
        csn = small[:, 100:148]
        posi = sb("posi", [P, TT], I32)
        gate_pad = tmp[:, 0:TT * P].rearrange("p (t n) -> p t n", t=TT)
        ada1 = yacc[:, :, :].rearrange("p t d -> p (t d)")
        vh = yacc[:, :, :].rearrange("p t d -> p (t d)")[:, 0:TT * HW_].rearrange("p (t n) -> p t n", t=TT)
        gu_a = mod[:, 0, :]
        gu_b = mod[:, 1, :]
        outs = mod[:, 2, :]
        gate2 = mod[:, 3, :]
        gfin = hb[:, 1, :]

        ld = {n: sem("ld_" + n) for n in
              "x c pos rows ada2_bias bgu hg ag wr br g2 bdown gfin".split()}
        raw = [sem(f"raw{s}") for s in range(SLOTS)]
        sig = {n: sem("s_" + n) for n in
               """ident consts masks_iota csil colsT ada1 a1 lb_max lb_done bguT bgu_read ssq rsq rstd rs1
               h1 h1T h1T_act h1T_dve sin_arg sins rot aT aT_copied sc_even sc sc_read sc_ready expd pT pT_copied
               o_att o_att_read aatt_ms aatt_sq cross cross_copied oh oh_sq oh_ms oh_rs hg_read hg_cat
               oT oT_act oT_dve ada2 mod_copied g2_read acc0 x1 ssq2 rms2 rs2 h2 h2T h2T_act h2T_dve logits v8 e4 gates
               routed cum y_zero npass out_rms out_ssq out_rs fin stored ofin""".split()}
        win_sig = sem("win_sig")
        act_evac = sem("act_evac")
        ada1_dve = sem("ada1_dve")
        win_pe = sem("win_pe")
        wout_pe = sem("wout_pe")
        ada_dve = sem("ada_dve")
        lev_done = [sem(f"lev_done{g}") for g in range(2)]
        q_upd = [sem(f"q_upd{g}") for g in range(2)]
        k_upd = [sem(f"k_upd{g}") for g in range(2)]
        tot_upd = sem("tot_upd")
        hq_ready = sem("hq_ready")
        hk_ready = sem("hk_ready")
        sct_done = sem("sct_done")
        dve_c = sem("dve_c")
        act_c = sem("act_c")
        pool_c = sem("pool_c")
        hi_rdy = sem("hi_rdy")
        lo_rdy = sem("lo_rdy")
        used = sem("used")
        m = {n: sem("m_" + n) for n in
             """xg_hi xg ga p pg gt gt_cp gua_cp gub_cp ta tb bias_a bias_b g_a g_b sig_a sig_b
             a_a a_b ah_a ah_b al_a al_b cb0 cb1 y0 y1 out_cp u_a u_b ug_a ug_b""".split()}

        def buffer_user(u):
            before = [v for v in SPLIT if v < u and BUF[v] == BUF[u]]
            return before[-1] + 1 + NU if before else max(v for v in SPLIT if BUF[v] == BUF[u]) + 1

        early = {k: sem(f"ada1_early{k}") for k in EARLY}

        block = ctx.enter_context(nc.Block())

        raw_base = [0] * SLOTS
        for n in range(len(plan)):
            raw_base[n % PRE] += 16

        def landed(eng, key):
            n = place[key]
            eng.wait_ge(raw[n % PRE], 16 * (n // PRE + 1))

        def used_by(eng, key):
            kind, j = key
            s = {"ada1": ada1_dve, "win": win_pe, "wout": wout_pe, "ada2": ada_dve}[kind]
            eng.wait_ge(s, j + 1)

        ada_v = w_ada.rearrange("l (p k) n -> l p k n", k=KC)
        win_v = w_in.rearrange("l (k p) n -> l p k n", p=P)
        wout_v = w_out.rearrange("l (k p) n -> l p k n", p=P)
        x_v = x.rearrange("b (t p) d -> (b p) t d", p=P)
        out_v = out.rearrange("b (t p) d -> (b p) t d", p=P)

        def unit_src(kind, j):
            if kind == "ada1":
                return ada_v[0, :, j, 0:U]
            if kind == "ada2":
                return ada_v[0, :, j % KC, U * (1 + j // KC):U * (2 + j // KC)]
            if kind == "win":
                return win_v[0, :, :, win_col[j]:win_col[j] + CG]
            return wout_v[0, :, :, CG * j:CG * (j + 1)]

        def model_chunk(k):
            return slice(k // 2 * 2 * P + k % 2, (k // 2 + 1) * 2 * P, 2)

        def expert_load(sp, e, u):
            dst = slot(u)
            if u < 2 * GU_UNITS:
                half, k2 = u // GU_UNITS, u % GU_UNITS
                src = w_gate_up[0, e, k2 * 2 * P:(k2 + 1) * 2 * P, :]
                src = src.rearrange("(p k) (g n) -> p (k g) n", p=P, g=2)[:, :, half * 512:(half + 1) * 512]
                sp.dma_start(dst.rearrange("p (k n) -> p k n", k=4), src).then_inc(raw[u], 16)
            else:
                k2 = u - 2 * GU_UNITS
                src = w_down[0, e, k2 * 2 * P:(k2 + 1) * 2 * P, :].rearrange("(k p) n -> p k n", p=P)
                sp.dma_start(dst.rearrange("p (k n) -> p k n", k=2), src).then_inc(raw[u], 16)

        @block.sync
        def _(sp):
            for n, (kind, j) in enumerate(plan):
                if n >= PRE:
                    used_by(sp, plan[n - PRE])
                src = unit_src(kind, j)
                dst = slot(n % PRE)
                if kind in ("win", "wout"):
                    dst = dst.rearrange("p (k n) -> p k n", k=KC)
                sp.dma_start(dst, src).then_inc(raw[n % PRE], 16)
                if n == PRE - 1:
                    for k in EARLY:
                        sp.dma_start(slot(EARLY[k]), unit_src("ada1", k)).then_inc(early[k], 16)
            sp.wait_ge(sig["hg_cat"], TT)
            for u in range(PRE, NU):
                expert_load(sp, 0, u)
            sp.wait_ge(wout_pe, D // CG)
            for u in range(PRE):
                expert_load(sp, 0, u)
            sp.wait_ge(sig["npass"], 1)
            turns = sp.value_load(count_i[0:1, 0:1], min_val=NE, max_val=NE * PASSES)
            with sp.Fori(1, turns) as i:
                e = sp.snap(i & (NE - 1))
                done = sp.snap(i >> (NE.bit_length() - 1))
                for u in range(NU):
                    if u in SPLIT:
                        sp.wait_ge(lo_rdy, done * (NE * len(SPLIT)) + e * len(SPLIT) + (SPLIT.index(u) + 1))
                    else:
                        sp.wait_ge(used, done * (NE * NU) + e * NU + (u + 1))
                    expert_load(sp, e, u)
            for n, t in enumerate((1, 0)):
                sp.wait_ge(sig["fin"], n + 1)
                sp.dma_start(out_v[:, t, :], xs[:, t, :]).then_inc(sig["stored"], 16)
            sp.wait_ge(sig["stored"], 16 * TT)

        def block_decay(n, g=None):
            if n == 1:
                v = fg if g is None else fg[:, 3 * g:3 * g + 3, :]
                return v.rearrange("p h (b r) -> p (h b) r", r=2)
            off = 0
            k = 2
            while k < n:
                off += HEADS * T // k
                k *= 2
            w = HEADS * T // n
            v = tot[:, off:off + w]
            if g is not None:
                v = v[:, g * w // 2:(g + 1) * w // 2]
            return v.rearrange("p (b r) -> p b r", r=2)

        @block.gpsimd
        def _(pool):
            own = [0]

            def link(ins):
                own[0] += 1
                ins.then_inc(pool_c, 1)
                pool.wait_ge(pool_c, own[0])

            link(pool.memset(ident[:, :], 0.0))
            pool.affine_select(out=ident[:, :], in_=ident[:, :], compare_op=ALU.not_equal, fill=1.0,
                               base=0, pattern=[[-1, P]], channel_multiplier=1).then_inc(sig["ident"], 1)
            link(pool.memset(twin[:, :], 0.0))
            for off in (0, CAP):
                link(pool.affine_select(out=twin[:, :], in_=twin[:, :], compare_op=ALU.not_equal, fill=1.0,
                                        base=-off, pattern=[[-1, CAP]], channel_multiplier=1))
            pool.memset(ones[:, :], 1.0).then_inc(sig["consts"], 1)
            pool.iota(tmp[:, 0:P].bitcast(I32), pattern=[[0, P]], base=0, channel_multiplier=1)
            pool.iota(tmp[:, P:2 * P].bitcast(I32), pattern=[[1, P]], base=0,
                      channel_multiplier=0).then_inc(sig["masks_iota"], 1)
            link(pool.memset(tri[:, :], 1.0))
            pool.affine_select(out=tri[:, :], in_=tri[:, :], compare_op=ALU.is_ge, fill=0.0,
                               base=0, pattern=[[1, P]], channel_multiplier=-1)
            link(pool.memset(cmask, 0.0))
            pool.affine_select(out=cmask, in_=cmask, compare_op=ALU.is_ge, fill=NEG,
                               base=0, pattern=[[-1, P]], channel_multiplier=1)
            for j in range(HALF):
                v = float(np.exp(np.float32(-math.log(THETA)) * np.float32(2 * j) / np.float32(ROT)))
                pool.memset(invf[:, j:j + 1], v)
            pool.iota(iota_s[:, :, :], pattern=[[0, TT], [1, CAP]], base=0, channel_multiplier=0,
                      allow_small_or_imprecise_dtypes=True)
            pool.iota(iota_e[:, :], pattern=[[1, NE]], base=0, channel_multiplier=0,
                      allow_small_or_imprecise_dtypes=True)
            pool.memset(sgz[:, :, :, :], 0.0)
            pool.memset(posx[:, :, :], -1.0)
            pool.memset(sct, 0.0).then_inc(sig["consts"], 1)

            for lv in range(1, 8):
                n = 1 << (lv - 1)
                for g in range(2):
                    if lv == 1:
                        pool.wait_ge(hk_ready, 3)
                    else:
                        pool.wait_ge(tot_upd, lv - 1)
                    pool.wait_ge(lev_done[g], lv + 1)
                    kv = kd[:, 3 * g:3 * g + 3, :].rearrange("p h (b r n) -> p (h b) r n", r=2, n=n)[:, :, 0, :]
                    right = block_decay(n, g)[:, :, 1]
                    nb = 3 * T // (2 * n)
                    pool.tensor_tensor(kv, kv, right.unsqueeze(2).to_broadcast([P, nb, n]),
                                       ALU.mult).then_inc(k_upd[g], 1)
            pool.wait_ge(sig["g2_read"], 1)
            pool.memset(yacc[:, :, :], 0.0).then_inc(sig["y_zero"], 1)
            pool.wait_ge(sig["h2"], TT)
            pool.memset(outs, 0.0).then_inc(m["out_cp"], 1)
            pool.wait_ge(sig["npass"], 1)

            turns = pool.value_load(count_i[0:1, 0:1], min_val=NE, max_val=NE * PASSES)
            with pool.Fori(0, turns) as i:
                e = pool.snap(i & (NE - 1))
                pool.wait_ge(m["p"], i + 1)
                pool.wait_ge(m["gt_cp"], i + 1)
                pool.tensor_tensor(pg[:, :, :, :], pe_[:, :, :].unsqueeze(2).to_broadcast([P, TT, 2, CAP]),
                                   gate[:, :, bass.ds(e, 1)].unsqueeze(3).to_broadcast([P, TT, 2, CAP]),
                                   ALU.mult).then_inc(m["pg"], 1)

        @block.scalar
        def _(act):
            own = [0]

            def link(ins):
                own[0] += 1
                ins.then_inc(act_c, 1)
                act.wait_ge(act_c, own[0])

            A = nc.scalar.activation
            act.dma_start(small[:, 0:8], c.rearrange("b (p k) -> (b p) k", p=P)).then_inc(ld["c"], 16)
            act.dma_start(xs[:, :, :], x_v).then_inc(ld["x"], 16)
            act.dma_start(tmp2[0:2 * KC, 0:P], b_ada[:, 0:U].rearrange("l (r f) -> (l r) f", f=P)).then_inc(ld["rows"], 16)
            act.dma_start(tmp2[2 * KC:3 * KC, 0:P], norm1_g.rearrange("l (r f) -> (l r) f", f=P)).then_inc(ld["rows"], 16)
            act.dma_start(tmp2[3 * KC:ROWS, 0:P], lb_logits.rearrange("l (h p) -> (l h) p", p=P)).then_inc(ld["rows"], 16)
            act.dma_start(posi[:, :], positions.rearrange("b (t p) -> p (b t)", p=P),
                          allow_slow_non_contiguous=True).then_inc(ld["pos"], 16)
            act.dma_start(bsrc.rearrange("p (a f) -> p a f", a=4),
                          b_gate_up.rearrange("l e (c f) -> (l e c) f", f=P)
                          .rearrange("(a r) f -> r a f", r=P)).then_inc(ld["bgu"], 16)
            act.dma_start(hgrow, hgrn_g.to_broadcast([P, P])).then_inc(ld["hg"], 16)
            act.dma_start(agrow, attn_g.to_broadcast([P, HD])).then_inc(ld["ag"], 16)
            act.dma_start(br[:, :], b_router.to_broadcast([P, NE])).then_inc(ld["br"], 16)
            act.dma_start(wr[:, :, :], w_router[0].rearrange("(k p) e -> p k e", p=P)).then_inc(ld["wr"], 16)
            act.wait_ge(sig["acc0"], 1)
            act.dma_start(mod[0:1, :, :].rearrange("p a d -> p (a d)"), b_ada[0:1, U:3 * U]).then_inc(ld["ada2_bias"], 16)

            act.wait_ge(ld["c"], 16)
            A(csil, crow, ACT.Sigmoid).then_inc(sig["csil"], 1)
            act.wait_ge(ld["x"], 16)
            for t in range(TT):
                A(slot(PRE)[:, t * D:(t + 1) * D], xs[:, t, :], ACT.Square, accum_out=ssq[:, t:t + 1]).then_inc(sig["ssq"], 1)
            act.wait_ge(sig["rsq"], 1)
            A(rstd, rstd, ACT.Sqrt).then_inc(sig["rstd"], 1)
            act.wait_ge(sig["rs1"], 1)
            for t in range(TT):
                A(hb[:, t, :], xs[:, t, :], ACT.Identity, scale=rstd[:, t:t + 1]).then_inc(sig["h1"], 1)
            act.wait_ge(sig["h1T"], 1)
            act.wait_ge(sig["a1"], 1)
            for k in range(KC // 2):
                last = A(ht[:, k, :], ps[:, 2048 + k * T:2048 + (k + 1) * T], ACT.Identity,
                         scale=a1[:, k:k + 1], bias=b1[:, k:k + 1])
            last.then_inc(sig["h1T_act"], 1)
            act.wait_ge(sig["lb_max"], 1)
            A(lbt, lbt, ACT.Exp).then_inc(sig["lb_done"], 1)
            act.wait_ge(sig["sin_arg"], 1)
            link(A(csn[:, 32:48], csn[:, 16:32], ACT.Sin, scale=0.5))
            A(csn[:, 16:32], csn[:, 16:32], ACT.Sin).then_inc(sig["sins"], 1)

            def half_copy(name):
                act.wait_ge(sig[name], 1)
                nc.scalar.copy(ht[:, 0:KC // 2, :].rearrange("p k t -> p (k t)"), bank(4, 2)).then_inc(sig[name + "_act"], 1)

            def group(j):
                b = 6 + j % 2
                act.wait_ge(win_pe, j + 1)
                wide = bank(b).rearrange("p (t n) -> p t n", t=TT)
                if j < 3:
                    A(fg[:, 2 * j:2 * j + 2, :].rearrange("p h t -> p (h t)"), bank(b), ACT.Sigmoid).then_inc(win_sig, 1)
                elif j < 6:
                    A(qd[:, 2 * (j - 3):2 * (j - 3) + 2, :].rearrange("p h t -> p (h t)"), bank(b),
                      ACT.Sigmoid).then_inc(win_sig, 1)
                elif j < 8:
                    nc.scalar.copy(aqk.rearrange("p (t n) -> p t n", t=TT)[:, :, (j - 6) * AW:(j - 5) * AW],
                                   wide).then_inc(act_evac, 1)
                elif j == 8:
                    nc.scalar.copy(av, wide).then_inc(act_evac, 1)
                elif j < 12:
                    nc.scalar.copy(vh[:, :, (j - 9) * CG:(j - 8) * CG], wide).then_inc(act_evac, 1)
                else:
                    A(hgate[:, :, (j - 12) * CG:(j - 11) * CG], wide, ACT.Sigmoid).then_inc(win_sig, 1)

            for j in range(WIN_UNITS):
                if j == 9:
                    act.wait_ge(sig["aT"], 1)
                    nc.scalar.copy(qkt.rearrange("p c t -> p (c t)"), bank(3, 2)).then_inc(sig["aT_copied"], 1)
                if j == 11:
                    act.wait_ge(sig["sc_ready"], 1)
                    A(pb.rearrange("p b s -> p (b s)"), pb.rearrange("p b s -> p (b s)"), ACT.Exp).then_inc(sig["expd"], 1)
                if j == 12:
                    act.wait_ge(sig["pT"], 1)
                    nc.scalar.copy(pt.rearrange("p b s -> p (b s)"), bank(3, 3)).then_inc(sig["pT_copied"], 1)
                if j == 14:
                    act.wait_ge(sig["aatt_ms"], 1)
                    A(asum, asum, ACT.Sqrt).then_inc(sig["aatt_sq"], 1)
                group(j)
            act.wait_ge(sig["cross"], 1)
            nc.scalar.copy(cross, ps[:, 0:HEADS * P]).then_inc(sig["cross_copied"], 1)
            act.wait_ge(sig["oh"], 1)
            A(fg.rearrange("p h t -> p (h t)"), bank(3, 3), ACT.Square).then_inc(sig["oh_sq"], 1)
            act.wait_ge(sig["oh_ms"], 1)
            A(rs2, rs2, ACT.Sqrt).then_inc(sig["oh_rs"], 1)
            for j in range(8):
                act.wait_ge(sig["ada2"], j + 1)
                nc.scalar.copy(mod[:, j // 2, (j % 2) * 512:(j % 2 + 1) * 512], bank(MOD_BANKS[j % 5])).then_inc(sig["mod_copied"], 1)
            half_copy("oT")
            act.wait_ge(sig["hg_cat"], TT)
            act.dma_start(yacc[:, 0, :], norm2_g.to_broadcast([P, D])).then_inc(ld["g2"], 16)
            for j in range(D // CG):
                act.wait_ge(sig["x1"], j + 1)
                if j:
                    act.wait_ge(sig["ssq2"], TT * j)
                for t in range(TT):
                    A(tmp2[:, t * CG:(t + 1) * CG], xs[:, t, j * CG:(j + 1) * CG], ACT.Square,
                      accum_out=ssq4[:, t, j:j + 1]).then_inc(sig["ssq2"], 1)
            act.wait_ge(sig["rms2"], 1)
            A(rstd, rstd, ACT.Sqrt).then_inc(sig["rs2"], 1)
            half_copy("h2T")
            act.wait_ge(m["out_cp"], 1)
            act.dma_start(outs[0:NE, :], b_down[0]).then_inc(ld["bdown"], 16)
            act.wait_ge(sig["v8"], 1)
            A(e4, e4, ACT.Exp).then_inc(sig["e4"], 1)

            def hi(i, u):
                act.wait_ge(raw[u], i * 16 + (raw_base[u] + 16))
                act.wait_ge(used, i * NU + buffer_user(u))
                nc.scalar.copy(whi[:, BUF[u], :], slot(u)).then_inc(hi_rdy, 1)

            def silu_part(i, s):
                act.wait_ge(m["g_" + s], i + 1)
                A(sg, guT[:, 0:4, :], ACT.Sigmoid, scale=ALPHA).then_inc(m["sig_" + s], 1)

            def act_hi(i, s):
                act.wait_ge(m["a_" + s], i + 1)
                nc.scalar.copy(at[:, AT[s], 0, :], sg[:, SG[s], :]).then_inc(m["ah_" + s], 1)

            def first_part(i, first=False):
                hi(i, 0)
                act.wait_ge(m["gt"], i + 1)
                nc.scalar.copy(gts[:, :], ps[:, 4 * 512:4 * 512 + T]).then_inc(m["gt_cp"], 1)
                hi(i, 1)
                if first:
                    hi(i, 2)
                    act.wait_ge(m["ga"], 1)
                    nc.scalar.copy(xg[:, :, 0, :], bank(5).rearrange("p (k s) -> p k s", k=KC)).then_inc(m["xg_hi"], 1)
                else:
                    act.wait_ge(used, i * NU + NU)
                    nc.scalar.copy(outs, bank(6, 2)).then_inc(m["out_cp"], 1)
                    hi(i, 2)
                for u in range(3, 6):
                    hi(i, u)
                act.wait_ge(used, i * NU + (NU + GU_UNITS))
                nc.scalar.copy(gu_a, bank(0, 2)).then_inc(m["gua_cp"], 1)
                for u in range(6, 9):
                    hi(i, u)

            def second_part(i):
                silu_part(i, "a")
                act_hi(i, "a")
                hi(i, 9)
                act.wait_ge(used, i * NU + (NU + 2 * GU_UNITS))
                nc.scalar.copy(gu_b, bank(2, 2)).then_inc(m["gub_cp"], 1)
                act.wait_ge(m["ga"], i + 2)
                nc.scalar.copy(xg[:, :, 0, :], bank(5).rearrange("p (k s) -> p k s", k=KC)).then_inc(m["xg_hi"], 1)
                hi(i, 11)
                silu_part(i, "b")
                act_hi(i, "b")

            first_part(0, first=True)
            act.wait_ge(sig["npass"], 1)
            turns = act.value_load(count_i[0:1, 0:1], min_val=NE, max_val=NE * PASSES)
            with act.Fori(0, act.snap(turns - 1)) as i:
                second_part(i)
                first_part(act.snap(i + 1))
            second_part(act.snap(turns - 1))
            act.wait_ge(m["gt"], turns + 1)
            nc.scalar.copy(gts[:, :], ps[:, 4 * 512:4 * 512 + T]).then_inc(m["gt_cp"], 1)
            act.wait_ge(used, turns * NU + NU)
            nc.scalar.copy(outs, bank(6, 2)).then_inc(m["out_cp"], 1)
            act.dma_start(gfin, final_g.rearrange("(a d) -> a d", a=1).to_broadcast([P, D])).then_inc(ld["gfin"], 16)
            for n, t in enumerate((1, 0)):
                act.wait_ge(sig["ofin"], n + 1)
                A(hb[:, 0, :], xs[:, t, :], ACT.Square,
                  accum_out=ssq[:, t:t + 1]).then_inc(sig["out_ssq"], 1)
                act.wait_ge(sig["out_rms"], n + 1)
                A(rstd[:, t:t + 1], rstd[:, t:t + 1], ACT.Sqrt).then_inc(sig["out_rs"], 1)

        @block.tensor
        def _(pe):
            mm = nc.tensor.matmul

            def turn_all(src, name, ready):
                for t in range(TT):
                    pe.wait_ge(ready, t + 1)
                    for k in range(KC):
                        last = nc.tensor.transpose(ps[:, 2048 + k * T + t * P:2048 + k * T + (t + 1) * P],
                                                   src[:, t, k * P:(k + 1) * P], ident[:, :])
                last.then_inc(sig[name], 1)

            pe.wait_ge(sig["ident"], 1)
            pe.wait_ge(ld["rows"], 3 * 16)
            nc.tensor.transpose(bank(1)[:, 0:ROWS], tmp2[0:ROWS, 0:P], ident[0:ROWS, 0:ROWS]).then_inc(sig["colsT"], 1)
            turn_all(hb, "h1T", sig["h1"])
            pe.wait_ge(sig["consts"], 2)
            pe.wait_ge(ada1_dve, KC)
            for n in range(2 * KC):
                last = mm(ps[:, n:n + 1], ada1[:, n * P:(n + 1) * P], ones[:, 0:1], start=True, stop=True)
            last.then_inc(sig["ada1"], 1)
            pe.wait_ge(sig["h1T_act"], 1)
            pe.wait_ge(sig["h1T_dve"], 1)

            def level(lv):
                b0 = 3 * (lv % 2)
                if lv > 1:
                    pe.wait_ge(sct_done, lv - 1)
                for g in range(2):
                    if lv == 0:
                        pe.wait_ge(hq_ready, 3)
                        pe.wait_ge(hk_ready, 3)
                    else:
                        pe.wait_ge(q_upd[g], lv)
                        if lv > 1:
                            pe.wait_ge(k_upd[g], lv - 1)
                    for h in range(3 * g, 3 * g + 3):
                        for t in range(TT):
                            j = h * TT + t
                            last = mm(ps[:, b0 * 512 + j * P:b0 * 512 + (j + 1) * P], kd[:, h, t * P:(t + 1) * P],
                                      qd[:, h, t * P:(t + 1) * P], start=True, stop=True)
                    last.then_inc(lev_done[g], 1)

            def attention_turn():
                pe.wait_ge(sct_done, 2)
                pe.wait_ge(sig["rot"], 1)
                for ch in range(4):
                    for t in range(TT):
                        last = nc.tensor.transpose(ps[:, 3 * 512 + ch * T + t * P:3 * 512 + ch * T + (t + 1) * P],
                                                   aqk[:, t * 2 * AW + ch * P:t * 2 * AW + (ch + 1) * P], ident[:, :])
                last.then_inc(sig["aT"], 1)

            def attention_scores():
                pe.wait_ge(sct_done, 3)
                pe.wait_ge(sig["aT_copied"], 1)
                for n, h in enumerate((0, 2, 1, 3)):
                    if n == 2:
                        pe.wait_ge(sig["sc_even"], 1)
                    r = slice(HD * (h % 2), HD * (h % 2) + HD)
                    q, k = qkt[r, h // 2, :], qkt[r, 2 + h // 2, :]
                    mm(ps[:, h * P:(h + 1) * P], q[:, 0:P], k[:, 0:P], start=True, stop=True)
                    last = mm(ps[:, (4 + 2 * h) * P:(6 + 2 * h) * P], q[:, P:T], k, start=True, stop=True)
                    if n == 1:
                        last.then_inc(sig["sc_even"], 1)
                last.then_inc(sig["sc"], 1)

            def attention_pt():
                pe.wait_ge(sct_done, 6)
                pe.wait_ge(sig["expd"], 1)
                for j in range(12):
                    last = nc.tensor.transpose(ps[:, 3 * 512 + j * P:3 * 512 + (j + 1) * P], pb[:, j, :], ident[:, :])
                last.then_inc(sig["pT"], 1)

            def attention_out():
                pe.wait_ge(sig["pT_copied"], 1)
                for h in range(AH):
                    o = ps[:, 3 * 512 + h * HD:3 * 512 + (h + 1) * HD]
                    mm(o, pt[:, h, :], av[:, 0, h * HD:(h + 1) * HD], start=True, stop=True)
                    o = ps[:, 3 * 512 + AW + h * HD:3 * 512 + AW + (h + 1) * HD]
                    for s in range(TT):
                        last = mm(o, pt[:, 4 + 2 * h + s, :], av[:, s, h * HD:(h + 1) * HD],
                                  start=(s == 0), stop=(s == 1))
                last.then_inc(sig["o_att"], 1)

            for j in range(WIN_UNITS):
                b = 6 + j % 2
                if j >= 2:
                    r = j - 2
                    s, v = (win_sig, r + 1) if r < 3 else (hq_ready, r - 2) if r < 6 else \
                        (act_evac, r - 5) if r < 12 else (sig["hg_read"], r - 11)
                    pe.wait_ge(s, v)
                landed(pe, ("win", j))
                w = slot(place[("win", j)] % PRE).rearrange("p (k n) -> p k n", k=KC)
                for i2 in range(2):
                    o = ps[:, b * 512 + i2 * T:b * 512 + (i2 + 1) * T]
                    for k in range(KC):
                        if j < 6:
                            last = mm(o, w[:, k, i2 * P:(i2 + 1) * P], ht[:, k, :], start=(k == 0), stop=(k == KC - 1))
                        else:
                            last = mm(o, ht[:, k, i2 * P:(i2 + 1) * P], w[:, k, :], start=(k == 0), stop=(k == KC - 1))
                last.then_inc(win_pe, 1)
                if j == 0:
                    pe.wait_ge(ld["bgu"], 16)
                    for a in range(4):
                        last = nc.tensor.transpose(bank(5)[:, a * P:(a + 1) * P], bsrc[:, a * P:(a + 1) * P], ident[:, :])
                    last.then_inc(sig["bguT"], 1)
                if j == 7:
                    pe.wait_ge(sig["bgu_read"], 1)
                    level(0)
                if j == 8:
                    level(1)
                    level(2)
                    attention_turn()
                if j == 9:
                    attention_scores()
                    level(3)
                if j == 10:
                    pe.wait_ge(sig["sc_read"], 1)
                    level(4)
                if j == 11:
                    level(5)
                    attention_pt()
                if j == 12:
                    attention_out()
                    level(6)
                if j == 13:
                    pe.wait_ge(sig["o_att_read"], 1)
                    level(7)
            pe.wait_ge(sct_done, 7)
            for g in range(2):
                pe.wait_ge(q_upd[g], 8)
                pe.wait_ge(k_upd[g], 7)
            for h in range(HEADS):
                last = mm(ps[:, h * P:(h + 1) * P], kd[:, h, 0:P], qd[:, h, P:T], start=True, stop=True)
            last.then_inc(sig["cross"], 1)
            pe.wait_ge(sct_done, 8)
            pe.wait_ge(act_evac, 6)
            pe.wait_ge(sig["cross_copied"], 1)
            sc4 = sct.rearrange("p (h t n) -> p h t n", h=HEADS, t=TT)
            for h in range(HEADS):
                for t in range(TT):
                    o = ps[:, 3 * 512 + (2 * h + t) * P:3 * 512 + (2 * h + t + 1) * P]
                    last = mm(o, sc4[:, h, t, :], vh[:, t, h * P:(h + 1) * P], start=True, stop=(t == 0))
                    if t == 1:
                        last = mm(o, cross[:, h * P:(h + 1) * P], vh[:, 0, h * P:(h + 1) * P], start=False, stop=True)
            last.then_inc(sig["oh"], 1)
            for j in range(8):
                b = MOD_BANKS[j % 5]
                if j < 2:
                    pe.wait_ge(sig["hg_read"], 3)
                elif j >= 5:
                    pe.wait_ge(sig["mod_copied"], j - 4)
                pe.wait_ge(ada_dve, KC * (1 + j // 4))
                mm(bank(b), ones[:, :], mod[:, j // 2, (j % 2) * 512:(j % 2 + 1) * 512],
                   start=True, stop=True).then_inc(sig["ada2"], 1)
            pe.wait_ge(sig["mod_copied"], 8)
            turn_all(hb, "oT", sig["hg_cat"])
            pe.wait_ge(sig["oT_act"], 1)
            pe.wait_ge(sig["oT_dve"], 1)
            for j in range(D // CG):
                landed(pe, ("wout", j))
                w = slot(place[("wout", j)] % PRE).rearrange("p (k n) -> p k n", k=KC)
                for t in range(TT):
                    for k in range(KC):
                        last = mm(ps[:, j * 512 + t * CG:j * 512 + (t + 1) * CG], ht[:, k, t * P:(t + 1) * P],
                                  w[:, k, :], start=(k == 0), stop=(k == KC - 1))
                last.then_inc(wout_pe, 1)
            turn_all(hb, "h2T", sig["h2"])
            pe.wait_ge(sig["h2T_act"], 1)
            pe.wait_ge(sig["h2T_dve"], 1)
            pe.wait_ge(ld["wr"], 16)
            for t in range(TT):
                for k in range(KC):
                    last = mm(ps[:, t * NE:(t + 1) * NE], ht[:, k, t * P:(t + 1) * P], wr[:, k, :],
                              start=(k == 0), stop=(k == KC - 1))
            last.then_inc(sig["logits"], 1)
            pe.wait_ge(sig["routed"], 1)
            mm(ps[:, 512:512 + NE], tri[:, :], msk[:, 0, :], start=True, stop=True)
            mm(ps[:, 512 + NE:512 + 2 * NE], tri[:, :], msk[:, 1, :], start=True, stop=False)
            mm(ps[:, 512 + NE:512 + 2 * NE], ones[:, :], msk[:, 0, :], start=False, stop=True)
            mm(ps[:, 512 + 2 * NE:512 + 3 * NE], ones[:, :], msk[:, 0, :], start=True, stop=False)
            mm(ps[:, 512 + 2 * NE:512 + 3 * NE], ones[:, :], msk[:, 1, :], start=False, stop=True).then_inc(sig["cum"], 1)
            pe.wait_ge(sig["gates"], 1)
            for t in range(TT):
                last = nc.tensor.transpose(ps[:, 4 * 512 + t * P:4 * 512 + (t + 1) * P], gate_pad[:, t, :], ident[:, :])
            last.then_inc(m["gt"], 1)

            def gather():
                for k in range(KC):
                    for t in range(TT):
                        last = mm(ps[:, 5 * 512 + k * CAP:5 * 512 + (k + 1) * CAP], hb[:, t, model_chunk(k)],
                                  pe_[:, t, :], start=(t == 0), stop=(t == TT - 1))
                last.then_inc(m["ga"], 1)

            def turn_gates():
                for t in range(TT):
                    last = nc.tensor.transpose(ps[:, 4 * 512 + t * P:4 * 512 + (t + 1) * P],
                                               pg[:, t, :, :].rearrange("p a s -> p (a s)"), ident[:, :])
                last.then_inc(m["gt"], 1)

            def combine(t):
                for n in range(2):
                    last = mm(bank((2, 6)[t] + n), gts[:, t * P:(t + 1) * P], outs[:, n * 512:(n + 1) * 512],
                              start=True, stop=True)
                last.then_inc(m["cb%d" % t], 1)

            def turn_gu(src, name):
                for ch in range(8):
                    last = mm(ps[:, 4 * 512 + ch * CAP:4 * 512 + (ch + 1) * CAP], src[:, ch * P:(ch + 1) * P],
                              twin[:, :], start=True, stop=True)
                last.then_inc(m[name], 1)

            pe.wait_ge(m["p"], 1)
            gather()
            pe.wait_ge(ld["bdown"], 16)
            pe.wait_ge(sig["npass"], 1)
            turns = pe.value_load(count_i[0:1, 0:1], min_val=NE, max_val=NE * PASSES)
            with pe.Fori(0, turns) as i:
                def unit(u, b0, lhs, first, k0):
                    for part, w in ((0, whi[:, BUF[u], :]), (1, wlo[:, BUF[u], :])):
                        pe.wait_ge((hi_rdy, lo_rdy)[part], i * len(SPLIT) + (SPLIT.index(u) + 1 + len(SPLIT)))
                        for k in range(2):
                            for n in range(2):
                                last = mm(bank(b0 + n), lhs[:, k0 + k, :, :].rearrange("p a s -> p (a s)"),
                                          w[:, (2 * k + n) * 512:(2 * k + n + 1) * 512],
                                          start=(first and part == 0 and k == 0),
                                          stop=(u % GU_UNITS == GU_UNITS - 1 and part == 1 and k == 1))
                    last.then_inc(used, 1)

                def unit_f32(u):
                    pe.wait_ge(raw[u], i * 16 + (raw_base[u] + 16))
                    for k in range(2):
                        for n in range(2):
                            last = mm(bank(6 + n), sgz[:, k, :, :].rearrange("p a s -> p (a s)"),
                                      slot(u)[:, (2 * k + n) * 512:(2 * k + n + 1) * 512],
                                      start=False, stop=False)
                    last.then_inc(used, 1)

                pe.wait_ge(m["xg"], i + 1)
                unit(0, 0, xg, True, 0)
                pe.wait_ge(m["out_cp"], i + 1)
                pe.wait_ge(m["gt_cp"], i + 1)
                combine(0)
                unit(1, 0, xg, False, 2)
                unit(2, 0, xg, False, 4)
                unit(3, 0, xg, False, 6)
                combine(1)
                pe.wait_ge(m["y0"], i + 1)
                unit(4, 2, xg, True, 0)
                unit(5, 2, xg, False, 2)
                pe.wait_ge(m["gua_cp"], i + 1)
                turn_gu(gu_a, "ta")
                unit(6, 2, xg, False, 4)
                pe.wait_ge(m["p"], i + 2)
                gather()
                unit(7, 2, xg, False, 6)
                pe.wait_ge(m["al_a"], i + 1)
                pe.wait_ge(m["y1"], i + 1)
                unit(8, 6, at, True, 0)
                pe.wait_ge(m["bias_a"], i + 1)
                pe.wait_ge(m["gub_cp"], i + 1)
                turn_gu(gu_b, "tb")
                unit(9, 6, at, False, 2)
                pe.wait_ge(m["bias_b"], i + 1)
                pe.wait_ge(m["pg"], i + 1)
                turn_gates()
                pe.wait_ge(m["a_b"], i + 1)
                unit_f32(F32_UNIT)
                pe.wait_ge(m["al_b"], i + 1)
                unit(11, 6, at, False, 4)
            pe.wait_ge(m["out_cp"], turns + 1)
            pe.wait_ge(m["gt_cp"], turns + 1)
            for t in (1, 0):
                combine(t)

        @block.vector
        def _(dve):
            own = [0]
            V = nc.vector

            def link(ins):
                own[0] += 1
                ins.then_inc(dve_c, 1)
                dve.wait_ge(dve_c, own[0])

            def mean_to_rsqrt(dst, src, n, done, sqrt_sem):
                V.tensor_scalar(dst, src, 1.0 / n, EPS, ALU.mult, ALU.add).then_inc(sig[done], 1)
                dve.wait_ge(sig[sqrt_sem], 1)
                link(V.reciprocal(dst, dst))

            V.memset(seed[:, 0:1], 0.0).then_inc(used, NU)
            V.memset(seed[:, 1:2], 0.0).then_inc(lo_rdy, len(SPLIT))
            V.memset(seed[:, 2:3], 0.0).then_inc(hi_rdy, len(SPLIT))
            V.memset(mod[:, :, :], 0.0).then_inc(sig["acc0"], 1)
            dve.wait_ge(sig["csil"], 1)
            link(V.tensor_tensor(csil, csil, crow, ALU.mult))
            for k in range(KC):
                if k in EARLY:
                    dve.wait_ge(early[k], 16)
                else:
                    landed(dve, ("ada1", k))
                w = slot(EARLY.get(k, k))
                if k == 0:
                    V.tensor_scalar(ada1, w, csil[:, 0:1], None, ALU.mult).then_inc(ada1_dve, 1)
                else:
                    V.scalar_tensor_tensor(out=ada1, in0=w, scalar=csil[:, k:k + 1], in1=ada1,
                                           op0=ALU.mult, op1=ALU.add).then_inc(ada1_dve, 1)
                dve.wait_ge(ada1_dve, k + 1)
                if k == 2:
                    dve.wait_ge(sig["ssq"], TT)
                    V.tensor_scalar(rstd, ssq, 1.0 / D, EPS, ALU.mult, ALU.add).then_inc(sig["rsq"], 1)
                if k == 3:
                    dve.wait_ge(sig["rstd"], 1)
                    V.reciprocal(rstd, rstd).then_inc(sig["rs1"], 1)
            dve.wait_ge(sig["colsT"], 1)
            link(V.tensor_copy(cols, bank(1)[:, 0:ROWS]))
            dve.wait_ge(sig["ada1"], 1)
            V.tensor_tensor(b1, ps[:, 0:KC], cols[:, 0:KC], ALU.add)
            link(V.tensor_tensor(a1, ps[:, KC:2 * KC], cols[:, KC:2 * KC], ALU.add))
            V.scalar_tensor_tensor(out=a1, in0=a1, scalar=1.0, in1=cols[:, 2 * KC:3 * KC],
                                   op0=ALU.add, op1=ALU.mult).then_inc(sig["a1"], 1)
            dve.wait_ge(sig["a1"], 1)
            dve.wait_ge(sig["h1T"], 1)
            for k in range(KC // 2, KC):
                last = V.tensor_scalar(ht[:, k, :], ps[:, 2048 + k * T:2048 + (k + 1) * T], a1[:, k:k + 1], b1[:, k:k + 1],
                                       ALU.mult, ALU.add)
            last.then_inc(sig["h1T_dve"], 1)
            link(V.tensor_tensor(omlb, lbt[:, 0:6], lbt[:, 6:12], ALU.max))
            V.tensor_tensor(lbt.rearrange("p (l h) -> p l h", l=2), lbt.rearrange("p (l h) -> p l h", l=2),
                            omlb.unsqueeze(1).to_broadcast([P, 2, HEADS]), ALU.subtract).then_inc(sig["lb_max"], 1)
            dve.wait_ge(sig["masks_iota"], 1)
            it = tmp[:, 0:2 * P].bitcast(I32)
            link(V.tensor_tensor(tmp[:, 2 * P:3 * P].bitcast(I32), it[:, 0:P], it[:, P:2 * P], ALU.bitwise_xor))
            link(V.tensor_copy(tmp2[:, 3 * P:4 * P], tmp[:, 2 * P:3 * P].bitcast(I32)))
            link(V.tensor_copy(tmp2[:, 2 * P:3 * P], it[:, 0:P]))
            link(V.tensor_copy(tmp[:, 3 * P:4 * P], it[:, P:2 * P]))
            link(V.tensor_tensor(tmp[:, 0:P], tmp[:, 3 * P:4 * P], tmp2[:, 2 * P:3 * P], ALU.is_ge))
            link(V.scalar_tensor_tensor(out=tmp[:, P:2 * P], in0=tmp2[:, 3 * P:4 * P], scalar=1.0,
                                        in1=tmp[:, 0:P], op0=ALU.add, op1=ALU.mult))
            for lv in range(8):
                lo = 0 if lv == 0 else 1 << (lv - 1)
                up = 1 if lv == 0 else 1 << lv
                link(V.tensor_scalar(tmp[:, 0:P], tmp[:, P:2 * P], float(up) + 0.5, None, ALU.is_lt))
                link(V.scalar_tensor_tensor(out=masks[:, lv, :], in0=tmp[:, P:2 * P], scalar=float(lo) + 0.5,
                                            in1=tmp[:, 0:P], op0=ALU.is_gt, op1=ALU.mult))
            dve.wait_ge(sig["lb_done"], 1)
            link(V.tensor_tensor(omlb, lbt[:, 0:6], lbt[:, 6:12], ALU.add))
            link(V.reciprocal(omlb, omlb))
            link(V.tensor_tensor(lbt[:, 0:6], lbt[:, 0:6], omlb, ALU.mult))
            V.tensor_scalar(omlb, lbt[:, 0:6], -1.0, 1.0, ALU.mult, ALU.add)
            dve.wait_ge(sig["bguT"], 1)
            V.tensor_copy(bgu[:, :, :].rearrange("p e c -> p (e c)"), bank(5)).then_inc(sig["bgu_read"], 1)
            dve.wait_ge(ld["pos"], 16)
            dve.wait_ge(sig["consts"], 2)
            link(V.tensor_copy(post, posi[:, :]))
            ang = csn[:, 16:32].rearrange("p (t j) -> p t j", t=TT)
            turn = csn[:, 0:16].rearrange("p (t j) -> p t j", t=TT)
            link(V.tensor_tensor(ang, post.unsqueeze(2).to_broadcast([P, TT, HALF]),
                                 invf.unsqueeze(1).to_broadcast([P, TT, HALF]), ALU.mult))
            magic = 12582912.0
            link(V.tensor_scalar(turn, ang, 1.0 / (2 * math.pi), magic, ALU.mult, ALU.add))
            link(V.tensor_scalar(turn, turn, -magic, None, ALU.add))
            c1 = 6.28125
            c2 = float(np.float32(np.floor((2 * math.pi - c1) * 2 ** 19) / 2 ** 19))
            c3 = 2 * math.pi - c1 - c2
            for cc in (c1, c2, c3):
                link(V.scalar_tensor_tensor(out=csn[:, 16:32], in0=csn[:, 0:16], scalar=-cc, in1=csn[:, 16:32],
                                            op0=ALU.mult, op1=ALU.add))
            V.tensor_scalar(ang, ang, 3.1415925, -3.1415925, ALU.min, ALU.max).then_inc(sig["sin_arg"], 1)
            dve.wait_ge(sig["sins"], 1)
            link(V.tensor_tensor(csn[:, 0:16], csn[:, 32:48], csn[:, 32:48], ALU.mult))
            link(V.tensor_scalar(csn[:, 0:16], csn[:, 0:16], -2.0, 1.0, ALU.mult, ALU.add))
            def half_copy(name):
                dve.wait_ge(sig[name], 1)
                V.tensor_copy(ht[:, KC // 2:KC, :].rearrange("p k t -> p (k t)"), bank(6, 2)).then_inc(sig[name + "_dve"], 1)

            dve.wait_ge(ld["ada2_bias"], 16)

            def accumulate(j):
                landed(dve, ("ada2", j))
                a = mod[:, 2 * (j // KC):2 * (j // KC) + 2, :].rearrange("p a d -> p (a d)")
                V.scalar_tensor_tensor(out=a, in0=slot(place[("ada2", j)] % PRE), scalar=csil[:, j % KC:j % KC + 1],
                                       in1=a, op0=ALU.mult, op1=ALU.add).then_inc(ada_dve, 1)
                dve.wait_ge(ada_dve, j + 1)

            def group(j):
                b = 6 + j % 2
                if j < 3:
                    dve.wait_ge(win_sig, j + 1)
                    for h in (2 * j, 2 * j + 1):
                        link(V.tensor_scalar(fg[:, h, :], fg[:, h, :], omlb[:, h:h + 1], lbt[:, h:h + 1],
                                             ALU.mult, ALU.add))
                    V.tensor_scalar(kd[:, 2 * j:2 * j + 2, :], fg[:, 2 * j:2 * j + 2, :], -1.0, 1.0,
                                    ALU.mult, ALU.add).then_inc(hk_ready, 1)
                elif j < 6:
                    dve.wait_ge(win_sig, j + 1)
                    q = qd[:, 2 * (j - 3):2 * (j - 3) + 2, :].rearrange("p h t -> p (h t)")
                    V.scalar_tensor_tensor(out=q, in0=bank(b), scalar=float(P) ** -0.5, in1=q,
                                           op0=ALU.mult, op1=ALU.mult).then_inc(hq_ready, 1)
                elif j >= 12:
                    dve.wait_ge(win_sig, j - 12 + 7)
                    g = hgate[:, :, (j - 12) * CG:(j - 11) * CG]
                    V.tensor_tensor(g, g, bank(b).rearrange("p (t n) -> p t n", t=TT), ALU.mult).then_inc(sig["hg_read"], 1)
                    dve.wait_ge(sig["hg_read"], j - 11)
                    gg = g.rearrange("p t (h n) -> p t h n", h=2)
                    for t in range(TT):
                        link(V.tensor_tensor(gg[:, t], gg[:, t], hgrow.unsqueeze(1).to_broadcast([P, 2, P]), ALU.mult))

            def update(lv):
                if lv == 1:
                    for g in range(2):
                        dve.wait_ge(lev_done[g], 1)
                        V.tensor_tensor(qd[:, 3 * g:3 * g + 3, :], qd[:, 3 * g:3 * g + 3, :], fg[:, 3 * g:3 * g + 3, :],
                                        ALU.mult).then_inc(q_upd[g], 1)
                    return
                n = 1 << (lv - 2)
                d = block_decay(n)
                if n > 1:
                    dve.wait_ge(tot_upd, lv - 2)
                if lv < 8:
                    V.tensor_tensor(block_decay(2 * n).rearrange("p b r -> p (b r)"), d[:, :, 0], d[:, :, 1],
                                    ALU.mult).then_inc(tot_upd, 1)
                for g in range(2):
                    dve.wait_ge(lev_done[g], lv)
                    dve.wait_ge(q_upd[g], lv - 1)
                    qv = qd[:, 3 * g:3 * g + 3, :].rearrange("p h (b r n) -> p (h b) r n", r=2, n=n)[:, :, 1, :]
                    left = block_decay(n, g)[:, :, 0]
                    V.tensor_tensor(qv, qv, left.unsqueeze(2).to_broadcast([P, 3 * T // (2 * n), n]),
                                    ALU.mult).then_inc(q_upd[g], 1)

            def merge(lv):
                b0 = 3 * (lv % 2)
                for g in range(2):
                    dve.wait_ge(lev_done[g], lv + 1)
                if lv:
                    dve.wait_ge(sct_done, lv)
                V.copy_predicated(sct.rearrange("p (j n) -> p j n", n=P),
                                  masks[:, lv, :].unsqueeze(1).to_broadcast([P, 12, P]),
                                  bank(b0, 3).rearrange("p (j n) -> p j n", n=P)).then_inc(sct_done, 1)

            def rotate():
                dve.wait_ge(act_evac, 2)
                q8 = aqk.rearrange("p (t h d) -> p t h d", t=TT, h=2 * AH)
                t1, t2 = q8[:, :, :, 0:HALF], q8[:, :, :, HALF:ROT]
                cos = csn[:, 0:16].rearrange("p (t j) -> p t j", t=TT).unsqueeze(2).to_broadcast([P, TT, 2 * AH, HALF])
                sin = csn[:, 16:32].rearrange("p (t j) -> p t j", t=TT).unsqueeze(2).to_broadcast([P, TT, 2 * AH, HALF])
                b = [tmp[:, n * P:(n + 1) * P].rearrange("p (t h j) -> p t h j", t=TT, h=2 * AH) for n in range(4)]
                V.tensor_tensor(b[0], t1, cos, ALU.mult)
                V.tensor_tensor(b[1], t2, sin, ALU.mult)
                V.tensor_tensor(b[2], t2, cos, ALU.mult)
                link(V.tensor_tensor(b[3], t1, sin, ALU.mult))
                V.tensor_tensor(t1, b[0], b[1], ALU.subtract)
                V.tensor_tensor(t2, b[2], b[3], ALU.add).then_inc(sig["rot"], 1)

            def softmax_in():
                dve.wait_ge(sig["sc"], 1)
                sc = bank(0, 3).rearrange("p (b s) -> p b s", b=12)
                scale = float(HD) ** -0.5
                cm = cmask.unsqueeze(1).to_broadcast([P, AH, P])
                V.scalar_tensor_tensor(out=pb[:, 0:4, :], in0=sc[:, 0:4, :], scalar=scale, in1=cm, op0=ALU.mult, op1=ALU.add)
                V.scalar_tensor_tensor(out=pb[:, 5:12:2, :], in0=sc[:, 5:12:2, :], scalar=scale, in1=cm,
                                       op0=ALU.mult, op1=ALU.add)
                V.tensor_scalar(pb[:, 4:12:2, :], sc[:, 4:12:2, :], scale, None, ALU.mult).then_inc(sig["sc_read"], 1)
                dve.wait_ge(sig["sc_read"], 1)
                late = pb[:, 4:12, :].rearrange("p (h s) n -> p h (s n)", h=AH)
                link(V.tensor_reduce(amax[:, 0:4], pb[:, 0:4, :], AX.X, ALU.max))
                link(V.tensor_reduce(amax[:, 4:8], late, AX.X, ALU.max))
                link(V.tensor_tensor(pb[:, 0:4, :], pb[:, 0:4, :], amax[:, 0:4].unsqueeze(2).to_broadcast([P, AH, P]),
                                     ALU.subtract))
                V.tensor_tensor(late, late, amax[:, 4:8].unsqueeze(2).to_broadcast([P, AH, T]),
                                ALU.subtract).then_inc(sig["sc_ready"], 1)

            def softmax_sum():
                dve.wait_ge(sig["expd"], 1)
                late = pb[:, 4:12, :].rearrange("p (h s) n -> p h (s n)", h=AH)
                V.tensor_reduce(asum[:, 0:4], pb[:, 0:4, :], AX.X, ALU.add)
                link(V.tensor_reduce(asum[:, 4:8], late, AX.X, ALU.add))
                link(V.reciprocal(amax, asum))

            oa = pb.rearrange("p b s -> p (b s)")[:, 0:512].rearrange("p (j d) -> p j d", d=HD)
            ob = pb.rearrange("p b s -> p (b s)")[:, 512:1024].rearrange("p (j d) -> p j d", d=HD)

            def attention_norm():
                dve.wait_ge(sig["o_att"], 1)
                V.tensor_tensor(oa, bank(3).rearrange("p (j d) -> p j d", d=HD),
                                amax.unsqueeze(2).to_broadcast([P, 8, HD]), ALU.mult).then_inc(sig["o_att_read"], 1)
                dve.wait_ge(sig["o_att_read"], 1)
                link(V.tensor_tensor(ob, oa, oa, ALU.mult))
                link(V.tensor_reduce(asum, ob, AX.X, ALU.add))
                V.tensor_scalar(asum, asum, 1.0 / HD, EPS, ALU.mult, ALU.add).then_inc(sig["aatt_ms"], 1)

            def attention_cat():
                dve.wait_ge(sig["aatt_sq"], 1)
                link(V.reciprocal(asum, asum))
                link(V.tensor_tensor(oa, oa, asum.unsqueeze(2).to_broadcast([P, 8, HD]), ALU.mult))
                for t in range(TT):
                    V.tensor_tensor(hb[:, t, HW_:D].rearrange("p (h d) -> p h d", h=AH), oa[:, 4 * t:4 * t + 4, :],
                                    agrow.unsqueeze(1).to_broadcast([P, AH, HD]), ALU.mult)

            dve.wait_ge(ld["hg"], 16)
            dve.wait_ge(ld["ag"], 16)
            for j in range(WIN_UNITS):
                accumulate(j)
                group(j)
                if j == 7:
                    rotate()
                    update(1)
                    merge(0)
                if j == 8:
                    update(2)
                    merge(1)
                    update(3)
                    merge(2)
                if j == 9:
                    softmax_in()
                    update(4)
                    merge(3)
                if j == 10:
                    update(5)
                    merge(4)
                if j == 11:
                    update(6)
                    merge(5)
                    softmax_sum()
                if j == 12:
                    attention_norm()
                    update(7)
                    merge(6)
                if j == 13:
                    update(8)
                    merge(7)
            attention_cat()
            accumulate(WIN_UNITS)
            dve.wait_ge(sig["oh_sq"], 1)
            link(V.tensor_reduce(rs2, fg.rearrange("p h (t n) -> p (h t) n", t=TT), AX.X, ALU.add))
            V.tensor_scalar(rs2, rs2, 1.0 / P, EPS, ALU.mult, ALU.add).then_inc(sig["oh_ms"], 1)
            dve.wait_ge(sig["oh_rs"], 1)
            link(V.reciprocal(rs2, rs2))
            tt3 = tot.rearrange("p (j n) -> p j n", n=P)
            link(V.tensor_tensor(tt3, bank(3, 3).rearrange("p (j n) -> p j n", n=P),
                                 rs2.unsqueeze(2).to_broadcast([P, 12, P]), ALU.mult))
            tt4 = tot.rearrange("p (h t n) -> p h t n", h=HEADS, t=TT)
            for t in range(TT):
                V.tensor_tensor(hb[:, t, 0:HW_].rearrange("p (h n) -> p h n", h=HEADS), tt4[:, :, t, :],
                                hgate[:, t, :].rearrange("p (h n) -> p h n", h=HEADS), ALU.mult).then_inc(sig["hg_cat"], 1)
            half_copy("oT")
            dve.wait_ge(sig["mod_copied"], 8)
            dve.wait_ge(ld["g2"], 16)
            V.scalar_tensor_tensor(out=mod[:, 2, :], in0=mod[:, 2, :], scalar=1.0, in1=yacc[:, 0, :],
                                   op0=ALU.add, op1=ALU.mult).then_inc(sig["g2_read"], 1)
            dve.wait_ge(sig["g2_read"], 1)
            for j in range(D // CG):
                dve.wait_ge(wout_pe, j + 1)
                mv = tmp[:, :].rearrange("p (t n) -> p t n", t=TT)
                link(V.tensor_tensor(mv, bank(j).rearrange("p (t n) -> p t n", t=TT),
                                     mod[:, 0, j * CG:(j + 1) * CG].unsqueeze(1).to_broadcast([P, TT, CG]), ALU.mult))
                xv = xs[:, :, j * CG:(j + 1) * CG]
                V.tensor_tensor(xv, xv, mv, ALU.add).then_inc(sig["x1"], 1)
                dve.wait_ge(sig["x1"], j + 1)
                link(V.tensor_tensor(hb[:, :, j * CG:(j + 1) * CG], xv,
                                     mod[:, 2, j * CG:(j + 1) * CG].unsqueeze(1).to_broadcast([P, TT, CG]), ALU.mult))
            dve.wait_ge(sig["ssq2"], TT * (D // CG))
            link(V.tensor_reduce(ssq, ssq4, AX.X, ALU.add))
            mean_to_rsqrt(rstd, ssq, D, "rms2", "rs2")
            for t in range(TT):
                V.scalar_tensor_tensor(out=hb[:, t, :], in0=hb[:, t, :], scalar=rstd[:, t:t + 1], in1=mod[:, 1, :],
                                       op0=ALU.mult, op1=ALU.add).then_inc(sig["h2"], 1)
            half_copy("h2T")
            def one_hot(i):
                col = posx[:, :, i:i + 1] if isinstance(i, int) else posx[:, :, bass.ds(i, 1)]
                V.tensor_tensor(pe_[:, :, :], iota_s[:, :, :], col.to_broadcast([P, TT, CAP]),
                                ALU.is_equal).then_inc(m["p"], 1)

            dve.wait_ge(sig["logits"], 1)
            dve.wait_ge(ld["br"], 16)
            lg = tmp2[:, 0:TT * NE].rearrange("p (t e) -> p t e", t=TT)
            V.memset(gate_pad, 0.0)
            link(V.tensor_tensor(lg, ps[:, 0:TT * NE].rearrange("p (t e) -> p t e", t=TT),
                                 br[:, :].unsqueeze(1).to_broadcast([P, TT, NE]), ALU.add))
            V.max(v8[:, 0, :], lg[:, 0, :])
            link(V.max(v8[:, 1, :], lg[:, 1, :]))
            V.tensor_tensor(e4, v8[:, :, 0:TOPK], v8[:, :, 0:1].to_broadcast([P, TT, TOPK]),
                            ALU.subtract).then_inc(sig["v8"], 1)
            V.max_index(ismall[:, 0:8], v8[:, 0, :], lg[:, 0, :])
            link(V.max_index(ismall[:, 8:16], v8[:, 1, :], lg[:, 1, :]))
            link(V.tensor_copy(idf, ismall[:, :].rearrange("p (t k) -> p t k", t=TT)))
            hot = tmp2[:, 0:TT * TOPK * NE].rearrange("p (t k e) -> p t k e", t=TT, k=TOPK)
            link(V.tensor_tensor(hot, iota_e[:, :].unsqueeze(1).unsqueeze(1).to_broadcast([P, TT, TOPK, NE]),
                                 idf[:, :, 0:TOPK].unsqueeze(3).to_broadcast([P, TT, TOPK, NE]), ALU.is_equal))
            V.tensor_reduce(msk[:, :, :], hot.rearrange("p t k e -> p t e k"), AX.X, ALU.add).then_inc(sig["routed"], 1)
            dve.wait_ge(sig["e4"], 1)
            link(V.tensor_reduce(esum, e4, AX.X, ALU.add))
            link(V.reciprocal(esum, esum))
            link(V.tensor_tensor(e4, e4, esum.unsqueeze(2).to_broadcast([P, TT, TOPK]), ALU.mult))
            link(V.tensor_tensor(hot, hot, e4.unsqueeze(3).to_broadcast([P, TT, TOPK, NE]), ALU.mult))
            link(V.tensor_reduce(gate[:, :, :], hot.rearrange("p t k e -> p t e k"), AX.X, ALU.add))
            V.tensor_copy(gate_pad[:, :, 0:NE], gate[:, :, :]).then_inc(sig["gates"], 1)
            dve.wait_ge(sig["cum"], 1)
            cum = ps[:, 512:512 + 2 * NE].rearrange("p (t e) -> p t e", t=TT)
            pos = tmp2[:, 256:256 + TT * NE].rearrange("p (t e) -> p t e", t=TT)
            link(V.tensor_tensor(pos, cum, msk[:, :, :], ALU.mult))
            V.tensor_reduce(cnt[:, 0:1], ps[:, 512 + 2 * NE:512 + 3 * NE], AX.X, ALU.max)
            for p_ in range(PASSES):
                last = V.tensor_scalar(posx[:, :, p_ * NE:(p_ + 1) * NE], pos, -1.0 - CAP * p_, None, ALU.add)
            link(last)
            one_hot(0)
            for p_ in range(1, PASSES):
                last = V.tensor_scalar(cnt[:, p_:p_ + 1], cnt[:, 0:1], p_ * CAP + 0.5, float(NE), ALU.is_gt, ALU.mult)
            link(last)
            link(V.tensor_reduce(cnt[:, 0:1], cnt[:, 1:PASSES], AX.X, ALU.add))
            V.tensor_scalar(count_i[:, :], cnt[:, 0:1], float(NE), None, ALU.add).then_inc(sig["npass"], 1)
            dve.wait_ge(sig["y_zero"], 1)
            dve.wait_ge(sig["npass"], 1)
            turns = dve.value_load(count_i[0:1, 0:1], min_val=NE, max_val=NE * PASSES)

            def lo(i, u):
                dve.wait_ge(hi_rdy, i * len(SPLIT) + (SPLIT.index(u) + 1 + len(SPLIT)))
                dve.wait_ge(used, i * NU + buffer_user(u))
                V.tensor_tensor(wlo[:, BUF[u], :], slot(u), whi[:, BUF[u], :].bitcast(F32),
                                ALU.subtract).then_inc(lo_rdy, 1)

            def tokens_lo(n):
                dve.wait_ge(m["xg_hi"], n)
                V.tensor_tensor(xg[:, :, 1, :], bank(5).rearrange("p (k s) -> p k s", k=KC),
                                xg[:, :, 0, :].bitcast(F32), ALU.subtract).then_inc(m["xg"], 1)

            def half_in(i, s, h):
                e = dve.snap(i & (NE - 1))
                dve.wait_ge(m["t" + s], i + 1)
                bias = bgu[:, bass.ds(e, 1), :].rearrange("p a (g c) -> p (a g) c", g=2)[:, :, 4 * h:4 * h + 4]
                V.tensor_tensor(guT[:, :, :].rearrange("p (g c) s -> p g c s", g=2),
                                bank(4).rearrange("p (g c s) -> p g c s", g=2, c=4),
                                bias.unsqueeze(3).to_broadcast([P, 2, 4, CAP]), ALU.add).then_inc(m["bias_" + s], 1)
                dve.wait_ge(m["bias_" + s], i + 1)
                V.tensor_scalar(guT[:, 0:4, :], guT[:, 0:4, :], LIMIT, None, ALU.min).then_inc(m["g_" + s], 1)
                V.tensor_scalar(guT[:, 4:8, :], guT[:, 4:8, :], LIMIT, -LIMIT, ALU.min, ALU.max).then_inc(m["u_" + s], 1)

            def half_act(i, s):
                dve.wait_ge(m["u_" + s], i + 1)
                V.scalar_tensor_tensor(out=guT[:, 4:8, :], in0=guT[:, 4:8, :], scalar=1.0, in1=guT[:, 0:4, :],
                                       op0=ALU.add, op1=ALU.mult).then_inc(m["ug_" + s], 1)
                dve.wait_ge(m["ug_" + s], i + 1)
                dve.wait_ge(m["sig_" + s], i + 1)
                V.tensor_tensor(sg, sg, guT[:, 4:8, :], ALU.mult).then_inc(m["a_" + s], 1)

            def half_lo(i, s):
                dve.wait_ge(m["ah_" + s], i + 1)
                V.tensor_tensor(at[:, AT[s], 1, :], sg[:, SG[s], :], at[:, AT[s], 0, :].bitcast(F32),
                                ALU.subtract).then_inc(m["al_" + s], 1)

            def add_share(i, t):
                dve.wait_ge(m["cb%d" % t], i + 1)
                V.tensor_tensor(yacc[:, t, :], yacc[:, t, :], bank((2, 6)[t], 2), ALU.add).then_inc(m["y%d" % t], 1)

            def first_part(i):
                for u in range(3):
                    lo(i, u)

            def second_part(i):
                lo(i, 3)
                add_share(i, 0)
                lo(i, 4)
                dve.wait_ge(m["pg"], i + 1)
                one_hot(dve.snap(i + 1))
                for u in range(5, 8):
                    lo(i, u)
                half_in(i, "a", 0)
                half_act(i, "a")
                add_share(i, 1)
                half_lo(i, "a")
                lo(i, 8)
                lo(i, 9)
                tokens_lo(i + 2)
                half_in(i, "b", 1)
                half_act(i, "b")
                half_lo(i, "b")
                lo(i, 11)

            first_part(0)
            tokens_lo(1)
            with dve.Fori(0, dve.snap(turns - 1)) as i:
                second_part(i)
                first_part(dve.snap(i + 1))
            second_part(dve.snap(turns - 1))
            for t in range(TT):
                dve.wait_ge(m["y%d" % t], turns)
                link(V.tensor_tensor(yacc[:, t, :], yacc[:, t, :], gate2, ALU.mult))
                link(V.tensor_tensor(xs[:, t, :], xs[:, t, :], yacc[:, t, :], ALU.add))
            for t in (1, 0):
                dve.wait_ge(m["cb%d" % t], turns + 1)
                link(V.tensor_tensor(yacc[:, t, :], bank((2, 6)[t], 2), gate2, ALU.mult))
                V.tensor_tensor(xs[:, t, :], xs[:, t, :], yacc[:, t, :], ALU.add).then_inc(sig["ofin"], 1)
            dve.wait_ge(ld["gfin"], 16)
            for n, t in enumerate((1, 0)):
                r_ = rstd[:, t:t + 1]
                dve.wait_ge(sig["out_ssq"], n + 1)
                V.tensor_scalar(r_, ssq[:, t:t + 1], 1.0 / D, EPS, ALU.mult, ALU.add).then_inc(sig["out_rms"], 1)
                dve.wait_ge(sig["out_rs"], n + 1)
                link(V.reciprocal(r_, r_))
                V.scalar_tensor_tensor(out=xs[:, t, :], in0=xs[:, t, :], scalar=r_, in1=gfin,
                                       op0=ALU.mult, op1=ALU.mult).then_inc(sig["fin"], 1)


_INS = ["x", "c", "positions", "w_ada", "b_ada", "norm1_g", "w_in", "hgrn_lb_logits", "hgrn_norm_g", "attn_norm_g",
        "w_out", "norm2_g", "w_router", "b_router", "w_gate_up", "b_gate_up", "w_down", "b_down", "final_norm_g"]


def kernel(**inputs):
    import concourse.bacc as _bacc
    from concourse.bass_utils import run_bass_kernel_spmd as _run

    nc = _bacc.Bacc("TRN2", target_bir_lowering=False, num_devices=1)
    arrays, args = {}, []
    for name in _INS:
        a = np.ascontiguousarray(inputs[name])
        arrays[f"in_{name}_dram"] = a
        args.append(nc.dram_tensor(f"in_{name}_dram", a.shape, mybir.dt.from_np(a.dtype), kind="ExternalInput").ap())
    args.append(nc.dram_tensor("out_dram", (1, T, D), F32, kind="ExternalOutput").ap())
    decoder_block(nc, *args)
    r = _run(nc, [arrays], core_ids=[0])
    return r.results[0]["out_dram"]
```
